# Optimizing a Trainium2 kernel written in Bass

```python
import math
import jax
import jax.numpy as jnp
from jax import lax
import numpy as np

D_MODEL = 1024
BATCH = 1
SEQ = 512
DEPTH = 1

DN_HEADS = 4
DN_HEAD_DIM = 128
DN_WIDTH = DN_HEADS * DN_HEAD_DIM
CONV_WIDTH = 4
CHUNK = 64
SWA_HEADS = 8
SWA_KV_HEADS = 2
SWA_GROUP = SWA_HEADS // SWA_KV_HEADS
SWA_HEAD_DIM = 64
SWA_WIDTH = SWA_HEADS * SWA_HEAD_DIM
SWA_KV_WIDTH = SWA_KV_HEADS * SWA_HEAD_DIM
WINDOW = 128
MIX_WIDTH = DN_WIDTH + SWA_WIDTH
IN_SIZES = (3 * DN_WIDTH, DN_WIDTH, DN_HEADS, DN_HEADS, SWA_WIDTH, SWA_KV_WIDTH, SWA_KV_WIDTH)
IN_COLS = sum(IN_SIZES)
N_EXPERTS = 32
TOP_K = 4
D_FF = D_MODEL
SWIGLU_ALPHA = 1.702
SWIGLU_LIMIT = 7.0
MOE_BLOCK = 128
EPS = 1e-6
NEG = -1e30


def _rmsnorm(x, w):
    xf = x.astype(jnp.float32)
    y = xf * lax.rsqrt(jnp.mean(xf * xf, axis=-1, keepdims=True) + EPS)
    return (y * w.astype(jnp.float32)).astype(x.dtype)

def _l2norm(x):
    xf = x.astype(jnp.float32)
    return xf * lax.rsqrt(jnp.sum(xf * xf, axis=-1, keepdims=True) + EPS)

def _causal_conv_silu(u, w):
    n_ch = u.shape[-1]
    y = lax.conv_general_dilated(u, w[:, None, :].astype(u.dtype), window_strides=(1,),
                                 padding=[(CONV_WIDTH - 1, 0)],
                                 dimension_numbers=('NWC', 'WIO', 'NWC'),
                                 feature_group_count=n_ch)
    return jax.nn.silu(y)

def _chunk_gated_delta_rule(q, k, v, g, beta):
    Bn, Sn, H, Dk = q.shape
    Dv = v.shape[-1]
    N = Sn // CHUNK

    def to_chunks(t):
        t = t.astype(jnp.float32).reshape(Bn, N, CHUNK, *t.shape[2:])
        return jnp.moveaxis(t, 3, 2)

    qc = to_chunks(q) * (Dk ** -0.5)
    kc, vc, gc, bc = to_chunks(k), to_chunks(v), to_chunks(g), to_chunks(beta)
    gcum = jnp.cumsum(gc, axis=-1)
    incl = jnp.tril(jnp.ones((CHUNK, CHUNK), bool))
    strict = jnp.tril(jnp.ones((CHUNK, CHUNK), bool), -1)
    diff = gcum[..., :, None] - gcum[..., None, :]
    decay = jnp.where(incl, jnp.exp(jnp.where(incl, diff, 0.0)), 0.0)
    k_beta = kc * bc[..., None]
    a_kk = jnp.where(strict, jnp.einsum('bnhcd,bnhsd->bnhcs', k_beta, kc) * decay, 0.0)
    t_mat = a_kk + jnp.eye(CHUNK, dtype=jnp.float32)
    rhs = jnp.concatenate([vc * bc[..., None], k_beta * jnp.exp(gcum)[..., None]], axis=-1)
    sol = jax.lax.linalg.triangular_solve(t_mat, rhs, left_side=True, lower=True,
                                          unit_diagonal=True)
    u, w = sol[..., :Dv], sol[..., Dv:]
    a_qk = jnp.where(incl, jnp.einsum('bnhcd,bnhsd->bnhcs', qc, kc) * decay, 0.0)
    q_dec = qc * jnp.exp(gcum)[..., None]
    g_last = gcum[..., -1]
    k_dec = kc * jnp.exp(g_last[..., None] - gcum)[..., None]
    chunk_decay = jnp.exp(g_last)
    xs = tuple(jnp.moveaxis(t, 1, 0) for t in (q_dec, k_dec, u, w, a_qk, chunk_decay))

    def step(state, inp):
        q_i, k_i, u_i, w_i, a_i, d_i = inp
        v_new = u_i - jnp.einsum('bhcd,bhde->bhce', w_i, state)
        o_i = (jnp.einsum('bhcd,bhde->bhce', q_i, state)
               + jnp.einsum('bhcs,bhse->bhce', a_i, v_new))
        state = state * d_i[..., None, None] + jnp.einsum('bhcd,bhce->bhde', k_i, v_new)
        return state, o_i

    state0 = jnp.zeros((Bn, H, Dk, Dv), jnp.float32)
    _, o = lax.scan(step, state0, xs)
    return jnp.transpose(o, (1, 0, 3, 2, 4)).reshape(Bn, Sn, H, Dv)

def _sliding_window_attention(q, k, v, q_norm_w, k_norm_w, sinks):
    Bn, Sn, _ = q.shape
    NB = Sn // WINDOW
    q = _rmsnorm(q.reshape(Bn, Sn, SWA_HEADS, SWA_HEAD_DIM), q_norm_w).astype(jnp.float32)
    k = _rmsnorm(k.reshape(Bn, Sn, SWA_KV_HEADS, SWA_HEAD_DIM), k_norm_w).astype(jnp.float32)
    v = v.reshape(Bn, Sn, SWA_KV_HEADS, SWA_HEAD_DIM).astype(jnp.float32)
    pad = jnp.zeros((Bn, WINDOW, SWA_KV_HEADS, SWA_HEAD_DIM), jnp.float32)

    def band(t):
        tp = jnp.concatenate([pad, t], axis=1).reshape(Bn, NB + 1, WINDOW, SWA_KV_HEADS, SWA_HEAD_DIM)
        return jnp.concatenate([tp[:, :-1], tp[:, 1:]], axis=2)

    kw, vw = band(k), band(v)
    qb = q.reshape(Bn, NB, WINDOW, SWA_KV_HEADS, SWA_GROUP, SWA_HEAD_DIM)
    s = jnp.einsum('bnqkgd,bnskd->bnkgqs', qb, kw) * (SWA_HEAD_DIM ** -0.5)
    qi = jnp.arange(WINDOW)[:, None]
    kj = jnp.arange(2 * WINDOW)[None, :]
    rel = (qi + WINDOW - kj).astype(jnp.float32)
    key_pos = jnp.arange(NB)[:, None, None] * WINDOW - WINDOW + kj[None]
    valid = (rel[None] >= 0) & (rel[None] < WINDOW) & (key_pos >= 0)
    slopes = (2.0 ** (-8.0 * jnp.arange(1, SWA_HEADS + 1, dtype=jnp.float32) / SWA_HEADS))
    slopes = slopes.reshape(SWA_KV_HEADS, SWA_GROUP)
    logits = s - slopes[None, None, :, :, None, None] * rel
    logits = jnp.where(valid[None, :, None, None], logits, NEG)
    sink = sinks.astype(jnp.float32).reshape(SWA_KV_HEADS, SWA_GROUP)[None, None, :, :, None]
    m = jnp.maximum(jnp.max(logits, axis=-1), sink)
    p = jnp.exp(logits - m[..., None])
    denom = jnp.sum(p, axis=-1) + jnp.exp(sink - m)
    o = jnp.einsum('bnkgqs,bnskd->bnqkgd', p / denom[..., None], vw)
    return o.reshape(Bn, Sn, SWA_WIDTH)

def _mixer(h, w_in, conv_w, a_log, dt_bias, dn_norm_w, q_norm_w, k_norm_w, sinks, w_out):
    Bn, Sn, _ = h.shape
    proj = h @ w_in
    split_idx = np.cumsum(IN_SIZES)[:-1].tolist()
    dn_qkv, dn_z, dn_a, dn_b, sw_q, sw_k, sw_v = jnp.split(proj, split_idx, axis=-1)
    qkv = _causal_conv_silu(dn_qkv, conv_w)
    q, k, v = jnp.split(qkv, 3, axis=-1)
    q = _l2norm(q.reshape(Bn, Sn, DN_HEADS, DN_HEAD_DIM))
    k = _l2norm(k.reshape(Bn, Sn, DN_HEADS, DN_HEAD_DIM))
    v = v.reshape(Bn, Sn, DN_HEADS, DN_HEAD_DIM)
    beta = jax.nn.sigmoid(dn_b.astype(jnp.float32))
    g = -jnp.exp(a_log.astype(jnp.float32)) * jax.nn.softplus(
        dn_a.astype(jnp.float32) + dt_bias.astype(jnp.float32))
    o_dn = _chunk_gated_delta_rule(q, k, v, g, beta)
    o_dn = _rmsnorm(o_dn, dn_norm_w) * jax.nn.silu(
        dn_z.reshape(Bn, Sn, DN_HEADS, DN_HEAD_DIM).astype(jnp.float32))
    o_dn = o_dn.reshape(Bn, Sn, DN_WIDTH)
    o_sw = _sliding_window_attention(sw_q, sw_k, sw_v, q_norm_w, k_norm_w, sinks)
    mixed = jnp.concatenate([o_dn.astype(h.dtype), o_sw.astype(h.dtype)], axis=-1)
    return mixed @ w_out

def _moe(h, w_router, b_router, w_up, b_up, w_down, b_down):
    Bn, Sn, D = h.shape
    T = Bn * Sn
    xf = h.reshape(T, D)
    logits = (xf @ w_router).astype(jnp.float32) + b_router.astype(jnp.float32)
    top_val, top_idx = lax.top_k(logits, TOP_K)
    gates = jax.nn.softmax(top_val, axis=-1)
    n_assign = T * TOP_K
    flat_e = top_idx.reshape(-1)
    flat_tok = jnp.arange(n_assign, dtype=jnp.int32) // TOP_K
    flat_gate = gates.reshape(-1)
    order = jnp.argsort(flat_e)
    se, stok, sgate = flat_e[order], flat_tok[order], flat_gate[order]
    counts = jnp.bincount(flat_e, length=N_EXPERTS)
    padded = (counts + MOE_BLOCK - 1) // MOE_BLOCK * MOE_BLOCK
    start = jnp.cumsum(counts) - counts
    pend = jnp.cumsum(padded)
    pstart = pend - padded
    dest = pstart[se] + (jnp.arange(n_assign) - start[se])
    n_pad = n_assign + N_EXPERTS * MOE_BLOCK
    n_blocks = n_pad // MOE_BLOCK
    row_tok = jnp.zeros((n_pad,), jnp.int32).at[dest].set(stok)
    row_gate = jnp.zeros((n_pad,), jnp.float32).at[dest].set(sgate)
    block_e = jnp.minimum(jnp.searchsorted(pend, jnp.arange(n_blocks) * MOE_BLOCK, side='right'),
                          N_EXPERTS - 1)
    xs = xf[row_tok].reshape(n_blocks, MOE_BLOCK, D)

    def expert_block(args):
        xb, e = args
        hu = xb @ w_up[e] + b_up[e]
        x_glu = jnp.minimum(hu[:, :D_FF], SWIGLU_LIMIT)
        x_lin = jnp.clip(hu[:, D_FF:], -SWIGLU_LIMIT, SWIGLU_LIMIT)
        act = x_glu * jax.nn.sigmoid(SWIGLU_ALPHA * x_glu) * (x_lin + 1.0)
        return act @ w_down[e] + b_down[e]

    ys = lax.map(expert_block, (xs, block_e)).reshape(n_pad, D)
    ys = ys.astype(jnp.float32) * row_gate[:, None]
    out = jax.ops.segment_sum(ys, row_tok, num_segments=T)
    return out.reshape(Bn, Sn, D).astype(h.dtype)

def first_inputs(seed: int = 0) -> dict:
    key = jax.random.key(seed)
    ks = jax.random.split(key, 24)
    L = DEPTH

    def nrm(k, shape, scale):
        return jax.random.normal(k, shape, jnp.float32) * scale

    dt = jnp.exp(jax.random.uniform(ks[8], (L, DN_HEADS), jnp.float32,
                                    math.log(1e-3), math.log(1e-1)))
    return {
        'x': nrm(ks[0], (BATCH, SEQ, D_MODEL), 1.0),
        'c': nrm(ks[1], (BATCH, D_MODEL), 1.0),
        'w_ada': nrm(ks[2], (L, D_MODEL, 6 * D_MODEL), 0.5 * D_MODEL ** -0.5),
        'b_ada': nrm(ks[3], (L, 6 * D_MODEL), 0.02),
        'norm1_w': 1.0 + nrm(ks[4], (L, D_MODEL), 0.02),
        'w_in': nrm(ks[5], (L, D_MODEL, IN_COLS), D_MODEL ** -0.5),
        'conv_w': nrm(ks[6], (L, CONV_WIDTH, 3 * DN_WIDTH), CONV_WIDTH ** -0.5),
        'a_log': jnp.log(jax.random.uniform(ks[7], (L, DN_HEADS), jnp.float32, 1.0, 16.0)),
        'dt_bias': dt + jnp.log(-jnp.expm1(-dt)),
        'dn_norm_w': 1.0 + nrm(ks[9], (L, DN_HEAD_DIM), 0.02),
        'q_norm_w': 1.0 + nrm(ks[10], (L, SWA_HEAD_DIM), 0.02),
        'k_norm_w': 1.0 + nrm(ks[11], (L, SWA_HEAD_DIM), 0.02),
        'sinks': nrm(ks[12], (L, SWA_HEADS), 1.0),
        'w_out': nrm(ks[13], (L, MIX_WIDTH, D_MODEL), MIX_WIDTH ** -0.5),
        'norm2_w': 1.0 + nrm(ks[14], (L, D_MODEL), 0.02),
        'w_router': nrm(ks[15], (L, D_MODEL, N_EXPERTS), D_MODEL ** -0.5),
        'b_router': nrm(ks[16], (L, N_EXPERTS), 0.01),
        'w_up': nrm(ks[17], (L, N_EXPERTS, D_MODEL, 2 * D_FF), D_MODEL ** -0.5),
        'b_up': nrm(ks[18], (L, N_EXPERTS, 2 * D_FF), 0.01),
        'w_down': nrm(ks[19], (L, N_EXPERTS, D_FF, D_MODEL), D_FF ** -0.5),
        'b_down': nrm(ks[20], (L, N_EXPERTS, D_MODEL), 0.01),
    }

def first_block(x, c, w_ada, b_ada, norm1_w, w_in, conv_w, a_log, dt_bias, dn_norm_w,
              q_norm_w, k_norm_w, sinks, w_out, norm2_w, w_router, b_router,
              w_up, b_up, w_down, b_down):
    out_dtype = x.dtype
    c_act = jax.nn.silu(c)
    for l in range(DEPTH):
        mod = (c_act @ w_ada[l] + b_ada[l])[:, None, :]
        shift1, scale1, gate1, shift2, scale2, gate2 = jnp.split(mod, 6, axis=-1)
        h = _rmsnorm(x, norm1_w[l]) * (1.0 + scale1) + shift1
        y = _mixer(h, w_in[l], conv_w[l], a_log[l], dt_bias[l], dn_norm_w[l],
                   q_norm_w[l], k_norm_w[l], sinks[l], w_out[l])
        x = x + gate1 * y
        h = _rmsnorm(x, norm2_w[l]) * (1.0 + scale2) + shift2
        x = x + gate2 * _moe(h, w_router[l], b_router[l], w_up[l], b_up[l], w_down[l], b_down[l])
    return x.astype(out_dtype)


DEPTH_2 = 2

GRID_W = 64
CTX_LEN = 256
Q_BLOCK = 128
ROPE_BASE = 10000.0
NEG_INF = -1e30

MLA_HEADS = 8
MLA_NOPE = 64
MLA_ROPE = 32
MLA_V = 64
MLA_Q_RANK = 256
MLA_KV_RANK = 256

GQA_HEADS = 8
GQA_KV_HEADS = 2
GQA_DIM = 64

WIN_HEADS = 8
WIN_KV_HEADS = 2
WIN_DIM = 64

CONV_CH = 512
CONV_K = 3

AB_MIX = MLA_HEADS * MLA_V + GQA_HEADS * GQA_DIM
AB_SPLIT = (MLA_Q_RANK, MLA_KV_RANK, MLA_ROPE,
            GQA_HEADS * GQA_DIM, GQA_KV_HEADS * GQA_DIM, GQA_KV_HEADS * GQA_DIM,
            AB_MIX)
AB_IN = sum(AB_SPLIT)
CD_MIX = WIN_HEADS * WIN_DIM + CONV_CH
CD_SPLIT = (WIN_HEADS * WIN_DIM, WIN_KV_HEADS * WIN_DIM, WIN_KV_HEADS * WIN_DIM,
            CONV_CH, CONV_CH, CONV_CH, CD_MIX)
CD_IN = sum(CD_SPLIT)


def rmsnorm(x, gain=None):
    xf = x.astype(jnp.float32)
    y = xf * lax.rsqrt(jnp.mean(xf * xf, axis=-1, keepdims=True) + EPS)
    if gain is not None:
        y = y * gain.astype(jnp.float32)
    return y.astype(x.dtype)

def adaln(x, mod):
    shift, scale, gate = jnp.split(mod, 3, axis=-1)
    return rmsnorm(x) * (1.0 + scale) + shift, gate

def split_cols(t, sizes):
    out, off = [], 0
    for n in sizes:
        out.append(t[..., off:off + n])
        off += n
    return out

def grid_positions(n):
    rows = n // GRID_W
    row = jnp.repeat(jnp.arange(rows, dtype=jnp.float32), GRID_W)
    col = jnp.tile(jnp.arange(GRID_W, dtype=jnp.float32), rows)
    return row, col

def rope_1d(x, pos):
    half = x.shape[-1] // 2
    inv = ROPE_BASE ** (-jnp.arange(half, dtype=jnp.float32) / half)
    ang = pos[:, None] * inv[None, :]
    cos = jnp.cos(ang)[:, None, :].astype(x.dtype)
    sin = jnp.sin(ang)[:, None, :].astype(x.dtype)
    x1, x2 = x[..., :half], x[..., half:]
    return jnp.concatenate([x1 * cos - x2 * sin, x2 * cos + x1 * sin], axis=-1)

def axial_rope(x, row, col):
    half = x.shape[-1] // 2
    return jnp.concatenate([rope_1d(x[..., :half], row), rope_1d(x[..., half:], col)], axis=-1)

def rope_tail(x, rot_dim, row, col):
    return jnp.concatenate([x[..., :-rot_dim], axial_rope(x[..., -rot_dim:], row, col)], axis=-1)

def ctx_attention(q, k, v, sink=None):
    b, l, h, d = q.shape
    hk = k.shape[2]
    g = h // hk
    qg = q.reshape(b, l, hk, g, d)
    s = jnp.einsum('bqkgd,bnkd->bkgqn', qg, k, preferred_element_type=jnp.float32) * (d ** -0.5)
    if sink is not None:
        sk = jnp.broadcast_to(sink.reshape(hk, g).astype(jnp.float32)[None, :, :, None, None], (b, hk, g, l, 1))
        p = jax.nn.softmax(jnp.concatenate([s, sk], axis=-1), axis=-1)[..., :l]
    else:
        p = jax.nn.softmax(s, axis=-1)
    o = jnp.einsum('bkgqn,bnkd->bqkgd', p.astype(v.dtype), v)
    return o.reshape(b, l, h, v.shape[-1])

def joint_dense_attention(q, k, v, kc, vc):
    b, s, h, d = q.shape
    hk = k.shape[2]
    g = h // hk
    nb = s // Q_BLOCK
    kk = jnp.concatenate([kc, k], axis=1)
    vv = jnp.concatenate([vc, v], axis=1)
    qb = jnp.moveaxis(q.reshape(b, nb, Q_BLOCK, hk, g, d), 1, 0)

    def block(qi):
        sc = jnp.einsum('bqkgd,bnkd->bkgqn', qi, kk, preferred_element_type=jnp.float32) * (d ** -0.5)
        p = jax.nn.softmax(sc, axis=-1)
        return jnp.einsum('bkgqn,bnkd->bqkgd', p.astype(vv.dtype), vv)

    o = lax.map(block, qb)
    return jnp.moveaxis(o, 0, 1).reshape(b, s, h, v.shape[-1])

def joint_window_attention(q, k, v, kc, vc, sink):
    b, s, h, d = q.shape
    hk = k.shape[2]
    g = h // hk
    nb = s // Q_BLOCK
    l = kc.shape[1]
    pad = ((0, 0), (Q_BLOCK, Q_BLOCK), (0, 0), (0, 0))
    kp, vp = jnp.pad(k, pad), jnp.pad(v, pad)

    def bands(t):
        return jnp.concatenate(
            [t[:, j * Q_BLOCK: j * Q_BLOCK + s].reshape(b, nb, Q_BLOCK, hk, t.shape[-1]) for j in range(3)], axis=2)

    kb = jnp.moveaxis(bands(kp), 1, 0)
    vb = jnp.moveaxis(bands(vp), 1, 0)
    qb = jnp.moveaxis(q.reshape(b, nb, Q_BLOCK, hk, g, d), 1, 0)
    blk = jnp.arange(nb)[:, None, None] * Q_BLOCK
    qpos = blk + jnp.arange(Q_BLOCK)[None, :, None]
    kpos = blk - Q_BLOCK + jnp.arange(3 * Q_BLOCK)[None, None, :]
    mask = (jnp.abs(qpos - kpos) <= WINDOW) & (kpos >= 0) & (kpos < s)
    sink_l = sink.reshape(hk, g).astype(jnp.float32)
    scale = d ** -0.5

    def block(args):
        qi, ki, vi, mi = args
        s_loc = jnp.einsum('bqkgd,bmkd->bkgqm', qi, ki, preferred_element_type=jnp.float32) * scale
        s_loc = jnp.where(mi[None, None, None], s_loc, NEG_INF)
        s_ctx = jnp.einsum('bqkgd,blkd->bkgql', qi, kc, preferred_element_type=jnp.float32) * scale
        s_snk = jnp.broadcast_to(sink_l[None, :, :, None, None], (b, hk, g, Q_BLOCK, 1))
        p = jax.nn.softmax(jnp.concatenate([s_ctx, s_loc, s_snk], axis=-1), axis=-1)
        return (jnp.einsum('bkgql,blkd->bqkgd', p[..., :l].astype(vc.dtype), vc)
                + jnp.einsum('bkgqm,bmkd->bqkgd', p[..., l:l + 3 * Q_BLOCK].astype(vi.dtype), vi))

    o = lax.map(block, (qb, kb, vb, mask))
    return jnp.moveaxis(o, 0, 1).reshape(b, s, h, v.shape[-1])

def short_conv(u, w):
    ch = u.shape[-1]
    return lax.conv_general_dilated(u, w[:, None, :].astype(u.dtype), window_strides=(1,),
                                    padding=((CONV_K // 2, CONV_K // 2),),
                                    dimension_numbers=('NWC', 'WIO', 'NWC'), feature_group_count=ch)

def heads_ab(pp, cq_gain, ckv_gain, w_uq, w_ukv, q_gain, k_gain, qg_gain, kg_gain):
    cq, ckv, kr, gq, gk, gv, gate = split_cols(pp, AB_SPLIT)
    lead = pp.shape[:-1]
    qa = (rmsnorm(cq, cq_gain) @ w_uq).reshape(lead + (MLA_HEADS, MLA_NOPE + MLA_ROPE))
    kv = (rmsnorm(ckv, ckv_gain) @ w_ukv).reshape(lead + (MLA_HEADS, MLA_NOPE + MLA_V))
    kr_h = jnp.broadcast_to(kr[..., None, :], lead + (MLA_HEADS, MLA_ROPE))
    ka = jnp.concatenate([kv[..., :MLA_NOPE], kr_h], axis=-1)
    va = kv[..., MLA_NOPE:]
    qb = rmsnorm(gq.reshape(lead + (GQA_HEADS, GQA_DIM)), qg_gain)
    kb = rmsnorm(gk.reshape(lead + (GQA_KV_HEADS, GQA_DIM)), kg_gain)
    vb = gv.reshape(lead + (GQA_KV_HEADS, GQA_DIM))
    return rmsnorm(qa, q_gain), rmsnorm(ka, k_gain), va, qb, kb, vb, gate

def ab_layer(x, xc, mod, mod_c, w_in, w_out, cq_gain, ckv_gain, w_uq, w_ukv, q_gain, k_gain,
             qg_gain, kg_gain, row, col, update_ctx):
    b, s, _ = x.shape
    h, gate = adaln(x, mod)
    hc, gate_c = adaln(xc, mod_c)
    wts = (cq_gain, ckv_gain, w_uq, w_ukv, q_gain, k_gain, qg_gain, kg_gain)
    qa, ka, va, qb, kb, vb, g = heads_ab(h @ w_in, *wts)
    qac, kac, vac, qbc, kbc, vbc, gc = heads_ab(hc @ w_in, *wts)
    qa, ka = rope_tail(qa, MLA_ROPE, row, col), rope_tail(ka, MLA_ROPE, row, col)
    qb, kb = axial_rope(qb, row, col), axial_rope(kb, row, col)
    oa = joint_dense_attention(qa, ka, va, kac, vac).reshape(b, s, -1)
    ob = joint_dense_attention(qb, kb, vb, kbc, vbc).reshape(b, s, -1)
    mix = jnp.concatenate([oa, ob], axis=-1) * jax.nn.silu(g)
    x = x + gate * (mix @ w_out)
    if update_ctx:
        l = xc.shape[1]
        oac = ctx_attention(qac, kac, vac).reshape(b, l, -1)
        obc = ctx_attention(qbc, kbc, vbc).reshape(b, l, -1)
        mixc = jnp.concatenate([oac, obc], axis=-1) * jax.nn.silu(gc)
        xc = xc + gate_c * (mixc @ w_out)
    return x, xc

def heads_cd(pp, q_gain, k_gain):
    pq, pk, pv, gb, gcc, gh, gate = split_cols(pp, CD_SPLIT)
    lead = pp.shape[:-1]
    q = rmsnorm(pq.reshape(lead + (WIN_HEADS, WIN_DIM)), q_gain)
    k = rmsnorm(pk.reshape(lead + (WIN_KV_HEADS, WIN_DIM)), k_gain)
    v = pv.reshape(lead + (WIN_KV_HEADS, WIN_DIM))
    return q, k, v, gb, gcc, gh, gate

def cd_layer(x, xc, mod, mod_c, w_in, w_out, q_gain, k_gain, sink, conv_w, row, col, update_ctx):
    b, s, _ = x.shape
    h, gate = adaln(x, mod)
    hc, gate_c = adaln(xc, mod_c)
    q, k, v, gb, gcv, gh, g = heads_cd(h @ w_in, q_gain, k_gain)
    qc, kc, vc, gbc, gcvc, ghc, gc = heads_cd(hc @ w_in, q_gain, k_gain)
    q, k = axial_rope(q, row, col), axial_rope(k, row, col)
    oc = joint_window_attention(q, k, v, kc, vc, sink).reshape(b, s, -1)
    od = gb * short_conv(gcv * gh, conv_w)
    mix = jnp.concatenate([oc, od], axis=-1) * jax.nn.silu(g)
    x = x + gate * (mix @ w_out)
    if update_ctx:
        l = xc.shape[1]
        occ = ctx_attention(qc, kc, vc, sink).reshape(b, l, -1)
        odc = gbc * short_conv(gcvc * ghc, conv_w)
        mixc = jnp.concatenate([occ, odc], axis=-1) * jax.nn.silu(gc)
        xc = xc + gate_c * (mixc @ w_out)
    return x, xc

def second_inputs(seed: int = 0) -> dict:
    key = jax.random.key(seed)
    ks = iter(jax.random.split(key, 32))
    f32 = jnp.float32
    n_ab = (DEPTH_2 + 1) // 2
    n_cd = DEPTH_2 // 2

    def nrm(shape, scale):
        return jax.random.normal(next(ks), shape, f32) * scale

    def gain(shape):
        return 1.0 + 0.1 * jax.random.normal(next(ks), shape, f32)

    return {
        'x': nrm((BATCH, SEQ, D_MODEL), 1.0),
        'c': nrm((BATCH, D_MODEL), 1.0),
        'ctx': nrm((BATCH, CTX_LEN, D_MODEL), 1.0),
        'c_ctx': nrm((D_MODEL,), 1.0),
        'mod_w': nrm((DEPTH_2, D_MODEL, 3 * D_MODEL), D_MODEL ** -0.5),
        'mod_b': nrm((DEPTH_2, 3 * D_MODEL), 0.02),
        'ab_w_in': nrm((n_ab, D_MODEL, AB_IN), D_MODEL ** -0.5),
        'ab_w_out': nrm((n_ab, AB_MIX, D_MODEL), AB_MIX ** -0.5),
        'mla_cq_gain': gain((n_ab, MLA_Q_RANK)),
        'mla_ckv_gain': gain((n_ab, MLA_KV_RANK)),
        'mla_w_uq': nrm((n_ab, MLA_Q_RANK, MLA_HEADS * (MLA_NOPE + MLA_ROPE)), MLA_Q_RANK ** -0.5),
        'mla_w_ukv': nrm((n_ab, MLA_KV_RANK, MLA_HEADS * (MLA_NOPE + MLA_V)), MLA_KV_RANK ** -0.5),
        'mla_q_gain': gain((n_ab, MLA_NOPE + MLA_ROPE)),
        'mla_k_gain': gain((n_ab, MLA_NOPE + MLA_ROPE)),
        'gqa_q_gain': gain((n_ab, GQA_DIM)),
        'gqa_k_gain': gain((n_ab, GQA_DIM)),
        'cd_w_in': nrm((n_cd, D_MODEL, CD_IN), D_MODEL ** -0.5),
        'cd_w_out': nrm((n_cd, CD_MIX, D_MODEL), CD_MIX ** -0.5),
        'win_q_gain': gain((n_cd, WIN_DIM)),
        'win_k_gain': gain((n_cd, WIN_DIM)),
        'win_sink': nrm((n_cd, WIN_HEADS), 0.5),
        'conv_w': nrm((n_cd, CONV_K, CONV_CH), CONV_K ** -0.5),
    }

def second_block(x, c, ctx, c_ctx, mod_w, mod_b, ab_w_in, ab_w_out, mla_cq_gain, mla_ckv_gain,
              mla_w_uq, mla_w_ukv, mla_q_gain, mla_k_gain, gqa_q_gain, gqa_k_gain,
              cd_w_in, cd_w_out, win_q_gain, win_k_gain, win_sink, conv_w):
    n = x.shape[1]
    row, col = grid_positions(n)
    sc = jax.nn.silu(c)
    scc = jax.nn.silu(c_ctx)
    xc = ctx
    for i in range(DEPTH_2):
        mod = (sc @ mod_w[i] + mod_b[i])[:, None, :]
        mod_c = scc @ mod_w[i] + mod_b[i]
        j = i // 2
        update = i < DEPTH_2 - 1
        if i % 2 == 0:
            x, xc = ab_layer(x, xc, mod, mod_c, ab_w_in[j], ab_w_out[j], mla_cq_gain[j], mla_ckv_gain[j],
                             mla_w_uq[j], mla_w_ukv[j], mla_q_gain[j], mla_k_gain[j],
                             gqa_q_gain[j], gqa_k_gain[j], row, col, update)
        else:
            x, xc = cd_layer(x, xc, mod, mod_c, cd_w_in[j], cd_w_out[j], win_q_gain[j], win_k_gain[j],
                             win_sink[j], conv_w[j], row, col, update)
    return x


def setup_inputs(seed=0):
    out = dict(first_inputs(seed))
    for name, value in second_inputs(seed + 1).items():
        if name != "x":
            out[name + "_2"] = value
    return out


def reference(
    x, c, w_ada, b_ada, norm1_w, w_in, conv_w, a_log, dt_bias, dn_norm_w, q_norm_w, k_norm_w,
    sinks, w_out, norm2_w, w_router, b_router, w_up, b_up, w_down, b_down, c_2, ctx_2, c_ctx_2,
    mod_w_2, mod_b_2, ab_w_in_2, ab_w_out_2, mla_cq_gain_2, mla_ckv_gain_2, mla_w_uq_2,
    mla_w_ukv_2, mla_q_gain_2, mla_k_gain_2, gqa_q_gain_2, gqa_k_gain_2, cd_w_in_2, cd_w_out_2,
    win_q_gain_2, win_k_gain_2, win_sink_2, conv_w_2,
):
    x = first_block(
        x, c, w_ada, b_ada, norm1_w, w_in, conv_w, a_log, dt_bias, dn_norm_w, q_norm_w,
        k_norm_w, sinks, w_out, norm2_w, w_router, b_router, w_up, b_up, w_down, b_down,
    )
    return second_block(
        x, c_2, ctx_2, c_ctx_2, mod_w_2, mod_b_2, ab_w_in_2, ab_w_out_2, mla_cq_gain_2,
        mla_ckv_gain_2, mla_w_uq_2, mla_w_ukv_2, mla_q_gain_2, mla_k_gain_2, gqa_q_gain_2,
        gqa_k_gain_2, cd_w_in_2, cd_w_out_2, win_q_gain_2, win_k_gain_2, win_sink_2, conv_w_2,
    )


_drawn_inputs = setup_inputs


def setup_inputs(seed=0):
    import zlib

    import numpy as np

    out = dict(_drawn_inputs(seed))
    spreads = {}
    factors = {'norm1_w': 3.921,
     'dn_norm_w': 4.838,
     'q_norm_w': 8.0,
     'k_norm_w': 8.0,
     'sinks': 120.196,
     'b_router': 3.209,
     'b_up': 23.116,
     'b_down': 28.417,
     'mla_cq_gain_2': 8.0,
     'mla_ckv_gain_2': 3.037,
     'mla_q_gain_2': 8.0,
     'mla_k_gain_2': 8.0,
     'gqa_q_gain_2': 8.0,
     'gqa_k_gain_2': 8.0,
     'win_q_gain_2': 8.0,
     'win_k_gain_2': 8.0,
     'win_sink_2': 8.0,
     'norm2_w': 3.029}
    for name, (base, spread) in spreads.items():
        noise = np.random.default_rng([zlib.crc32(name.encode()), seed]).standard_normal(out[name].shape)
        drawn = base * np.exp(spread * noise) if base else spread * noise
        out[name] = jnp.asarray(drawn.astype(out[name].dtype))
    for name, factor in factors.items():
        out[name] = (out[name] * factor).astype(out[name].dtype)
    return out
```

```python
import numpy as np
import concourse.bass as bass
from concourse import mybir
from concourse.alu_op_type import AluOpType as ALU
from contextlib import ExitStack

F32 = mybir.dt.float32
I32 = mybir.dt.int32
U32 = mybir.dt.uint32
BF16 = mybir.dt.bfloat16
ACT = mybir.ActivationFunctionType
AX = mybir.AxisListType
EPS = 1e-6
NEG = -1e30
NSLOT = 5
NEXP = 32
NXB = 15
NBLK = NEXP + NXB
NBU = 3


class Engine:

    def __init__(self, eng, sem):
        self.eng, self.sem, self.n, self.on = eng, sem, 0, True
        self.seen = {}

    def wait(self, *deps):
        for d in deps:
            if d is None:
                continue
            if isinstance(d, list):
                self.wait(*d)
                continue
            sem, v = d
            if self.on and self.seen.get(id(sem), 0) < v:
                self.eng.wait_ge(sem, v)
                self.seen[id(sem)] = v

    def __call__(self, f, *deps):
        self.wait(*deps)
        if self.on:
            f(self.eng).then_inc(self.sem, 1)
        self.n += 1
        return (self.sem, self.n)

    def last(self):
        return (self.sem, self.n)


class DmaSem:

    def __init__(self, sem):
        self.sem, self.n = sem, 0

    def __call__(self, E, out, in_, *deps, f=None):
        E.wait(*deps)
        if E.on:
            i = E.eng.dma_start(out, in_) if f is None else f(E.eng)
            i.then_inc(self.sem, 16)
        self.n += 16
        return (self.sem, self.n)


def constants():
    p = np.arange(128)[:, None]
    j = np.arange(128)[None, :]
    same = (p // 64) == (j // 64)
    eye = np.eye(128)
    c0 = np.concatenate([eye, np.ones((128, 128))], 1)
    m1 = same & (p <= j)
    m2 = same & (p > j)
    cols = [m2, m1, same]
    for b in (1, 2, 4, 8, 16, 32):
        cols.append((p // (2 * b) == j // (2 * b)) & ((p // b) % 2 == 0) & ((j // b) % 2 == 1))
    cols.append((p // 2 == j // 2) & (p % 2 == 1) & (j % 2 == 0))
    c1 = np.concatenate(cols, 1)
    k2 = np.arange(256)[None, :]
    rel = (p + 128 - k2).astype(np.float32)
    slopes = 2.0 ** (-8.0 * np.arange(1, 9, dtype=np.float32) / 8)
    ok = (rel >= 0) & (rel < 128)
    swa = np.concatenate([np.where(ok, -s * rel, NEG) for s in slopes], 1)
    c2 = np.concatenate([
        p < j,
        np.broadcast_to(j, (128, 128)),
        np.broadcast_to(128.0 * np.arange(32), (128, 32)),
        np.broadcast_to(np.repeat(np.arange(NXB), 32), (128, NXB * 32)),
        p + 128 * np.arange(4)[None, :]], 1)
    t = np.arange(512)
    pos = np.stack([(t // 64), (t % 64)], 1).astype(np.float32)

    def rope(half):
        inv = (np.float32(10000.0) ** (-np.arange(half, dtype=np.float32) / np.float32(half))).astype(np.float32)
        ang = (pos[:, :, None] * inv).astype(np.float32)
        out = []
        for f in (np.cos, np.sin):
            out.append(f(ang).reshape(4, 128, 2 * half).transpose(1, 0, 2).reshape(128, 8 * half))
        return out

    wm = [np.where(j >= p, 0.0, NEG), np.where(j <= p, 0.0, NEG)]
    c3 = np.concatenate(rope(16) + rope(8) + wm, 1)
    return {n: np.ascontiguousarray(a, np.float32) for n, a in
            dict(cst0=c0, cst1=c1, cst1b=swa, cst2=c2, cst3=c3).items()}


def program(nc, D, out, dbg=None, stop=None):
    ctx = ExitStack()
    with ctx:
        def sem(name):
            return ctx.enter_context(nc.semaphore(name))

        def dram(name, shape, dt=F32):
            return nc.dram_tensor(name, shape, dt, kind="Internal").ap()

        engs = [nc.tensor, nc.vector, nc.scalar, nc.gpsimd, nc.sync]
        names = ["pe", "dve", "act", "pool", "sp"]
        T, V, A, G, S = [Engine(e, sem("s_" + n)) for e, n in zip(engs, names)]
        EN = [T, V, A, G, S]

        def dsem(name):
            return DmaSem(sem("d_" + name))

        def everyone():
            return [e.last() for e in EN[:4]]

        def fin():
            S.wait(*[(q.sem, q.n) for q in W.sems], everyone())

        dead = []

        def barrier(*dmas):
            t = everyone()
            for e in EN[:4]:
                e.wait(t, *dmas)
            dead[:] = t

        ring = ctx.enter_context(nc.sbuf_tensor("ring", [128, NSLOT * 4096], F32))
        WORDS = 32400
        mem = ctx.enter_context(nc.sbuf_tensor("mem", [128, WORDS], F32))
        PP = [ctx.enter_context(nc.psum_tensor(f"ps{i}", [128, 1024], F32)) for i in range(4)]
        PS = [PP[b // 2][:, (b % 2) * 512:(b % 2) * 512 + 512] for b in range(8)]
        rel = [None] * 8
        turn = [0]

        def bank():
            turn[0] = (turn[0] + 1) % 8
            return turn[0]

        top = [0]

        def alloc(*dims, dt=F32, at=None):
            n = int(np.prod(dims))
            if at is None:
                at = top[0]
                top[0] += n
            assert at + n <= WORDS, (at, n)
            v = mem[:, at:at + n]
            if dt != F32:
                v = v.bitcast(dt)
            if len(dims) == 2:
                v = v.rearrange("p (a b) -> p a b", b=dims[1])
            if len(dims) == 3:
                v = v.rearrange("p (a b c) -> p a b c", b=dims[1], c=dims[2])
            return v

        loads = []

        class Stream:
            def __init__(self, tag):
                self.sems = [dsem(f"w{tag}{i}") for i in range(NSLOT)]
                self.issued = self.taken = 0
                self.free = [None] * NSLOT

            def issue(self):
                if self.issued >= len(loads):
                    return
                s = self.issued % NSLOT
                for dst, src in loads[self.issued]:
                    self.sems[s](S, dst(ring[:, s * 4096:(s + 1) * 4096]), src, self.free[s])
                self.issued += 1

            def take(self):
                s = self.taken % NSLOT
                assert self.taken < self.issued
                self.taken += 1
                return s, ring[:, s * 4096:(s + 1) * 4096], (self.sems[s].sem, self.sems[s].n)

            def give(self, s, tok):
                self.free[s] = tok
                self.issue()

        def cols(n0, n):
            return lambda v: v.rearrange("p (k n) -> p k n", n=512)[:, :, n0:n0 + n]

        def kp(w):
            return w.rearrange("(k p) n -> p k n", p=128)

        def pk(w):
            return w.rearrange("(p k) n -> p k n", k=8)

        for c in range(12):
            loads.append([(cols(0, 512), pk(D["w_ada"][0])[:, :, c * 512:c * 512 + 512])])
        wi = kp(D["w_in"][0])
        loads.append([(cols(0, 512), wi[:, :, 2056:2568])])
        loads.append([(cols(0, 8), wi[:, :, 2048:2056])]
                     + [(cols(8 + 64 * i, 64), wi[:, :, 2568 + 64 * (i // 2):2632 + 64 * (i // 2)]) for i in range(4)]
                     + [(cols(264, 128), wi[:, :, 2696:2824])])
        for c in range(4):
            loads.append([(cols(0, 512), wi[:, :, c * 512:c * 512 + 512])])
        for l in range(2):
            for c in range(6):
                loads.append([(cols(0, 512), pk(D["mod_w_2"][l])[:, :, c * 512:c * 512 + 512])])
        wo = kp(D["w_out"][0])
        for c in range(2):
            loads.append([(cols(0, 512), wo[:, :, c * 512:c * 512 + 512])])

        def up_loads(w):
            w = kp(w)
            return [[(lambda v: v.rearrange("p (k n) -> p k n", n=2048), w[:, 2 * q:2 * q + 2, :])] for q in range(4)]

        def down_loads(w):
            w = kp(w)
            return [[(lambda v: v.rearrange("p (k n) -> p k n", n=1024), w[:, 4 * q:4 * q + 4, :])] for q in range(2)]

        for e in range(NEXP):
            loads += up_loads(D["w_up"][0, e])
            if e:
                loads += down_loads(D["w_down"][0, e - 1])
        loads += down_loads(D["w_down"][0, NEXP - 1])
        n_first = len(loads)
        ab = kp(D["ab_w_in_2"][0])
        loads.append([(cols(0, 512), ab[:, :, 544:1056])])
        loads.append([(cols(0, 32), ab[:, :, 512:544]), (cols(32, 256), ab[:, :, 1056:1312])])
        loads.append([(cols(0, 512), ab[:, :, 0:512])])
        loads.append([(cols(0, 512), ab[:, :, 1312:1824])])
        loads.append([(cols(0, 512), ab[:, :, 1824:2336])])
        uq = D["mla_w_uq_2"][0].rearrange("(k p) n -> p k n", p=128)
        ukv = D["mla_w_ukv_2"][0].rearrange("(k p) n -> p k n", p=128)
        loads.append([(lambda v: v[:, 0:1536].rearrange("p (k n) -> p k n", n=768), uq),
                      (lambda v: v[:, 1536:3584].rearrange("p (k n) -> p k n", n=1024), ukv)])
        for c in range(2):
            loads.append([(cols(0, 512), kp(D["ab_w_out_2"][0])[:, :, c * 512:c * 512 + 512])])
        cd = kp(D["cd_w_in_2"][0])
        loads.append([(cols(0, 512), cd[:, :, 0:512])])
        loads.append([(cols(0, 256), cd[:, :, 512:768])])
        for c in range(5):
            loads.append([(cols(0, 512), cd[:, :, 768 + 512 * c:1280 + 512 * c])])
        for c in range(2):
            loads.append([(cols(0, 512), kp(D["cd_w_out_2"][0])[:, :, c * 512:c * 512 + 512])])
        later = loads[n_first:]
        del loads[n_first:]

        W = Stream("a")

        def dump(name, ap, *deps):
            if dbg is not None and name in dbg:
                d = dsem("dbg_" + name)
                t = d(G, dbg[name], ap, *deps)
                for e in EN:
                    e.wait(t)

        alt = [0]

        def evac(o, i, *deps):
            alt[0] ^= 1
            if alt[0]:
                return V(lambda e: e.tensor_copy(o, i), *deps)
            return A(lambda e: e.activation(o, i, ACT.Copy), *deps)

        def rsqrt(o, i, scale, *deps, eps=EPS):
            t = V(lambda e: e.tensor_scalar(o, i, scale, eps, ALU.mult, ALU.add), *deps)
            t2 = A(lambda e: e.activation(o, o, ACT.Sqrt), t)
            return V(lambda e: e.reciprocal(o, o), t2), t

        def mms(o, pairs):
            def f(e):
                for n, (l, r) in enumerate(pairs):
                    i = e.matmul(o, l, r, start=(n == 0), stop=(n == len(pairs) - 1))
                return i
            return f

        def transposes(items):
            def f(e):
                for o, i in items:
                    k = i.shape[0]
                    r = e.transpose(o, i, ident[0:k, 0:k])
                return r
            return f

        cst0 = alloc(256)
        ident, ones = cst0[:, 0:128], cst0[:, 128:256]
        VF = alloc(80)
        modF = alloc(48)
        mod2F = alloc(2, 48)
        small = alloc(64)
        rows4 = alloc(32)
        sinkr = alloc(16)
        gains = alloc(448)
        rout = alloc(4, 32)
        GT = alloc(4, 4)
        DEST = alloc(16, dt=I32)
        ROW = alloc(48, dt=I32)
        XE = alloc(16, dt=I32)
        cact = alloc(3, 8)
        ones3 = alloc(64).bitcast(BF16)
        base = top[0]
        MOD = dram("mod_rows", (6144,))
        MOD2 = dram("mod2_rows", (2, 2, 3072))
        H2D = dram("h2_rows", (512, 1024))
        BIASD = dram("bias_rows", (NEXP, 3, 3072), BF16)
        YD = dram("y_rows", (NBLK * 128, 1024))

        for _ in range(NSLOT):
            W.issue()

        dcv = dsem("cvec")
        for i, n in enumerate(["c", "c_2", "c_ctx_2"]):
            src = D[n] if n == "c_ctx_2" else D[n][0]
            tcv = dcv(A, cact[:, i, :], src.rearrange("(p j) -> p j", j=8))
        dc = dsem("const")
        dc(A, cst0, D["cst0"])
        vrows = alloc(128)
        nv = [0]

        def vrow(src, n):
            dc(A, vrows[nv[0]:nv[0] + n, :], src)
            nv[0] += n
            return nv[0] - n

        r_n1 = vrow(D["norm1_w"][0].rearrange("(a p) -> a p", p=128), 8)
        r_cw = vrow(D["conv_w"][0].rearrange("i (t p) -> (i t) p", p=128), 48)
        r_dn = vrow(D["dn_norm_w"], 1)

        def vrow2(src):
            for h in range(2):
                dc(A, vrows[nv[0]:nv[0] + 1, 64 * h:64 * h + 64], src)
            nv[0] += 1
            return nv[0] - 1

        r_qn = vrow2(D["q_norm_w"])
        r_kn = vrow2(D["k_norm_w"])
        r_c2 = vrow(D["conv_w_2"][0].rearrange("i (t p) -> (i t) p", p=128), 12)
        r_cq = vrow(D["mla_cq_gain_2"][0].rearrange("(a p) -> a p", p=128), 2)
        r_ck = vrow(D["mla_ckv_gain_2"][0].rearrange("(a p) -> a p", p=128), 2)
        dc(A, rows4[:, 0:4], D["a_log"].partition_broadcast(128))
        dc(A, rows4[:, 4:8], D["dt_bias"].partition_broadcast(128))
        dc(A, sinkr[:, 0:8], D["sinks"].partition_broadcast(128))
        dc(A, sinkr[:, 8:16], D["win_sink_2"].partition_broadcast(128))
        for n, (o, k) in dict(mla_q_gain_2=(0, 96), mla_k_gain_2=(96, 96), gqa_q_gain_2=(192, 64),
                              gqa_k_gain_2=(256, 64), win_q_gain_2=(320, 64), win_k_gain_2=(384, 64)).items():
            dc(A, gains[:, o:o + k], D[n].partition_broadcast(128))
        brow = alloc(6144)
        modrow = alloc(6144)
        dc(A, brow[0:1, :], D["b_ada"])
        tc_ = (dc.sem, dc.n)
        X = alloc(4, 1024)
        dx = dsem("x")
        tx = dx(G, X, D["x"][0].rearrange("(t p) d -> p t d", p=128))

        BI, BH = alloc(3072), alloc(3 * 1536).bitcast(BF16).rearrange("p (a n) -> p a n", n=3072)
        dbi = dsem("bias_in")
        dbi(G, BI[0:NEXP, 0:2048], D["b_up"][0])
        tbi = dbi(G, BI[0:NEXP, 2048:3072], D["b_down"][0])
        for a in range(3):
            tbi = V(lambda e: e.tensor_copy(BH[0:NEXP, a, :], BI[0:NEXP, :]), tbi)
            if a < 2:
                tbi = V(lambda e: e.tensor_tensor(BI[0:NEXP, :], BI[0:NEXP, :], BH[0:NEXP, a, :], ALU.subtract), tbi)
        dbo = dsem("bias_out")
        tbs = dbo(G, BIASD, BH[0:NEXP], tbi)

        tca = A(lambda e: e.activation(cact, cact, ACT.Silu), tcv)
        V(lambda e: e.memset(ones3, 1.0))

        def modulation(n, first, m, dst, bias, doff):
            for c in range(n):
                s, w, tw = W.take()
                w = w.rearrange("p (k n) -> p k n", n=512)
                b = bank()
                o = PS[b][0:m, :]
                t = T(mms(o, [(cact[:, first:first + m, k], w[:, k, :]) for k in range(8)]), tw, tca, rel[b])
                W.give(s, t)
                q = c * 512
                rel[b] = V(lambda e: e.tensor_tensor(dst[0:m, q:q + 512], o, bias[0:m, q:q + 512], ALU.add), t, tc_)
            return rel[b]

        tm = modulation(12, 0, 1, modrow, brow, 0)
        b = bank()
        t = T(transposes([(PS[b][:, 0:nv[0]], vrows[0:nv[0], :])]), tc_, rel[b])
        tvf = V(lambda e: e.tensor_copy(VF[:, 0:nv[0]], PS[b][:, 0:nv[0]]), t)
        rel[b] = tvf
        dm = dsem("mod")
        tmd = dm(G, MOD.rearrange("(a n) -> a n", a=1), modrow[0:1, :], tm)

        def by_feature(src, dst, n, *deps):
            d = dsem(f"bf{nc.next_id()}")
            t0 = d(G, vrows[0:n, :], src, *deps)
            b = bank()
            t = T(transposes([(PS[b][:, 0:n], vrows[0:n, :])]), t0, rel[b])
            rel[b] = V(lambda e: e.tensor_copy(dst, PS[b][:, 0:n]), t)
            return rel[b], t

        tmf, tvr = by_feature(MOD.rearrange("(a p) -> a p", p=128), modF, 48, tmd, t)
        A1 = small[:, 0:8]
        ta1 = V(lambda e: e.scalar_tensor_tensor(A1, modF[:, 8:16], 1.0, VF[:, r_n1:r_n1 + 8], ALU.add, ALU.mult), tmf, tvf)

        junk = modrow[:, 0:1024]

        def rstd_rows(x, n, st, junk, *deps):
            for i in range(n):
                t = A(lambda e: e.activation(junk, x[:, i, :], ACT.Square, accum_out=st[:, i:i + 1]), *deps, *([t] if i else []))
            t, _ = rsqrt(st[:, 0:n], st[:, 0:n], 1.0 / 1024, t)
            return t

        st = small[:, 8:16]
        t = rstd_rows(X, 4, st, brow[:, 0:1024], tx, tm)
        for i in range(4):
            t = V(lambda e: e.tensor_scalar(X[:, i, :], X[:, i, :], st[:, i:i + 1], None, ALU.mult), t)

        def to_features(src, dst, tcs, off, mul, add, *deps):
            for k in range(8):
                b = bank()
                n = len(tcs) * 128
                t = T(transposes([(PS[b][:, i * 128:i * 128 + 128], src[:, c, k * 128:k * 128 + 128])
                                  for i, c in enumerate(tcs)]), rel[b], *deps)
                o = dst[:, k, off:off + n]
                if mul is None:
                    rel[b] = evac(o, PS[b][:, 0:n], t)
                elif k % 2:
                    rel[b] = V(lambda e: e.tensor_scalar(o, PS[b][:, 0:n], mul[:, k:k + 1], add[:, k:k + 1],
                                                         ALU.mult, ALU.add), t)
                else:
                    rel[b] = A(lambda e: e.activation(o, PS[b][:, 0:n], ACT.Identity, bias=add[:, k:k + 1],
                                                      scale=mul[:, k:k + 1]), t)
            return [V.last(), A.last()]

        top[0] = X_at = base
        barrier(tmd, tbs)
        H1 = alloc(8, 512, at=WORDS - 4096)
        t = to_features(X, H1, range(4), 0, A1, modF[:, 0:8], t, ta1)
        dump("h1T", H1, t)
        barrier()
        th = t
        if stop == "h":
            return fin()

        top[0] = base
        MIX = alloc(8, 512)
        mark = top[0]
        swq = alloc(4, 512)
        swk = alloc(2, 512)
        swv = alloc(4, 128)
        BG = alloc(4, 8)
        swb = alloc(8, 256)
        c1 = alloc(10, 128)
        d1 = dsem("cst1")
        d1(G, swb, D["cst1b"].rearrange("p (a b) -> p a b", b=256))
        tk1 = d1(G, c1, D["cst1"].rearrange("p (a b) -> p a b", b=128))
        M2, M1, BD = c1[:, 0, :], c1[:, 1, :], c1[:, 2, :]

        def gemm_f(w, n0, tok, o, b, *deps):
            return T(mms(o, [(w[:, k, n0:n0 + 128], tok(k)) for k in range(8)]), rel[b], *deps)

        s, w, tw = W.take()
        w = w.rearrange("p (k n) -> p k n", n=512)
        for i in range(4):
            b = bank()
            t = gemm_f(w, i * 128, lambda k: H1[:, k, :], PS[b], b, tw, th)
            rel[b] = evac(swq[:, i, :], PS[b], t)
        W.give(s, t)
        s, w, tw = W.take()
        w = w.rearrange("p (k n) -> p k n", n=512)
        for i in range(2):
            b = bank()
            t = gemm_f(w, 8 + i * 128, lambda k: H1[:, k, :], PS[b], b, tw)
            rel[b] = evac(swk[:, i, :], PS[b], t)
        for i in range(4):
            b = bank()
            t = T(mms(PS[b][:, 0:8], [(H1[:, k, i * 128:i * 128 + 128], w[:, k, 0:8]) for k in range(8)]), rel[b])
            t = T(mms(PS[b][:, 8:136], [(H1[:, k, i * 128:i * 128 + 128], w[:, k, 264:392]) for k in range(8)]))
            V(lambda e: e.tensor_copy(BG[:, i, :], PS[b][:, 0:8]), t)
            rel[b] = V(lambda e: e.tensor_copy(swv[:, i, :], PS[b][:, 8:136]))
        W.give(s, t)
        tmp = alloc(2, 512)
        rs = alloc(2, 512)
        free = [None, None]
        for i in range(6):
            x = swq[:, i, :] if i < 4 else swk[:, i - 4, :]
            g = VF[:, r_qn:r_qn + 1] if i < 4 else VF[:, r_kn:r_kn + 1]
            u = i % 2
            t = A(lambda e: e.activation(tmp[:, u, :], x, ACT.Square), V.last(), A.last(), free[u])
            b = bank()
            t = T(mms(PS[b], [(BD, tmp[:, u, :])]), t, rel[b], tk1)
            t, rel[b] = rsqrt(rs[:, u, :], PS[b], 1.0 / 64, t, free[u])
            free[u] = V(lambda e: e.scalar_tensor_tensor(x, x, g, rs[:, u, :], ALU.mult, ALU.mult), t)
        tn = free[1]
        LG = alloc(2, 4 * 256)
        PT = alloc(2, 4 * 256)
        OS = alloc(4, 512)
        sm = alloc(2, 24)
        for u in range(2):
            t0 = G(lambda e: e.memset(LG[:, u, 0:128], NEG))
        lgf, ptf, smf = [None] * 2, [None] * 2, [None] * 2
        for h in range(8):
            u, p0, kv = h % 2, 64 * (h % 2), h // 4
            lg = LG[:, u, :].rearrange("p (a b) -> p a b", b=256)
            m = sm[:, u, :]
            sk = sinkr[:, h:h + 1]
            for n in range(4):
                lo = max(n - 1, 0) * 128
                N = (n + 1) * 128 - lo
                b = bank()
                q = swq[p0:p0 + 64, h // 2, n * 128:n * 128 + 128]
                k = swk[p0:p0 + 64, kv, lo:lo + N]
                t = T(mms(PS[b][:, 0:N], [(q, k)]), tn, rel[b])
                t = rel[b] = V(lambda e: e.scalar_tensor_tensor(lg[:, n, 256 - N:256], PS[b][:, 0:N], 0.125,
                                                                swb[:, h, 256 - N:256], ALU.mult, ALU.add),
                               t, lgf[u], t0, tk1)
                if n == 0:
                    lg0 = t
            t = V(lambda e: e.tensor_reduce(m[:, 0:4], lg, AX.X, ALU.max), t, smf[u])
            t = V(lambda e: e.tensor_scalar(m[:, 0:4], m[:, 0:4], sk, -1.0, ALU.max, ALU.mult), t)
            for n in range(4):
                kl = slice(0 if n else 128, 256)
                tp = A(lambda e: e.activation(lg[:, n, kl], lg[:, n, kl], ACT.Exp, bias=m[:, n:n + 1],
                                              accum_out=m[:, 4 + n:5 + n]), t, smf[u])
            t = A(lambda e: e.activation(m[:, 8:12], m[:, 0:4], ACT.Exp, bias=sk), t)
            t = V(lambda e: e.tensor_tensor(m[:, 12:16], m[:, 4:8], m[:, 8:12], ALU.add), t, tp)
            tr = V(lambda e: e.reciprocal(m[:, 16:20], m[:, 12:16]), t)
            pt = PT[:, u, :].rearrange("p (a b) -> p a b", b=256)
            for n in range(4):
                b = bank()
                ks = [0, 1] if n else [1]
                t = T(transposes([(PS[b][:, k * 128:k * 128 + 128], lg[:, n, k * 128:k * 128 + 128]) for k in ks]),
                      tp, rel[b])
                lgf[u] = t
                t = rel[b] = evac(pt[:, n, ks[0] * 128:256], PS[b][:, ks[0] * 128:256], t, ptf[u])
                b = bank()
                t = T(mms(PS[b][:, 0:64], [(pt[:, n, k * 128:k * 128 + 128], swv[:, n - 1 + k, kv * 64:kv * 64 + 64])
                                           for k in ks]), t, rel[b], V.last())
                pl = t
                rel[b] = smf[u] = V(lambda e: e.tensor_scalar(OS[:, n, h * 64:h * 64 + 64], PS[b][:, 0:64],
                                                              m[:, 16 + n:17 + n], None, ALU.mult), t, tr)
            ptf[u] = pl
        for k in range(4):
            b = bank()
            t = T(transposes([(PS[b][:, i * 128:i * 128 + 128], OS[:, i, k * 128:k * 128 + 128]) for i in range(4)]),
                  rel[b], V.last())
            rel[b] = evac(MIX[:, 4 + k, :], PS[b], t)
        dump("osT", MIX[:, 4:8, :], V.last(), A.last())
        if stop == "swa":
            return fin()
        barrier()

        top[0] = mark
        BG2 = alloc(4, 8)
        c1n = alloc(10, 128)
        t = V(lambda e: e.tensor_copy(BG2, BG))
        t = V(lambda e: e.tensor_copy(small[:, 16:48].rearrange("p (a b) -> p a b", b=8), BG2), t)
        BG = small[:, 16:48].rearrange("p (a b) -> p a b", b=8)
        barrier()
        top[0] = mark
        c1 = alloc(10, 128)
        tk1 = d1(G, c1, D["cst1"].rearrange("p (a b) -> p a b", b=128), everyone())
        M2, M1 = c1[:, 0, :], c1[:, 1, :]
        QKV = alloc(12, 512)
        ZT = alloc(4, 512)
        gsm = alloc(8, 16)
        g16, bet, eg, kd, bE, ngm = [gsm[:, i, :] for i in range(6)]
        sub = top[0]
        U = alloc(2, 515)
        tz = G(lambda e: e.memset(U[:, :, 0:3], 0.0))
        uf = [None, None]
        for c in range(4):
            s, w, tw = W.take()
            w = w.rearrange("p (k n) -> p k n", n=512)
            for i in range(4):
                b = bank()
                tmm = gemm_f(w, i * 128, lambda k: H1[:, k, :], PS[b], b, tw)
                if c == 3:
                    rel[b] = A(lambda e: e.activation(ZT[:, i, :], PS[b], ACT.Silu), tmm)
                    continue
                n = c * 4 + i
                u = n % 2
                y = QKV[:, n, :]
                t = rel[b] = A(lambda e: e.activation(U[:, u, 3:515], PS[b], ACT.Copy), tmm, uf[u], tz)
                for j in range(4):
                    cw = VF[:, r_cw + j * 12 + n:r_cw + j * 12 + n + 1]
                    uv = U[:, u, j:j + 512]
                    if j == 0:
                        t = V(lambda e: e.tensor_scalar(y, uv, cw, None, ALU.mult), t)
                    else:
                        t = V(lambda e: e.scalar_tensor_tensor(y, uv, cw, y, ALU.mult, ALU.add), t)
                uf[u] = t
                A(lambda e: e.activation(y, y, ACT.Silu), t)
            W.give(s, tmm)
        tq = A.last()
        gv = g16.rearrange("p (a b) -> p a b", b=4)
        bv = bet.rearrange("p (a b) -> p a b", b=4)
        nv_ = ngm.rearrange("p (a b) -> p a b", b=4)
        t = A(lambda e: e.activation(bv, BG[:, :, 4:8], ACT.Sigmoid), V.last())
        dtb = rows4[:, 4:8]
        for i in range(4):
            t1 = V(lambda e: e.tensor_tensor(gv[:, i, :], BG[:, i, 0:4], dtb, ALU.add))
        t2 = A(lambda e: e.activation(ngm, g16, ACT.Abs), t1)
        t2 = A(lambda e: e.activation(ngm, ngm, ACT.Exp, scale=-1.0), t2)
        t3 = A(lambda e: e.activation(rows4[:, 8:12], rows4[:, 0:4], ACT.Exp))
        t2 = V(lambda e: e.tensor_scalar(ngm, ngm, 1.0, None, ALU.add), t2)
        t2 = A(lambda e: e.activation(ngm, ngm, ACT.Ln), t2)
        t2 = V(lambda e: e.scalar_tensor_tensor(g16, g16, 0.0, ngm, ALU.max, ALU.add), t2)
        t2 = V(lambda e: e.tensor_scalar(g16, g16, -1.0, None, ALU.mult), t2)
        for i in range(4):
            tg = V(lambda e: e.tensor_tensor(gv[:, i, :], gv[:, i, :], rows4[:, 8:12], ALU.mult), t2, t3)
        b = bank()
        t = T(mms(PS[b][:, 0:16], [(M1, g16)]), tg, rel[b], tk1)
        t = T(mms(PS[b][:, 16:32], [(M2, g16)]))
        A(lambda e: e.activation(eg, PS[b][:, 0:16], ACT.Exp), t)
        rel[b] = t = A(lambda e: e.activation(kd, PS[b][:, 16:32], ACT.Exp), t)
        tgs = V(lambda e: e.tensor_tensor(bE, bet, eg, ALU.mult), t)
        tmp = alloc(2, 512)
        rs = alloc(2, 512)
        free = [None, None]
        for i in range(8):
            u = i % 2
            x = QKV[:, i, :]
            t = A(lambda e: e.activation(tmp[:, u, :], x, ACT.Square), tq, free[u])
            b = bank()
            t = T(mms(PS[b], [(ones, tmp[:, u, :])]), t, rel[b])
            t, rel[b] = rsqrt(rs[:, u, :], PS[b], 1.0, t, free[u])
            f = 128.0 ** -0.5 if i < 4 else 1.0
            free[u] = V(lambda e: e.scalar_tensor_tensor(x, x, f, rs[:, u, :], ALU.mult, ALU.mult), t)
        dump("qkvT", QKV, V.last())
        if stop == "qkv":
            return fin()
        barrier()

        for hp in range(2):
            top[0] = sub
            heads = [2 * hp, 2 * hp + 1]
            units = [(a, h, i) for a, h in enumerate(heads) for i in range(4)]
            VB, KB, KD = alloc(8, 128), alloc(8, 128), alloc(8, 128)
            EE = alloc(8, 384)
            LT, AQ = alloc(8, 128), alloc(8, 128)
            XX = alloc(8, 256)
            UU, WT = alloc(8, 128), alloc(8, 128)
            ST = alloc(2, 128)
            ZZ = alloc(8, 128)
            GM = alloc(4, 256)
            assert top[0] <= WORDS
            ttok = {}
            for a, h, i in units:
                n = a * 4 + i
                c = i * 4 + h
                tok = slice(i * 128, i * 128 + 128)
                b = bank()
                t = T(transposes([(PS[b][:, 0:128], QKV[:, 8 + h, tok]), (PS[b][:, 128:256], QKV[:, 4 + h, tok])]),
                      rel[b])
                A(lambda e: e.activation(VB[:, n, :], PS[b][:, 0:128], ACT.Copy, scale=bet[:, c:c + 1]), t)
                A(lambda e: e.activation(KB[:, n, :], PS[b][:, 128:256], ACT.Copy, scale=bE[:, c:c + 1]))
                rel[b] = A(lambda e: e.activation(KD[:, n, :], PS[b][:, 128:256], ACT.Copy, scale=kd[:, c:c + 1]))
            gf = [None] * 4
            tE = {}
            for a, h, i in units:
                n = a * 4 + i
                c = i * 4 + h
                gm = GM[:, n % 4, :]
                G(lambda e: e.tensor_scalar(gm[:, 0:128], M2, g16[:, c:c + 1], None, ALU.mult), gf[n % 4])
                t = G(lambda e: e.tensor_scalar(gm[:, 128:256], ones, g16[:, c:c + 1], None, ALU.mult))
                b = bank()
                T(mms(PS[b][:, 0:128], [(M1, gm[:, 0:128])]), t, rel[b])
                T(mms(PS[b][:, 128:256], [(gm[:, 0:128], M1)]))
                t = gf[n % 4] = T(mms(PS[b][:, 256:384], [(gm[:, 128:256], M1)]))
                rel[b] = t = A(lambda e: e.activation(EE[:, n, :], PS[b][:, 0:384], ACT.Exp), t)
                tE[n] = G(lambda e: e.tensor_tensor(EE[:, n, 0:256], EE[:, n, 0:256],
                                                    c1[:, 0:2, :].rearrange("p a b -> p (a b)"), ALU.mult), t)
            tX = {}
            for a, h, i in units:
                n = a * 4 + i
                c = i * 4 + h
                tok = slice(i * 128, i * 128 + 128)
                kT, qT = QKV[:, 4 + h, tok], QKV[:, h, tok]
                b = bank()
                T(mms(PS[b][:, 0:128], [(kT, kT)]), rel[b])
                t = T(mms(PS[b][:, 128:256], [(kT, qT)]))
                L = ZZ[:, n, :]
                tl = V(lambda e: e.scalar_tensor_tensor(L, PS[b][:, 0:128], bet[:, c:c + 1], EE[:, n, 0:128],
                                                        ALU.mult, ALU.mult), t, tE[n])
                rel[b] = V(lambda e: e.tensor_tensor(AQ[:, n, :], PS[b][:, 128:256], EE[:, n, 128:256], ALU.mult))
                tqd = V(lambda e: e.tensor_tensor(qT, qT, EE[:, n, 256:384], ALU.mult), t)
                b = bank()
                t = T(transposes([(PS[b][:, 0:128], L)]), tl, rel[b])
                rel[b] = t = A(lambda e: e.activation(LT[:, n, :], PS[b][:, 0:128], ACT.Copy), t)
                t1 = G(lambda e: e.tensor_tensor(XX[:, n, 0:128], L, c1[:, 9, :], ALU.mult), tl)
                t2 = G(lambda e: e.tensor_tensor(XX[:, n, 128:256], LT[:, n, :], c1[:, 3, :], ALU.mult), t)
                t1 = G(lambda e: e.tensor_tensor(XX[:, n, 0:128], ident, XX[:, n, 0:128], ALU.subtract), t1)
                tX[n] = G(lambda e: e.tensor_tensor(XX[:, n, 128:256], ident, XX[:, n, 128:256], ALU.subtract), t2)
            LB = [alloc(8, 128, at=sub + 0)] if False else None
            for lv in range(1, 6):
                mk = c1[:, 3 + lv, :]
                tb = {}
                for n in range(8):
                    gm = GM[:, n % 4, 0:128]
                    t = G(lambda e: e.tensor_tensor(gm, LT[:, n, :], mk, ALU.mult), gf[n % 4])
                    b = bank()
                    gf[n % 4] = t = T(mms(PS[b][:, 0:128], [(gm, XX[:, n, 0:128])]), t, tX[n], rel[b])
                    rel[b] = tb[n] = A(lambda e: e.activation(ZZ[:, n, :], PS[b][:, 0:128], ACT.Copy), t)
                for n in range(8):
                    b = bank()
                    T(mms(PS[b][:, 0:128], [(XX[:, n, 128:256], ZZ[:, n, :])]), tb[n], rel[b])
                    t = T(mms(PS[b][:, 128:256], [(ZZ[:, n, :], XX[:, n, 128:256])]))
                    rel[b] = tX[n] = V(lambda e: e.tensor_tensor(XX[:, n, :], XX[:, n, :], PS[b][:, 0:256],
                                                                 ALU.subtract), t)
            tU = {}
            for n in range(8):
                XT = XX[:, n, 128:256]
                b = bank()
                T(mms(PS[b][:, 0:128], [(XT, VB[:, n, :])]), tX[n], rel[b])
                t = T(mms(PS[b][:, 128:256], [(KB[:, n, :], XT)]))
                V(lambda e: e.tensor_copy(UU[:, n, :], PS[b][:, 0:128]), t)
                rel[b] = tU[n] = V(lambda e: e.tensor_copy(WT[:, n, :], PS[b][:, 128:256]))
            barrier()
            VN = alloc(2, 128, at=sub + 8 * 128 * 3 + 8 * 384)
            OB = [PS[6], PS[7]]
            tS = [None, None]
            tO = [None, None]
            vf = [None, None]
            for i in range(8):
                n_, hf = i // 2, 64 * (i % 2)
                hs = slice(hf, hf + 64)
                for a, h in enumerate(heads):
                    n = a * 4 + n_
                    vn = VN[:, a, :]
                    sb = ST[:, a, :]
                    q = QKV[:, h, i * 64:i * 64 + 64]
                    if i:
                        b = 3 * a
                        t = T(mms(PS[b][:, 0:128], [(WT[:, n, :], sb)]), tS[a], rel[b])
                        rel[b] = tv = V(lambda e: e.tensor_tensor(vn[hs, :], UU[hs, n, :], PS[b][hs, 0:128],
                                                                  ALU.subtract), t, vf[a])
                    else:
                        tv = V(lambda e: e.tensor_copy(vn[hs, :], UU[hs, n, :]))
                    b = 3 * a + 1 + i % 2
                    t = T(mms(PS[b][:, 0:128], [(KD[hs, n, :], vn[hs, :])]), tv, rel[b])
                    pairs = ([(sb, q)] if i else []) + [(vn[hs, :], AQ[hs, n, hs])]
                    vf[a] = tO[a] = T(mms(OB[a][:, i * 64:i * 64 + 64], pairs))
                    if i:
                        dcol = EE[:, n, 256 + hf + 63:256 + hf + 64]
                        rel[b] = tS[a] = V(lambda e: e.scalar_tensor_tensor(sb, sb, dcol, PS[b][:, 0:128],
                                                                            ALU.mult, ALU.add), t, tO[a])
                    else:
                        rel[b] = tS[a] = V(lambda e: e.tensor_copy(sb, PS[b][:, 0:128]), t)
            rel[6], rel[7] = None, None
            tmp = alloc(2, 512, at=sub)
            rs = alloc(2, 512, at=sub + 1024)
            osb = alloc(2, 512, at=sub + 2048)
            for a, h in enumerate(heads):
                te = A(lambda e: e.activation(osb[:, a, :], OB[a], ACT.Copy), tO[a], tO[0], tO[1])
                t = A(lambda e: e.activation(tmp[:, a, :], OB[a], ACT.Square))
                rel[6 + a] = t
                b = a
                t = T(mms(PS[b], [(ones, tmp[:, a, :])]), t, rel[b])
                t, rel[b] = rsqrt(rs[:, a, :], PS[b], 1.0 / 128, t)
                t = V(lambda e: e.scalar_tensor_tensor(osb[:, a, :], osb[:, a, :], VF[:, r_dn:r_dn + 1], rs[:, a, :],
                                                       ALU.mult, ALU.mult), t, te)
                V(lambda e: e.tensor_tensor(MIX[:, h, :], osb[:, a, :], ZT[:, h, :], ALU.mult), t)
            barrier()
        dump("mixT", MIX, V.last())
        if stop == "mix":
            return fin()

        top[0] = WORDS - 4096 - 12288 - 128
        br2, mr2, vrows = alloc(2, 3072), alloc(2, 3072), alloc(128)
        zero = alloc(1024, at=mark)
        tz = G(lambda e: e.memset(zero, 0.0), everyone())
        dz = dsem("zero")
        for j in range(NXB):
            tz_ = dz(G, YD[(NEXP + j) * 128:(NEXP + j + 1) * 128, :], zero, tz)
        X = alloc(4, 1024, at=WORDS - 4096)
        d2 = dsem("mod2")
        for l in range(2):
            tb2 = d2(G, br2[0:2, l, :], D["mod_b_2"][l:l + 1, :].partition_broadcast(2), everyone())
        tx = dx(G, X, D["x"][0].rearrange("(t p) d -> p t d", p=128))
        tc_ = tb2
        for l in range(2):
            tm = modulation(6, 1, 2, mr2[:, l, :], br2[:, l, :], 0)
            tmd = d2(G, MOD2[l], mr2[0:2, l, :], tm)
            t0, _ = by_feature(MOD2[l].rearrange("r (a p) -> (r a) p", p=128), mod2F[:, l, :], 48, tmd,
                               (T.sem, T.n))
        barrier(tmd, tz_)

        top[0] = mark
        GR = alloc(1024)
        TM = alloc(2, 512)
        dg = dsem("gate")
        tg = dg(G, GR, MOD[2048:3072].rearrange("(a n) -> a n", a=1).partition_broadcast(128), everyone())

        def project(src, tcs, x_of, gate_of, *deps):
            f = [None, None]
            for c in range(2):
                s, w, tw = W.take()
                w = w.rearrange("p (k n) -> p k n", n=512)
                for i in tcs:
                    b = bank()
                    t = T(mms(PS[b], [(src[:, k, i * 128:i * 128 + 128], w[:, k, :]) for k in range(8)]), tw, rel[b])
                    u = i % 2
                    gr = gate_of(i)[:, c * 512:c * 512 + 512]
                    xo = x_of(i)[:, c * 512:c * 512 + 512]
                    rel[b] = tt = V(lambda e: e.tensor_tensor(TM[:, u, :], PS[b], gr, ALU.mult), t, f[u], *deps)
                    f[u] = V(lambda e: e.tensor_tensor(xo, xo, TM[:, u, :], ALU.add), tt)
                W.give(s, t)
            return f

        t = project(MIX, range(4), lambda i: X[:, i, :], lambda i: GR, tg, tx)
        dump("x1", X, t)
        barrier()
        if stop == "x1":
            return fin()

        top[0] = base
        A2, B2, N2 = alloc(1024), alloc(1024), alloc(1024)
        H2 = alloc(4, 1024)
        H2T = alloc(8, 512)
        c2 = alloc(128 + 128 + 32 + NXB * 32 + 4)
        wr = alloc(8, 32)
        brt = alloc(32)
        dr = dsem("rt")
        row = lambda a: a.rearrange("(a n) -> a n", a=1).partition_broadcast(128)
        ev = everyone()
        dr(G, A2, row(MOD[4096:5120]), ev)
        dr(G, B2, row(MOD[3072:4096]))
        dr(G, N2, D["norm2_w"].partition_broadcast(128))
        dr(G, c2, D["cst2"])
        dr(G, wr, kp(D["w_router"][0]))
        tr = dr(G, brt, D["b_router"].partition_broadcast(128))
        ta = V(lambda e: e.scalar_tensor_tensor(A2, A2, 1.0, N2, ALU.add, ALU.mult), tr)
        st = small[:, 8:16]
        t = rstd_rows(X, 4, st, H2[:, 0, :], None)
        dh = dsem("h2")
        for i in range(4):
            th = V(lambda e: e.scalar_tensor_tensor(H2[:, i, :], X[:, i, :], st[:, i:i + 1], A2, ALU.mult, ALU.mult), t, ta)
            th = V(lambda e: e.tensor_tensor(H2[:, i, :], H2[:, i, :], B2, ALU.add), th)
            td = dh(G, H2D[i * 128:i * 128 + 128, :], H2[:, i, :], th)
        t = to_features(H2, H2T, range(4), 0, None, None, th)
        U_, I128 = c2[:, 0:128], c2[:, 128:256]
        B0 = c2[:, 256:288]
        JJ = c2[:, 288:288 + NXB * 32].rearrange("p (a b) -> p a b", b=32)
        TID = c2[:, 288 + NXB * 32:292 + NXB * 32]
        LGT = rout
        for i in range(4):
            b = bank()
            t1 = T(mms(PS[b][:, 0:32], [(H2T[:, k, i * 128:i * 128 + 128], wr[:, k, :]) for k in range(8)]), t, tr, rel[b])
            rel[b] = tl = V(lambda e: e.tensor_tensor(LGT[:, i, :], PS[b][:, 0:32], brt, ALU.add), t1)
        dump("logits", LGT, tl)
        V8 = alloc(4, 8)
        I8 = alloc(4, 8, dt=U32)
        I8f = alloc(4, 8)
        OH = alloc(16, 32)
        MM = alloc(4, 32)
        POS = alloc(4, 32)
        CN, NX, CS, BD1 = alloc(32), alloc(32), alloc(32), alloc(32)
        SL = alloc(4, 32)
        T5 = alloc(NXB, 32)
        DF = alloc(16)
        DI = alloc(2, 16, dt=I32)
        DIF = alloc(2, 16)
        gs = alloc(16)
        for i in range(4):
            t = V(lambda e: e.max(V8[:, i, :], LGT[:, i, :]), tl)
            t = V(lambda e: e.max_index(I8[:, i, :], V8[:, i, :], LGT[:, i, :]), t)
        t = V(lambda e: e.tensor_copy(I8f, I8), t)
        for i in range(4):
            for k in range(4):
                to = V(lambda e: e.tensor_scalar(OH[:, i * 4 + k, :], I128[:, 0:32], I8f[:, i, k:k + 1], None,
                                                 ALU.is_equal), t, tr)
        O4 = OH.rearrange("p (i k) e -> p i k e", k=4)
        t = V(lambda e: e.tensor_tensor(MM, O4[:, :, 0, :], O4[:, :, 1, :], ALU.add), to)
        t = V(lambda e: e.tensor_tensor(MM, MM, O4[:, :, 2, :], ALU.add), t)
        tmk = V(lambda e: e.tensor_tensor(MM, MM, O4[:, :, 3, :], ALU.add), t)
        b = bank()
        for i in range(4):
            t = T(mms(PS[b][:, i * 32:i * 32 + 32], [(U_, MM[:, i, :])] + [(ones, MM[:, q, :]) for q in range(i)]), tmk, rel[b])
        t = T(mms(PS[b][:, 128:160], [(ones, MM[:, q, :]) for q in range(4)]))
        V(lambda e: e.tensor_copy(POS, PS[b][:, 0:128].rearrange("p (a b) -> p a b", b=32)), t)
        rel[b] = t = V(lambda e: e.tensor_copy(CN, PS[b][:, 128:160]))
        t = V(lambda e: e.tensor_scalar(NX, CN, 128.0, None, ALU.is_gt), t)
        t = V(lambda e: e.scalar_tensor_tensor(NX, CN, 256.0, NX, ALU.is_gt, ALU.add), t)
        t = V(lambda e: e.scalar_tensor_tensor(NX, CN, 384.0, NX, ALU.is_gt, ALU.add), t)
        t = V(lambda e: e.tensor_tensor_scan(CS, ones[:, 0:32], NX, 0.0, ALU.mult, ALU.add), t)
        t1 = V(lambda e: e.tensor_tensor(BD1, CS, NX, ALU.subtract), t)
        t1 = V(lambda e: e.tensor_scalar(BD1, BD1, 128.0, 128.0 * (NEXP - 1), ALU.mult, ALU.add), t1)
        t1 = V(lambda e: e.tensor_tensor(BD1, BD1, B0, ALU.subtract), t1)
        bc = lambda v, n: v.unsqueeze(1).to_broadcast([128, n, 32])
        t5 = V(lambda e: e.tensor_tensor(T5, bc(CS, NXB), JJ, ALU.is_le), t)
        t5 = V(lambda e: e.tensor_reduce(gs[:, 0:NXB], T5, AX.X, ALU.add), t5)
        t5 = V(lambda e: e.tensor_scalar(gs[:, 0:NXB], gs[:, 0:NXB], float(NEXP - 1), None, ALU.min), t5)
        V(lambda e: e.tensor_copy(XE[:, 0:NXB], gs[:, 0:NXB]), t5)
        txe = V(lambda e: e.tensor_copy(XE[:, NXB:NXB + 1], CS[:, 31:32]))
        t = V(lambda e: e.tensor_scalar(SL, POS, 128.0, None, ALU.is_ge), t1)
        t = V(lambda e: e.tensor_tensor(SL, SL, bc(BD1, 4), ALU.mult), t)
        t = V(lambda e: e.tensor_tensor(SL, SL, POS, ALU.add), t)
        ts = V(lambda e: e.tensor_tensor(SL, SL, bc(B0, 4), ALU.add), t)
        for i in range(4):
            t = V(lambda e: e.tensor_tensor(O4[:, i, :, :], O4[:, i, :, :], bc(SL[:, i, :], 4), ALU.mult), ts)
        t = V(lambda e: e.tensor_reduce(DF, OH, AX.X, ALU.add), t)
        td1 = V(lambda e: e.tensor_copy(DEST, DF), t)
        V(lambda e: e.tensor_scalar(DI[:, 0, :], DEST, 7, None, ALU.logical_shift_right), td1)
        t = V(lambda e: e.tensor_scalar(DI[:, 1, :], DEST, 127, None, ALU.bitwise_and))
        tdf = V(lambda e: e.tensor_copy(DIF, DI), t)
        OP = alloc(2, 128)
        OBK = alloc(2, 48)
        opf = [None, None]
        b = bank()
        rb = rel[b]
        for n in range(16):
            u = n % 2
            V(lambda e: e.tensor_scalar(OP[:, u, :], I128, DIF[:, 1, n:n + 1], None, ALU.is_equal), tdf, opf[u])
            t = V(lambda e: e.tensor_scalar(OBK[:, u, 0:NBLK], I128[:, 0:NBLK], DIF[:, 0, n:n + 1],
                                            TID[:, n // 4:n // 4 + 1], ALU.is_equal, ALU.mult))
            T.wait(t, rb)
            opf[u] = T(lambda e: e.matmul(PS[b][:, 0:NBLK], OP[:, u, :], OBK[:, u, 0:NBLK], start=(n == 0), stop=(n == 15)))
        rel[b] = trow = V(lambda e: e.tensor_copy(ROW[:, 0:NBLK], PS[b][:, 0:NBLK]), opf[1])
        gf_ = gs
        for i in range(4):
            t = V(lambda e: e.tensor_scalar(gs[:, i:i + 1], V8[:, i, 0:1], -1.0, None, ALU.mult), V.last())
            t = A(lambda e: e.activation(GT[:, i, :], V8[:, i, 0:4], ACT.Exp, bias=gs[:, i:i + 1], accum_out=gs[:, 4 + i:5 + i]), t)
            t = V(lambda e: e.reciprocal(gs[:, 8 + i:9 + i], gs[:, 4 + i:5 + i]), t)
            tgt = V(lambda e: e.tensor_scalar(GT[:, i, :], GT[:, i, :], gs[:, 8 + i:9 + i], None, ALU.mult), t)
        dump("gt", GT, tgt)
        dump("dest", DEST, tgt)
        dump("row", ROW[:, 0:NBLK], tgt)
        dump("xe", XE, tgt)
        barrier(td)
        if stop == "route":
            return fin()

        top[0] = base
        XG, XGT = alloc(2, 1024), alloc(2, 1024)
        T1, SG, T2 = alloc(1024), alloc(1024), alloc(1024)
        ACTV, ACTT = alloc(1024), alloc(1024)
        Y = alloc(2, 1024)
        BU = alloc(NBU * 1536).bitcast(BF16).rearrange("p (a n) -> p a n", n=3072)
        assert top[0] <= WORDS - 4096

        def expert_steps(w, gather_sem, bias_sem, store_sem):
            gathered, biased, x_turned, x_copied, up_done, glu_read, lin_read = [], [], [], [], [], [], []
            act_done, a_turned, a_copied, down_done, y_copied, stored = [], [], [], [], [], []

            def before(steps, i):
                return steps[i] if i >= 0 else None

            def gather(i, col):
                gathered.append(gather_sem[i % 2](G, None, None, before(x_turned, 2 * (i - 2) + 1), f=lambda e: e.indirect_dma_start(
                    XG[:, i % 2, :], None, H2D, bass.IndirectOffsetOnAxis(ap=ROW[:, col:col + 1], axis=0))))

            def biases(i, rows):
                biased.append(bias_sem[i % NBU](G, BU[0:3, i % NBU, :], rows, before(down_done, i - NBU)))

            def turn_x(i, hh):
                u, n = i % 2, 2 * i + hh
                x_turned.append(T(transposes([(PS[4][:, q * 128:q * 128 + 128], XG[:, u, (hh * 4 + q) * 128:(hh * 4 + q + 1) * 128])
                                              for q in range(4)]), gathered[i], before(x_copied, n - 1)))
                x_copied.append(V(lambda e: e.tensor_copy(XGT[:, u, hh * 512:hh * 512 + 512], PS[4]), x_turned[n],
                                  before(up_done, i - 2)))

            def up(i, between):
                u = i % 2
                T.wait(biased[i], before(glu_read, i - 1), before(lin_read, i - 1))

                def bias_rows(e):
                    for n in range(4):
                        r = e.matmul(PS[n], ones3[0:3, :], BU[0:3, i % NBU, n * 512:n * 512 + 512], start=True, stop=False)
                    return r
                T(bias_rows)
                for q in range(4):
                    s, wt, loaded = w.take()
                    wt = wt.rearrange("p (k n) -> p k n", n=2048)

                    def products(e):
                        for kk in range(2):
                            k = 2 * q + kk
                            for n in range(4):
                                r = e.matmul(PS[n], XGT[:, u, k * 128:k * 128 + 128], wt[:, kk, n * 512:n * 512 + 512],
                                             start=False, stop=(k == 7))
                        return r
                    t = T(products, loaded, x_copied[2 * i + q // 2])
                    w.give(s, t)
                    between(q)
                up_done.append(t)
                for n in range(2):
                    c = slice(n * 512, n * 512 + 512)
                    ta = V(lambda e: e.tensor_scalar(T1[:, c], PS[n], 7.0, None, ALU.min), up_done[i], before(act_done, i - 1))
                    sg = A(lambda e: e.activation(SG[:, c], T1[:, c], ACT.Sigmoid, scale=1.702), ta, before(act_done, i - 1))
                glu_read.append(ta)
                for n in range(2):
                    c = slice(n * 512, n * 512 + 512)
                    tb = V(lambda e: e.tensor_scalar(T2[:, c], PS[2 + n], 7.0, -7.0, ALU.min, ALU.max), up_done[i])
                lin_read.append(tb)
                tb = V(lambda e: e.scalar_tensor_tensor(T2, T2, 1.0, T1, ALU.add, ALU.mult), tb, ta)
                act_done.append(V(lambda e: e.tensor_tensor(ACTV, T2, SG, ALU.mult), tb, sg, before(a_turned, 2 * (i - 1) + 1)))

            def turn_a(i, hh):
                n = 2 * i + hh
                a_turned.append(T(transposes([(PS[5][:, q * 128:q * 128 + 128], ACTV[:, (hh * 4 + q) * 128:(hh * 4 + q + 1) * 128])
                                              for q in range(4)]), act_done[i], before(a_copied, n - 1)))
                a_copied.append(V(lambda e: e.tensor_copy(ACTT[:, hh * 512:hh * 512 + 512], PS[5]), a_turned[n],
                                  before(down_done, i - 1)))

            def down(i, col):
                u = i % 2
                T.wait(before(y_copied, i - 1))

                def bias_rows(e):
                    for n in range(2):
                        r = e.matmul(PS[6 + n], ones3[0:3, :], BU[0:3, i % NBU, 2048 + n * 512:2560 + n * 512], start=True, stop=False)
                    return r
                T(bias_rows)
                for q in range(2):
                    s, wt, loaded = w.take()
                    wt = wt.rearrange("p (k n) -> p k n", n=1024)

                    def products(e):
                        for kk in range(4):
                            k = 4 * q + kk
                            for n in range(2):
                                r = e.matmul(PS[6 + n], ACTT[:, k * 128:k * 128 + 128], wt[:, kk, n * 512:n * 512 + 512],
                                             start=False, stop=(k == 7))
                        return r
                    t = T(products, loaded, a_copied[2 * i + q])
                    w.give(s, t)
                down_done.append(t)
                for n in range(2):
                    ty = A(lambda e: e.activation(Y[:, u, n * 512:n * 512 + 512], PS[6 + n], ACT.Copy), t, before(stored, i - 2))
                y_copied.append(ty)
                stored.append(store_sem[u](G, YD[col * 128:col * 128 + 128, :], Y[:, u, :], ty))
                return stored[i]

            return gather, biases, turn_x, up, turn_a, down

        def expert_sems(tag):
            return [[dsem(f"{n}{tag}{i}") for i in range(c)] for n, c in (("gather", 2), ("bias", NBU), ("store", 2))]

        gather, biases, turn_x, up, turn_a, down = expert_steps(W, *expert_sems("a"))
        for i in range(NBU):
            biases(i, BIASD[i])
        for i in range(2):
            gather(i, i)
        turn_x(0, 0)
        turn_x(0, 1)
        stored = [None, None]
        for i in range(NEXP):
            def between(q):
                if q < 2 and i:
                    turn_a(i - 1, q)
                if q >= 2 and i + 1 < NEXP:
                    turn_x(i + 1, q - 2)
            up(i, between)
            if i + 2 < NEXP:
                gather(i + 2, i + 2)
            if i:
                stored[(i - 1) % 2] = down(i - 1, i - 1)
                if i - 1 + NBU < NEXP:
                    biases(i - 1 + NBU, BIASD[i - 1 + NBU])
        turn_a(NEXP - 1, 0)
        turn_a(NEXP - 1, 1)
        stored[1] = down(NEXP - 1, NEXP - 1)
        barrier(stored)

        main = [(e.sem, e.n, dict(e.seen)) for e in EN]
        S.wait(everyone())
        xsem = [sem("x_" + n) for n in names]
        loads[:] = []
        proto = Stream("x")
        extra_sems = expert_sems("x")
        counted = [proto.sems] + extra_sems

        def extras(E):
            for e, q in zip(EN, xsem):
                e.sem, e.n, e.on, e.seen = q, 0, e is E, {}
            loads[:] = []
            for grp in counted:
                for q in grp:
                    q.n = 0
            proto.issued = proto.taken = 0
            proto.free = [None] * NSLOT
            gather, biases, turn_x, up, turn_a, down = expert_steps(proto, *extra_sems)
            eng = E.eng
            cnt = eng.value_load(XE[0:1, NXB:NXB + 1], min_val=0, max_val=NXB)
            for j in range(NXB):
                with eng.If(cnt > j):
                    if E is S or E is G:
                        ex = eng.value_load(XE[0:1, j:j + 1], min_val=0, max_val=NEXP - 1)
                        w1 = D["w_up"][0, bass.ds(ex, 1)].rearrange("a k n -> (a k) n")
                        w2 = D["w_down"][0, bass.ds(ex, 1)].rearrange("a k n -> (a k) n")
                        b3 = BIASD[bass.ds(ex, 1)].rearrange("a k n -> (a k) n")
                    else:
                        w1, w2, b3 = D["w_up"][0, 0], D["w_down"][0, 0], BIASD[0]
                    loads.extend(up_loads(w1) + down_loads(w2))
                    gather(j, NEXP + j)
                    biases(j, b3)
                    while proto.issued < proto.taken + NSLOT and proto.issued < len(loads):
                        proto.issue()
                    turn_x(j, 0)
                    turn_x(j, 1)
                    up(j, lambda q: None)
                    turn_a(j, 0)
                    turn_a(j, 1)
                    stored = down(j, NEXP + j)
                    E.wait(*[(q, e.n) for e, q in zip(EN[:4], xsem)], stored)

        with nc.Block() as block:
            @block.tensor
            def _(e):
                extras(T)

            @block.vector
            def _(e):
                extras(V)

            @block.scalar
            def _(e):
                extras(A)

            @block.gpsimd
            def _(e):
                extras(G)

            @block.sync
            def _(e):
                extras(S)
        for e, (q, n, seen) in zip(EN, main):
            e.sem, e.n, e.seen, e.on = q, n, seen, True
        rel[:] = [None] * 8
        loads[:] = later
        W = Stream("b")
        for _ in range(NSLOT):
            W.issue()

        top[0] = base
        XC = alloc(2, 1024)
        YG = alloc(4, 1024)
        GR = alloc(1024)
        ACC = alloc(2, 1024)
        d3 = dsem("late")
        t3 = d3(G, GR, MOD[5120:6144].rearrange("(a n) -> a n", a=1).partition_broadcast(128))
        t3 = d3(G, XC, D["ctx_2"][0].rearrange("(t p) d -> p t d", p=128))
        dyg = [dsem(f"yg{k}") for k in range(4)]
        yf = [None] * 4
        af = [None] * 2
        for i in range(4):
            acc = ACC[:, i % 2, :]
            for k in range(4):
                n = i * 4 + k
                ty = dyg[k](G, None, None, yf[k], f=lambda e: e.indirect_dma_start(
                    YG[:, k, :], None, YD, bass.IndirectOffsetOnAxis(ap=DEST[:, n:n + 1], axis=0)))
                if k == 0:
                    t = V(lambda e: e.tensor_scalar(acc, YG[:, k, :], GT[:, i, 0:1], None, ALU.mult), ty, af[i % 2])
                else:
                    t = V(lambda e: e.scalar_tensor_tensor(acc, YG[:, k, :], GT[:, i, k:k + 1], acc, ALU.mult, ALU.add), ty, t)
                yf[k] = t
            t = V(lambda e: e.tensor_tensor(acc, acc, GR, ALU.mult), t, t3)
            af[i % 2] = V(lambda e: e.tensor_tensor(X[:, i, :], X[:, i, :], acc, ALU.add), t)
        dump("x2", X, V.last())
        barrier(t3)
        if stop == "x2":
            return fin()

        xrow = lambda i: X[:, i, :] if i < 4 else XC[:, i - 4, :]

        def adaln(l, HT, XN):
            st = small[:, 8:16]
            for i in range(6):
                t = A(lambda e: e.activation(XN[:, 0, :], xrow(i), ACT.Square, accum_out=st[:, i:i + 1]), *([t] if i else []))
            t, _ = rsqrt(st[:, 0:6], st[:, 0:6], 1.0 / 1024, t)
            for i in range(6):
                t1 = V(lambda e: e.tensor_scalar(XN[:, i, :], xrow(i), st[:, i:i + 1], None, ALU.mult), t)
            mp = small[:, 16:32]
            m2 = mod2F[:, l, :].rearrange("p (r a) -> p r a", a=24)
            t2 = V(lambda e: e.tensor_scalar(mp.rearrange("p (r a) -> p r a", a=8), m2[:, :, 8:16], 1.0, None, ALU.add))
            to_features(XN, HT, range(4), 0, mp[:, 0:8], m2[:, 0, 0:8], t1, t2)
            return to_features(XN, HT, range(4, 6), 512, mp[:, 8:16], m2[:, 1, 0:8])

        def gemm_t(HT, w, n0, n, tcs, dst, *deps, func=None):
            for i in tcs:
                b = bank()
                t = T(mms(PS[b][:, 0:n], [(HT[:, k, i * 128:i * 128 + 128], w[:, k, n0:n0 + n]) for k in range(8)]),
                      rel[b], *deps)
                if func is None:
                    rel[b] = evac(dst(i), PS[b][:, 0:n], t)
                else:
                    rel[b] = A(lambda e: e.activation(dst(i), PS[b][:, 0:n], func), t)
            return t

        def head_norm(x, H, d, gain, scale, sq, st, *deps):
            x3 = x.rearrange("p (h d) -> p h d", d=d)
            s3 = sq[:, 0:H * d].rearrange("p (h d) -> p h d", d=d)
            t = V(lambda e: e.tensor_tensor(s3, x3, x3, ALU.mult), *deps)
            t = V(lambda e: e.tensor_reduce(st[:, 0:H], s3, AX.X, ALU.add), t)
            t, _ = rsqrt(st[:, 0:H], st[:, 0:H], 1.0 / d, t)
            t = V(lambda e: e.tensor_tensor(x3, x3, st[:, 0:H].unsqueeze(2).to_broadcast([128, H, d]), ALU.mult), t)
            return V(lambda e: e.scalar_tensor_tensor(x3, x3, scale, gain.unsqueeze(1).to_broadcast([128, H, d]),
                                                      ALU.mult, ALU.mult), t)

        def rope(x, H, d, off, r, i, big, tmp, *deps):
            o = 0 if big else 256
            n = 2 * r
            x3 = x.rearrange("p (h d) -> p h d", d=d)
            w = 64 * 4 // (1 if big else 2) // 2
            cs = c3[:, o + i * n:o + i * n + n].rearrange("p (a r) -> p a r", r=r)
            sn = c3[:, o + 4 * n + i * n:o + 4 * n + i * n + n].rearrange("p (a r) -> p a r", r=r)
            for ax in range(2):
                x1 = x3[:, :, off + ax * n:off + ax * n + r]
                x2 = x3[:, :, off + ax * n + r:off + ax * n + n]
                c = cs[:, ax, :].unsqueeze(1).to_broadcast([128, H, r])
                s = sn[:, ax, :].unsqueeze(1).to_broadcast([128, H, r])
                ta, tb, tc, td = [tmp[:, q * H * r:(q + 1) * H * r].rearrange("p (h r) -> p h r", r=r) for q in range(4)]
                V(lambda e: e.tensor_tensor(ta, x1, c, ALU.mult), *deps)
                V(lambda e: e.tensor_tensor(tb, x2, s, ALU.mult))
                V(lambda e: e.tensor_tensor(tc, x2, c, ALU.mult))
                t = V(lambda e: e.tensor_tensor(td, x1, s, ALU.mult))
                V(lambda e: e.tensor_tensor(x1, ta, tb, ALU.subtract), t)
                t = V(lambda e: e.tensor_tensor(x2, tc, td, ALU.add), t)
                deps = (t,)
            return t

        def heads_t(src, H, d, dst, tcs, *deps):
            for h in range(H):
                for g in range(0, len(tcs), 4):
                    part = list(tcs)[g:g + 4]
                    b = bank()
                    t = T(transposes([(PS[b][0:d, q * 128:q * 128 + 128], src(i)[:, h * d:h * d + d])
                                      for q, i in enumerate(part)]), rel[b], *deps)
                    lo = part[0] * 128
                    rel[b] = evac(dst[0:d, h, lo:lo + len(part) * 128], PS[b][0:d, 0:len(part) * 128], t)

        def attention(units, PB, PTB, sb):
            scored = []

            def score(x):
                q, ks, lo, n, vs, masks, sink, o, gate = units[x]
                p = PP[x % 2]
                T.wait(before(exped, x - 2))
                for k, at in ks:
                    t = T(lambda e: e.matmul(p[:, at:at + k.shape[1]], q, k, start=True, stop=True))
                for m, at in masks:
                    t = V(lambda e: e.tensor_tensor(p[:, at:at + 128], p[:, at:at + 128], m, ALU.add), t)
                scored.append(t)

            exped, summed, turned, copied, valued, taken = [], [], [], [], [], []

            def before(steps, x):
                return steps[x] if x >= 0 else None

            def soften(x):
                q, ks, lo, n, vs, masks, sink, o, gate = units[x]
                u = x % 2
                p = PP[u]
                m = sb[:, u * 8:u * 8 + 8]
                t = V(lambda e: e.tensor_reduce(m[:, 0:1], p[:, lo:lo + n], AX.X, ALU.max), scored[x], before(taken, x - 2))
                if sink is not None:
                    t = V(lambda e: e.tensor_scalar(m[:, 0:1], m[:, 0:1], sink, -1.0, ALU.max, ALU.mult), t)
                else:
                    t = V(lambda e: e.tensor_scalar(m[:, 0:1], m[:, 0:1], -1.0, None, ALU.mult), t)
                exped.append(A(lambda e: e.activation(PB[:, u, 0:n], p[:, lo:lo + n], ACT.Exp, bias=m[:, 0:1],
                                                      accum_out=m[:, 1:2]), t, before(turned, x - 2)))
                t = exped[x]
                if sink is not None:
                    t = A(lambda e: e.activation(m[:, 2:3], m[:, 0:1], ACT.Exp, bias=sink), t)
                    t = V(lambda e: e.tensor_tensor(m[:, 1:2], m[:, 1:2], m[:, 2:3], ALU.add), t)
                summed.append(V(lambda e: e.reciprocal(m[:, 3:4], m[:, 1:2]), t))

            def turn(x):
                q, ks, lo, n, vs, masks, sink, o, gate = units[x]
                u, pt = x % 2, PP[2]
                turned.append(T(transposes([(pt[:, k * 128:k * 128 + 128], PB[:, u, k * 128:k * 128 + 128])
                                            for k in range(n // 128)]), exped[x], before(copied, x - 1)))
                if x % 2:
                    copied.append(V(lambda e: e.tensor_copy(PTB[:, u, 0:n], pt[:, 0:n]), turned[x], before(valued, x - 2)))
                else:
                    copied.append(A(lambda e: e.activation(PTB[:, u, 0:n], pt[:, 0:n], ACT.Copy), turned[x], before(valued, x - 2)))

            def value(x):
                q, ks, lo, n, vs, masks, sink, o, gate = units[x]
                u = x % 2
                ob = PS[6 + u][:, 0:64]
                valued.append(T(mms(ob, [(PTB[:, u, k * 128:k * 128 + 128], vs[k]) for k in range(n // 128)]),
                                copied[x], before(taken, x - 2)))
                taken.append(V(lambda e: e.scalar_tensor_tensor(o, ob, sb[:, u * 8 + 3:u * 8 + 4], gate, ALU.mult, ALU.mult),
                               valued[x], summed[x]))

            score(0)
            for x in range(len(units)):
                soften(x)
                if x + 1 < len(units):
                    score(x + 1)
                if x:
                    value(x - 1)
                turn(x)
            value(len(units) - 1)

        mark = base + 2048
        top[0] = mark
        c3 = alloc(640)
        t3 = d3(G, c3, D["cst3"])
        GTE = alloc(6, 1024)
        CQ = alloc(4, 768)
        KR = alloc(6, 32)
        m1 = top[0]
        GKV = alloc(6, 256)
        GQ = alloc(6, 512)
        m2 = top[0]
        HT = alloc(8, 768)
        end = top[0]
        XN = alloc(6, 1024, at=mark + 640)
        assert end <= WORDS - 4096
        th = adaln(0, HT, XN)
        barrier(t3)
        x512 = lambda w: w.rearrange("p (k n) -> p k n", n=512)
        s, w, tw = W.take()
        W.give(s, gemm_t(HT, x512(w), 0, 512, range(6), lambda i: GQ[:, i, :], tw))
        s, w, tw = W.take()
        gemm_t(HT, x512(w), 0, 32, range(6), lambda i: KR[:, i, :], tw)
        W.give(s, gemm_t(HT, x512(w), 32, 256, range(6), lambda i: GKV[:, i, :]))
        s, w, tw = W.take()
        w = x512(w)
        for i in range(4):
            for lo, n in ((0, 512), (512, 256)):
                b = bank()
                t = gemm_f(w, i * 128, lambda k: HT[:, k, lo:lo + n], PS[b][:, 0:n], b, tw)
                rel[b] = evac(CQ[:, i, lo:lo + n], PS[b][:, 0:n], t)
        W.give(s, t)
        for c in range(2):
            s, w, tw = W.take()
            W.give(s, gemm_t(HT, x512(w), 0, 512, range(6), lambda i: GTE[:, i, c * 512:c * 512 + 512], tw, func=ACT.Silu))
        barrier()
        top[0] = m2
        SQ = alloc(768)
        ss = alloc(16)
        rt = alloc(1024)
        for i in range(6):
            t = head_norm(GQ[:, i, :], 8, 64, gains[:, 192:256], 0.125, SQ, ss, V.last())
            if i < 4:
                t = rope(GQ[:, i, :], 8, 64, 0, 16, i, True, rt, t)
            t = head_norm(GKV[:, i, 0:128], 2, 64, gains[:, 256:320], 1.0, SQ, ss, t)
            if i < 4:
                t = rope(GKV[:, i, 0:128], 2, 64, 0, 16, i, True, rt, t)
        dump("gq", GQ, t)
        barrier()
        top[0] = m2
        QT = alloc(8, 768)
        KT = alloc(2, 768)
        assert top[0] + 0 <= WORDS - 4096, top[0]
        heads_t(lambda i: GQ[:, i, :], 8, 64, QT, range(6))
        heads_t(lambda i: GKV[:, i, 0:128], 2, 64, KT, range(6))
        barrier()
        gq_at = m1 + 6 * 256
        PB = alloc(2, 768, at=gq_at)
        PTB = alloc(2, 768, at=gq_at + 1536)
        sb = alloc(16, at=mark + 640 + 6144 + 3072 + 192 - 0) if False else small[:, 32:48]

        def dense(H, qs, kts, vals, off):
            units = []
            for h in range(H):
                for i in range(6):
                    q = qs(h)[:, i * 128:i * 128 + 128]
                    o = GTE[:, i, off + h * 64:off + h * 64 + 64]
                    if i < 4:
                        units.append((q, [(kts(h)[:, 0:512], 0), (kts(h)[:, 512:768], 512)], 0, 768,
                                      [vals(h, k) for k in range(6)], [], None, o, o))
                    else:
                        units.append((q, [(kts(h)[:, 512:768], 512)], 512, 256,
                                      [vals(h, k) for k in (4, 5)], [], None, o, o))
            return units

        attention(dense(8, lambda h: QT[0:64, h, :], lambda h: KT[0:64, h // 4, :],
                        lambda h, k: GKV[:, k, 128 + 64 * (h // 4):192 + 64 * (h // 4)], 512), PB, PTB, sb)
        dump("gte", GTE, V.last())
        rel[:] = [None] * 8
        barrier()
        if stop == "gqa":
            return fin()
        top[0] = m1
        s, w, tw = W.take()
        wq = w[:, 0:1536].rearrange("p (k n) -> p k n", n=768)
        wkv = w[:, 1536:3584].rearrange("p (k n) -> p k n", n=1024)
        tmp = alloc(2, 768)
        rs = alloc(768)
        for a in range(2):
            for i in range(2):
                t = A(lambda e: e.activation(tmp[:, i, :], CQ[:, 2 * a + i, :], ACT.Square), V.last(), T.last())
            g0 = r_cq if a == 0 else r_ck
            for lo, n in ((0, 512), (512, 256)):
                b = bank()
                t1 = T(mms(PS[b][:, 0:n], [(ones, tmp[:, i, lo:lo + n]) for i in range(2)]), t, rel[b])
                t2, rel[b] = rsqrt(rs[:, lo:lo + n], PS[b][:, 0:n], 1.0 / 256, t1, V.last())
            for i in range(2):
                x = CQ[:, 2 * a + i, :]
                V(lambda e: e.scalar_tensor_tensor(x, x, VF[:, g0 + i:g0 + i + 1], rs, ALU.mult, ALU.mult), t2)
        barrier()
        for hh in range(2):
            top[0] = m1
            VA = alloc(6, 256)
            QT, KT = alloc(4, 768), alloc(4, 768)
            PB = alloc(2, 768)
            m3 = top[0]
            QA = alloc(6, 384, at=m3)
            KA = alloc(6, 384, at=m3 + 2304)
            PTB = alloc(2, 768, at=m3)
            SQ, ss, rt = PB[:, 0, :], small[:, 48:56], PB[:, 1, :]
            assert m3 + 4608 <= WORDS - 4096, m3
            for i in range(6):
                tok = slice(i * 128, i * 128 + 128)
                b = bank()
                t = T(mms(PS[b][:, 0:384], [(CQ[:, k, tok], wq[:, k, hh * 384:hh * 384 + 384]) for k in range(2)]), tw, rel[b])
                rel[b] = evac(QA[:, i, :], PS[b][:, 0:384], t)
                b = bank()
                t = T(mms(PS[b], [(CQ[:, 2 + k, tok], wkv[:, k, hh * 512:hh * 512 + 512]) for k in range(2)]), rel[b])
                kv = PS[b].rearrange("p (h d) -> p h d", d=128)
                ka = KA[:, i, :].rearrange("p (h d) -> p h d", d=96)
                va = VA[:, i, :].rearrange("p (h d) -> p h d", d=64)
                t1 = V(lambda e: e.tensor_copy(ka[:, :, 0:64], kv[:, :, 0:64]), t)
                rel[b] = V(lambda e: e.tensor_copy(va, kv[:, :, 64:128]))
                V(lambda e: e.tensor_copy(ka[:, :, 64:96], KR[:, i, :].unsqueeze(1).to_broadcast([128, 4, 32])), t1)
            if hh == 1:
                W.give(s, T.last())
            barrier()
            for i in range(6):
                t = head_norm(QA[:, i, :], 4, 96, gains[:, 0:96], 96.0 ** -0.5, SQ, ss, V.last())
                if i < 4:
                    t = rope(QA[:, i, :], 4, 96, 64, 8, i, False, rt, t)
                t = head_norm(KA[:, i, :], 4, 96, gains[:, 96:192], 1.0, SQ, ss, t)
                if i < 4:
                    t = rope(KA[:, i, :], 4, 96, 64, 8, i, False, rt, t)
            heads_t(lambda i: QA[:, i, :], 4, 96, QT, range(6), t)
            heads_t(lambda i: KA[:, i, :], 4, 96, KT, range(6))
            barrier()
            attention(dense(4, lambda h: QT[0:96, h, :], lambda h: KT[0:96, h, :],
                            lambda h, k: VA[:, k, h * 64:h * 64 + 64], hh * 256), PB, PTB, sb)
            rel[:] = [None] * 8
            barrier()
        dump("gte2", GTE, V.last())
        top[0] = m1
        MT = alloc(8, 768)
        GR, GC = alloc(1024), alloc(1024)
        TM = alloc(2, 512)
        for l_, (g, r) in enumerate(((GR, 0), (GC, 1))):
            t3 = d3(G, g, MOD2[0, r:r + 1, 2048:3072].partition_broadcast(128), everyone())
        to_features(GTE, MT, range(4), 0, None, None)
        t = to_features(GTE, MT, range(4, 6), 512, None, None)
        T.wait(t)
        project(MT, range(6), xrow, lambda i: GR if i < 4 else GC, t3)
        dump("x3", X, V.last())
        dump("xc3", XC, V.last())
        barrier()
        if stop == "x3":
            return fin()

        top[0] = mark + 640
        GA = alloc(4, 512)
        PQ = alloc(4, 512)
        PKV = alloc(6, 256)
        m1 = top[0]
        MT = alloc(8, 512)
        UP = alloc(4, 514)
        HT = alloc(8, 768)
        YF = alloc(2, 512)
        assert top[0] <= WORDS - 4096, top[0]
        XN = alloc(6, 1024, at=mark + 640)
        assert mark + 640 + 6144 <= m1 + 4096
        adaln(1, HT, XN)
        barrier()
        s, w, tw = W.take()
        W.give(s, gemm_t(HT, x512(w), 0, 512, range(4), lambda i: PQ[:, i, :], tw))
        s, w, tw = W.take()
        W.give(s, gemm_t(HT, x512(w), 0, 256, range(6), lambda i: PKV[:, i, :], tw))
        tz = G(lambda e: e.memset(UP, 0.0))
        for c in range(3):
            s, w, tw = W.take()
            w = x512(w)
            for i in range(4):
                b = bank()
                t = gemm_f(w, i * 128, lambda k: HT[:, k, 0:512], PS[b], b, tw)
                if c == 0:
                    rel[b] = V(lambda e: e.tensor_copy(MT[:, 4 + i, :], PS[b]), t)
                elif c == 1:
                    rel[b] = V(lambda e: e.tensor_copy(UP[:, i, 1:513], PS[b]), t, tz)
                else:
                    rel[b] = V(lambda e: e.tensor_tensor(UP[:, i, 1:513], UP[:, i, 1:513], PS[b], ALU.mult), t, V.last())
            W.give(s, t)
        yf = [None, None]
        for i in range(4):
            u = i % 2
            y = YF[:, u, :]
            t = V.last()
            for j in range(3):
                cw = VF[:, r_c2 + j * 4 + i:r_c2 + j * 4 + i + 1]
                uv = UP[:, i, j:j + 512]
                if j == 0:
                    t = V(lambda e: e.tensor_scalar(y, uv, cw, None, ALU.mult), t)
                else:
                    t = V(lambda e: e.scalar_tensor_tensor(y, uv, cw, y, ALU.mult, ALU.add), t)
            V(lambda e: e.tensor_tensor(MT[:, 4 + i, :], MT[:, 4 + i, :], y, ALU.mult), t)
        s, w, tw = W.take()
        W.give(s, gemm_t(HT, x512(w), 0, 512, range(4), lambda i: GA[:, i, :], tw, func=ACT.Silu))
        s, w, tw = W.take()
        w = x512(w)
        yf = [None, None]
        for i in range(4):
            b = bank()
            u = i % 2
            t = gemm_f(w, i * 128, lambda k: HT[:, k, 0:512], PS[b], b, tw)
            rel[b] = t1 = A(lambda e: e.activation(YF[:, u, :], PS[b], ACT.Silu), t, V.last())
            yf[u] = V(lambda e: e.tensor_tensor(MT[:, 4 + i, :], MT[:, 4 + i, :], YF[:, u, :], ALU.mult), t1)
        W.give(s, t)
        barrier()
        top[0] = m1 + 4096
        SQ, ss, rt = alloc(768), alloc(16), alloc(1024)
        for i in range(6):
            t = V.last()
            if i < 4:
                t = head_norm(PQ[:, i, :], 8, 64, gains[:, 320:384], 0.125, SQ, ss, t)
                t = rope(PQ[:, i, :], 8, 64, 0, 16, i, True, rt, t)
            t = head_norm(PKV[:, i, 0:128], 2, 64, gains[:, 384:448], 1.0, SQ, ss, t)
            if i < 4:
                t = rope(PKV[:, i, 0:128], 2, 64, 0, 16, i, True, rt, t)
        QT, KT = alloc(8, 512), alloc(2, 768)
        PB, PTB = alloc(2, 768), alloc(2, 768)
        heads_t(lambda i: PQ[:, i, :], 8, 64, QT, range(4), t)
        heads_t(lambda i: PKV[:, i, 0:128], 2, 64, KT, range(6))
        barrier()
        wmp, wmn = c3[:, 384:512], c3[:, 512:640]
        units = []
        for h in range(8):
            for n in range(4):
                kt = KT[0:64, h // 4, :]
                lo, hi = max(n - 1, 0), min(n + 2, 4)
                L = (hi - lo) * 128
                at = 512 - L
                masks = ([(wmp, at)] if n else []) + ([(wmn, 384)] if n < 3 else [])
                v = lambda k: PKV[:, k, 128 + 64 * (h // 4):192 + 64 * (h // 4)]
                o = GA[:, n, h * 64:h * 64 + 64]
                units.append((QT[0:64, h, n * 128:n * 128 + 128], [(kt[:, lo * 128:hi * 128], at), (kt[:, 512:768], 512)],
                              at, L + 256, [v(k) for k in list(range(lo, hi)) + [4, 5]], masks,
                              sinkr[:, 8 + h:9 + h], o, o))
        attention(units, PB, PTB, sb)
        rel[:] = [None] * 8
        barrier()
        for k in range(4):
            b = bank()
            t = T(transposes([(PS[b][:, i * 128:i * 128 + 128], GA[:, i, k * 128:k * 128 + 128]) for i in range(4)]), rel[b])
            rel[b] = evac(MT[:, k, :], PS[b], t)
        top[0] = m1 + 4096
        GR = alloc(1024)
        TM = alloc(2, 512)
        t3 = d3(G, GR, MOD2[1, 0:1, 2048:3072].partition_broadcast(128), everyone())
        T.wait(V.last(), A.last())
        t = project(MT, range(4), xrow, lambda i: GR, t3)
        do = dsem("out")
        t = do(S, out[0].rearrange("(t p) d -> p t d", p=128), X, t)
        S.wait(t)


_INS = ['x', 'c', 'w_ada', 'b_ada', 'norm1_w', 'w_in', 'conv_w', 'a_log', 'dt_bias', 'dn_norm_w', 'q_norm_w',
        'k_norm_w', 'sinks', 'w_out', 'norm2_w', 'w_router', 'b_router', 'w_up', 'b_up', 'w_down', 'b_down', 'c_2',
        'ctx_2', 'c_ctx_2', 'mod_w_2', 'mod_b_2', 'ab_w_in_2', 'ab_w_out_2', 'mla_cq_gain_2', 'mla_ckv_gain_2',
        'mla_w_uq_2', 'mla_w_ukv_2', 'mla_q_gain_2', 'mla_k_gain_2', 'gqa_q_gain_2', 'gqa_k_gain_2', 'cd_w_in_2',
        'cd_w_out_2', 'win_q_gain_2', 'win_k_gain_2', 'win_sink_2', 'conv_w_2']


def build(nc, arrays, dbg_shapes=None, stop=None):
    D = {}
    for n, a in arrays.items():
        D[n] = nc.dram_tensor("in_" + n, a.shape, F32, kind="ExternalInput").ap()
    out = nc.dram_tensor("out_0", (1, 512, 1024), F32, kind="ExternalOutput").ap()
    dbg = None
    if dbg_shapes:
        dbg = {n: nc.dram_tensor("dbg_" + n, s, dt, kind="ExternalOutput").ap() for n, (s, dt) in dbg_shapes.items()}
    program(nc, D, out, dbg, stop)


def kernel(**inputs):
    import concourse.bacc as _bacc
    from concourse.bass_utils import run_bass_kernel_spmd as _run

    nc = _bacc.Bacc("TRN2", target_bir_lowering=False, num_devices=1)
    arrays = {n: np.ascontiguousarray(inputs[n]) for n in _INS}
    arrays.update(constants())
    build(nc, arrays)
    r = _run(nc, [{"in_" + n: a for n, a in arrays.items()}], core_ids=[0])
    return r.results[0]["out_0"]
```

```python
import numpy as np
import concourse.bass as bass
from concourse import mybir
from concourse.alu_op_type import AluOpType as ALU
from contextlib import ExitStack

F32 = mybir.dt.float32
I32 = mybir.dt.int32
U32 = mybir.dt.uint32
BF16 = mybir.dt.bfloat16
ACT = mybir.ActivationFunctionType
AX = mybir.AxisListType
EPS = 1e-6
NEG = -1e30
NSLOT = 5
NEXP = 32
NXB = 15
NBLK = NEXP + NXB
NBU = 3


class Engine:

    def __init__(self, eng, sem):
        self.eng, self.sem, self.n, self.on = eng, sem, 0, True
        self.seen = {}

    def wait(self, *deps):
        for d in deps:
            if d is None:
                continue
            if isinstance(d, list):
                self.wait(*d)
                continue
            sem, v = d
            if self.on and self.seen.get(id(sem), 0) < v:
                self.eng.wait_ge(sem, v)
                self.seen[id(sem)] = v

    def __call__(self, f, *deps):
        self.wait(*deps)
        if self.on:
            f(self.eng).then_inc(self.sem, 1)
        self.n += 1
        return (self.sem, self.n)

    def last(self):
        return (self.sem, self.n)


class DmaSem:

    def __init__(self, sem):
        self.sem, self.n = sem, 0

    def __call__(self, E, out, in_, *deps, f=None):
        E.wait(*deps)
        if E.on:
            i = E.eng.dma_start(out, in_) if f is None else f(E.eng)
            i.then_inc(self.sem, 16)
        self.n += 16
        return (self.sem, self.n)


def constants():
    p = np.arange(128)[:, None]
    j = np.arange(128)[None, :]
    same = (p // 64) == (j // 64)
    eye = np.eye(128)
    c0 = np.concatenate([eye, np.ones((128, 128))], 1)
    m1 = same & (p <= j)
    m2 = same & (p > j)
    cols = [m2, m1, same]
    for b in (1, 2, 4, 8, 16, 32):
        cols.append((p // (2 * b) == j // (2 * b)) & ((p // b) % 2 == 0) & ((j // b) % 2 == 1))
    cols.append((p // 2 == j // 2) & (p % 2 == 1) & (j % 2 == 0))
    c1 = np.concatenate(cols, 1)
    k2 = np.arange(256)[None, :]
    rel = (p + 128 - k2).astype(np.float32)
    slopes = 2.0 ** (-8.0 * np.arange(1, 9, dtype=np.float32) / 8)
    ok = (rel >= 0) & (rel < 128)
    swa = np.concatenate([np.where(ok, -s * rel, NEG) for s in slopes], 1)
    c2 = np.concatenate([
        p < j,
        np.broadcast_to(j, (128, 128)),
        np.broadcast_to(128.0 * np.arange(32), (128, 32)),
        np.broadcast_to(np.repeat(np.arange(NXB), 32), (128, NXB * 32)),
        p + 128 * np.arange(4)[None, :]], 1)
    t = np.arange(512)
    pos = np.stack([(t // 64), (t % 64)], 1).astype(np.float32)

    def rope(half):
        inv = (np.float32(10000.0) ** (-np.arange(half, dtype=np.float32) / np.float32(half))).astype(np.float32)
        ang = (pos[:, :, None] * inv).astype(np.float32)
        out = []
        for f in (np.cos, np.sin):
            out.append(f(ang).reshape(4, 128, 2 * half).transpose(1, 0, 2).reshape(128, 8 * half))
        return out

    wm = [np.where(j >= p, 0.0, NEG), np.where(j <= p, 0.0, NEG)]
    c3 = np.concatenate(rope(16) + rope(8) + wm, 1)
    return {n: np.ascontiguousarray(a, np.float32) for n, a in
            dict(cst0=c0, cst1=c1, cst1b=swa, cst2=c2, cst3=c3).items()}


def program(nc, D, out, dbg=None, stop=None):
    ctx = ExitStack()
    with ctx:
        def sem(name):
            return ctx.enter_context(nc.semaphore(name))

        def dram(name, shape, dt=F32):
            return nc.dram_tensor(name, shape, dt, kind="Internal").ap()

        engs = [nc.tensor, nc.vector, nc.scalar, nc.gpsimd, nc.sync]
        names = ["pe", "dve", "act", "pool", "sp"]
        T, V, A, G, S = [Engine(e, sem("s_" + n)) for e, n in zip(engs, names)]
        EN = [T, V, A, G, S]

        def dsem(name):
            return DmaSem(sem("d_" + name))

        def everyone():
            return [e.last() for e in EN[:4]]

        def fin():
            S.wait(*[(q.sem, q.n) for q in W.sems], everyone())

        dead = []

        def barrier(*dmas):
            t = everyone()
            for e in EN[:4]:
                e.wait(t, *dmas)
            dead[:] = t

        ring = ctx.enter_context(nc.sbuf_tensor("ring", [128, NSLOT * 4096], F32))
        WORDS = 32400
        mem = ctx.enter_context(nc.sbuf_tensor("mem", [128, WORDS], F32))
        PP = [ctx.enter_context(nc.psum_tensor(f"ps{i}", [128, 1024], F32)) for i in range(4)]
        PS = [PP[b // 2][:, (b % 2) * 512:(b % 2) * 512 + 512] for b in range(8)]
        rel = [None] * 8
        turn = [0]

        def bank():
            turn[0] = (turn[0] + 1) % 8
            return turn[0]

        top = [0]

        def alloc(*dims, dt=F32, at=None):
            n = int(np.prod(dims))
            if at is None:
                at = top[0]
                top[0] += n
            assert at + n <= WORDS, (at, n)
            v = mem[:, at:at + n]
            if dt != F32:
                v = v.bitcast(dt)
            if len(dims) == 2:
                v = v.rearrange("p (a b) -> p a b", b=dims[1])
            if len(dims) == 3:
                v = v.rearrange("p (a b c) -> p a b c", b=dims[1], c=dims[2])
            return v

        loads = []

        class Stream:
            def __init__(self, tag, slots=NSLOT):
                self.slots = slots
                self.sems = [dsem(f"w{tag}{i}") for i in range(slots)]
                self.issued = self.taken = 0
                self.free = [None] * slots

            def issue(self):
                if self.issued >= len(loads):
                    return
                s = self.issued % self.slots
                for dst, src in loads[self.issued]:
                    self.sems[s](S, dst(ring[:, s * 4096:(s + 1) * 4096]), src, self.free[s])
                self.issued += 1

            def take(self):
                s = self.taken % self.slots
                assert self.taken < self.issued
                self.taken += 1
                return s, ring[:, s * 4096:(s + 1) * 4096], (self.sems[s].sem, self.sems[s].n)

            def give(self, s, tok):
                self.free[s] = tok
                self.issue()

        def cols(n0, n):
            return lambda v: v.rearrange("p (k n) -> p k n", n=512)[:, :, n0:n0 + n]

        def kp(w):
            return w.rearrange("(k p) n -> p k n", p=128)

        def pk(w):
            return w.rearrange("(p k) n -> p k n", k=8)

        for c in range(12):
            loads.append([(cols(0, 512), pk(D["w_ada"][0])[:, :, c * 512:c * 512 + 512])])
        wi = kp(D["w_in"][0])
        loads.append([(cols(0, 512), wi[:, :, 2056:2568])])
        loads.append([(cols(0, 8), wi[:, :, 2048:2056])]
                     + [(cols(8 + 64 * i, 64), wi[:, :, 2568 + 64 * (i // 2):2632 + 64 * (i // 2)]) for i in range(4)]
                     + [(cols(264, 128), wi[:, :, 2696:2824])])
        for c in range(4):
            loads.append([(cols(0, 512), wi[:, :, c * 512:c * 512 + 512])])
        for l in range(2):
            for c in range(6):
                loads.append([(cols(0, 512), pk(D["mod_w_2"][l])[:, :, c * 512:c * 512 + 512])])
        wo = kp(D["w_out"][0])
        for c in range(2):
            loads.append([(cols(0, 512), wo[:, :, c * 512:c * 512 + 512])])

        def up_loads(w):
            w = kp(w)
            return [[(lambda v: v.rearrange("p (k n) -> p k n", n=2048), w[:, 2 * q:2 * q + 2, :])] for q in range(4)]

        def down_loads(w):
            w = kp(w)
            return [[(lambda v: v.rearrange("p (k n) -> p k n", n=1024), w[:, 4 * q:4 * q + 4, :])] for q in range(2)]

        for e in range(NEXP):
            loads += up_loads(D["w_up"][0, e])
            if e:
                loads += down_loads(D["w_down"][0, e - 1])
        loads += down_loads(D["w_down"][0, NEXP - 1])
        n_first = len(loads)
        ab = kp(D["ab_w_in_2"][0])
        loads.append([(cols(0, 512), ab[:, :, 544:1056])])
        loads.append([(cols(0, 32), ab[:, :, 512:544]), (cols(32, 256), ab[:, :, 1056:1312])])
        loads.append([(cols(0, 512), ab[:, :, 0:512])])
        loads.append([(cols(0, 512), ab[:, :, 1312:1824])])
        loads.append([(cols(0, 512), ab[:, :, 1824:2336])])
        uq = D["mla_w_uq_2"][0].rearrange("(k p) n -> p k n", p=128)
        ukv = D["mla_w_ukv_2"][0].rearrange("(k p) n -> p k n", p=128)
        loads.append([(lambda v: v[:, 0:1536].rearrange("p (k n) -> p k n", n=768), uq),
                      (lambda v: v[:, 1536:3584].rearrange("p (k n) -> p k n", n=1024), ukv)])
        for c in range(2):
            loads.append([(cols(0, 512), kp(D["ab_w_out_2"][0])[:, :, c * 512:c * 512 + 512])])
        cd = kp(D["cd_w_in_2"][0])
        loads.append([(cols(0, 512), cd[:, :, 0:512])])
        loads.append([(cols(0, 256), cd[:, :, 512:768])])
        for c in range(5):
            loads.append([(cols(0, 512), cd[:, :, 768 + 512 * c:1280 + 512 * c])])
        for c in range(2):
            loads.append([(cols(0, 512), kp(D["cd_w_out_2"][0])[:, :, c * 512:c * 512 + 512])])
        later = loads[n_first:]
        del loads[n_first:]

        W = Stream("a")

        def dump(name, ap, *deps):
            if dbg is not None and name in dbg:
                d = dsem("dbg_" + name)
                t = d(G, dbg[name], ap, *deps)
                for e in EN:
                    e.wait(t)

        alt = [0]

        def evac(o, i, *deps):
            alt[0] ^= 1
            if alt[0]:
                return V(lambda e: e.tensor_copy(o, i), *deps)
            return A(lambda e: e.activation(o, i, ACT.Copy), *deps)

        def rsqrt(o, i, scale, *deps, eps=EPS):
            t = V(lambda e: e.tensor_scalar(o, i, scale, eps, ALU.mult, ALU.add), *deps)
            t2 = A(lambda e: e.activation(o, o, ACT.Sqrt), t)
            return V(lambda e: e.reciprocal(o, o), t2), t

        def mms(o, pairs):
            def f(e):
                for n, (l, r) in enumerate(pairs):
                    i = e.matmul(o, l, r, start=(n == 0), stop=(n == len(pairs) - 1))
                return i
            return f

        def transposes(items):
            def f(e):
                for o, i in items:
                    k = i.shape[0]
                    r = e.transpose(o, i, ident[0:k, 0:k])
                return r
            return f

        cst0 = alloc(256)
        ident, ones = cst0[:, 0:128], cst0[:, 128:256]
        VF = alloc(80)
        modF = alloc(48)
        mod2F = alloc(2, 48)
        small = alloc(64)
        rows4 = alloc(32)
        sinkr = alloc(16)
        gains = alloc(448)
        rout = alloc(4, 32)
        GT = alloc(4, 4)
        DEST = alloc(16, dt=I32)
        ROW = alloc(48, dt=I32)
        XE = alloc(16, dt=I32)
        cact = alloc(3, 8)
        ones3 = alloc(64).bitcast(BF16)
        base = top[0]
        MOD = dram("mod_rows", (6144,))
        MOD2 = dram("mod2_rows", (2, 2, 3072))
        H2D = dram("h2_rows", (512, 1024))
        BIASD = dram("bias_rows", (NEXP, 3, 3072), BF16)
        YD = dram("y_rows", (NBLK * 128, 1024))

        for _ in range(NSLOT):
            W.issue()

        dcv = dsem("cvec")
        for i, n in enumerate(["c", "c_2", "c_ctx_2"]):
            src = D[n] if n == "c_ctx_2" else D[n][0]
            tcv = dcv(A, cact[:, i, :], src.rearrange("(p j) -> p j", j=8))
        dc = dsem("const")
        dc(A, cst0, D["cst0"])
        vrows = alloc(128)
        nv = [0]

        def vrow(src, n):
            dc(A, vrows[nv[0]:nv[0] + n, :], src)
            nv[0] += n
            return nv[0] - n

        r_n1 = vrow(D["norm1_w"][0].rearrange("(a p) -> a p", p=128), 8)
        r_cw = vrow(D["conv_w"][0].rearrange("i (t p) -> (i t) p", p=128), 48)
        r_dn = vrow(D["dn_norm_w"], 1)

        def vrow2(src):
            for h in range(2):
                dc(A, vrows[nv[0]:nv[0] + 1, 64 * h:64 * h + 64], src)
            nv[0] += 1
            return nv[0] - 1

        r_qn = vrow2(D["q_norm_w"])
        r_kn = vrow2(D["k_norm_w"])
        r_c2 = vrow(D["conv_w_2"][0].rearrange("i (t p) -> (i t) p", p=128), 12)
        r_cq = vrow(D["mla_cq_gain_2"][0].rearrange("(a p) -> a p", p=128), 2)
        r_ck = vrow(D["mla_ckv_gain_2"][0].rearrange("(a p) -> a p", p=128), 2)
        dc(A, rows4[:, 0:4], D["a_log"].partition_broadcast(128))
        dc(A, rows4[:, 4:8], D["dt_bias"].partition_broadcast(128))
        dc(A, sinkr[:, 0:8], D["sinks"].partition_broadcast(128))
        dc(A, sinkr[:, 8:16], D["win_sink_2"].partition_broadcast(128))
        for n, (o, k) in dict(mla_q_gain_2=(0, 96), mla_k_gain_2=(96, 96), gqa_q_gain_2=(192, 64),
                              gqa_k_gain_2=(256, 64), win_q_gain_2=(320, 64), win_k_gain_2=(384, 64)).items():
            dc(A, gains[:, o:o + k], D[n].partition_broadcast(128))
        brow = alloc(6144)
        modrow = alloc(6144)
        dc(A, brow[0:1, :], D["b_ada"])
        tc_ = (dc.sem, dc.n)
        X = alloc(4, 1024)
        dx = dsem("x")
        tx = dx(G, X, D["x"][0].rearrange("(t p) d -> p t d", p=128))

        BI, BH = alloc(3072), alloc(3 * 1536).bitcast(BF16).rearrange("p (a n) -> p a n", n=3072)
        dbi = dsem("bias_in")
        dbi(G, BI[0:NEXP, 0:2048], D["b_up"][0])
        tbi = dbi(G, BI[0:NEXP, 2048:3072], D["b_down"][0])
        for a in range(3):
            tbi = V(lambda e: e.tensor_copy(BH[0:NEXP, a, :], BI[0:NEXP, :]), tbi)
            if a < 2:
                tbi = V(lambda e: e.tensor_tensor(BI[0:NEXP, :], BI[0:NEXP, :], BH[0:NEXP, a, :], ALU.subtract), tbi)
        dbo = dsem("bias_out")
        tbs = dbo(G, BIASD, BH[0:NEXP], tbi)

        tca = A(lambda e: e.activation(cact, cact, ACT.Silu), tcv)
        V(lambda e: e.memset(ones3, 1.0))

        def modulation(n, first, m, dst, bias, doff):
            for c in range(n):
                s, w, tw = W.take()
                w = w.rearrange("p (k n) -> p k n", n=512)
                b = bank()
                o = PS[b][0:m, :]
                t = T(mms(o, [(cact[:, first:first + m, k], w[:, k, :]) for k in range(8)]), tw, tca, rel[b])
                W.give(s, t)
                q = c * 512
                rel[b] = V(lambda e: e.tensor_tensor(dst[0:m, q:q + 512], o, bias[0:m, q:q + 512], ALU.add), t, tc_)
            return rel[b]

        tm = modulation(12, 0, 1, modrow, brow, 0)
        b = bank()
        t = T(transposes([(PS[b][:, 0:nv[0]], vrows[0:nv[0], :])]), tc_, rel[b])
        tvf = V(lambda e: e.tensor_copy(VF[:, 0:nv[0]], PS[b][:, 0:nv[0]]), t)
        rel[b] = tvf
        dm = dsem("mod")
        tmd = dm(G, MOD.rearrange("(a n) -> a n", a=1), modrow[0:1, :], tm)

        def by_feature(src, dst, n, *deps):
            d = dsem(f"bf{nc.next_id()}")
            t0 = d(G, vrows[0:n, :], src, *deps)
            b = bank()
            t = T(transposes([(PS[b][:, 0:n], vrows[0:n, :])]), t0, rel[b])
            rel[b] = V(lambda e: e.tensor_copy(dst, PS[b][:, 0:n]), t)
            return rel[b], t

        tmf, tvr = by_feature(MOD.rearrange("(a p) -> a p", p=128), modF, 48, tmd, t)
        A1 = small[:, 0:8]
        ta1 = V(lambda e: e.scalar_tensor_tensor(A1, modF[:, 8:16], 1.0, VF[:, r_n1:r_n1 + 8], ALU.add, ALU.mult), tmf, tvf)

        junk = modrow[:, 0:1024]

        def rstd_rows(x, n, st, junk, *deps):
            for i in range(n):
                t = A(lambda e: e.activation(junk, x[:, i, :], ACT.Square, accum_out=st[:, i:i + 1]), *deps, *([t] if i else []))
            t, _ = rsqrt(st[:, 0:n], st[:, 0:n], 1.0 / 1024, t)
            return t

        st = small[:, 8:16]
        t = rstd_rows(X, 4, st, brow[:, 0:1024], tx, tm)
        for i in range(4):
            t = V(lambda e: e.tensor_scalar(X[:, i, :], X[:, i, :], st[:, i:i + 1], None, ALU.mult), t)

        def to_features(src, dst, tcs, off, mul, add, *deps):
            for k in range(8):
                b = bank()
                n = len(tcs) * 128
                t = T(transposes([(PS[b][:, i * 128:i * 128 + 128], src[:, c, k * 128:k * 128 + 128])
                                  for i, c in enumerate(tcs)]), rel[b], *deps)
                o = dst[:, k, off:off + n]
                if mul is None:
                    rel[b] = evac(o, PS[b][:, 0:n], t)
                elif k % 2:
                    rel[b] = V(lambda e: e.tensor_scalar(o, PS[b][:, 0:n], mul[:, k:k + 1], add[:, k:k + 1],
                                                         ALU.mult, ALU.add), t)
                else:
                    rel[b] = A(lambda e: e.activation(o, PS[b][:, 0:n], ACT.Identity, bias=add[:, k:k + 1],
                                                      scale=mul[:, k:k + 1]), t)
            return [V.last(), A.last()]

        top[0] = X_at = base
        barrier(tmd, tbs)
        H1 = alloc(8, 512, at=WORDS - 4096)
        t = to_features(X, H1, range(4), 0, A1, modF[:, 0:8], t, ta1)
        dump("h1T", H1, t)
        barrier()
        th = t
        if stop == "h":
            return fin()

        top[0] = base
        MIX = alloc(8, 512)
        mark = top[0]
        c1 = alloc(10, 128)
        QKV = alloc(12, 512)
        ZT = alloc(4, 512)
        gsm = alloc(8, 16)
        g16, bet, eg, kd, bE, ngm = [gsm[:, i, :] for i in range(6)]
        sub = top[0]
        U = alloc(2, 515)
        swq = alloc(4, 512)
        swk = alloc(2, 512)
        swv = alloc(4, 128)
        BG = alloc(4, 8)
        swb = alloc(8, 256)
        LG_at = top[0]
        tmp = alloc(2, 512)
        rs = alloc(2, 512)
        LG = alloc(2, 4 * 256, at=LG_at)
        PT = alloc(2, 4 * 256)
        sm = alloc(2, 24)
        assert top[0] <= WORDS - 4096
        d1 = dsem("cst1")
        d1(G, c1, D["cst1"].rearrange("p (a b) -> p a b", b=128))
        tk1 = d1(G, swb, D["cst1b"].rearrange("p (a b) -> p a b", b=256))
        M2, M1, BD = c1[:, 0, :], c1[:, 1, :], c1[:, 2, :]

        def gemm_f(w, n0, tok, o, b, *deps):
            return T(mms(o, [(w[:, k, n0:n0 + 128], tok(k)) for k in range(8)]), rel[b], *deps)

        def delta_projections():
            tz = G(lambda e: e.memset(U[:, :, 0:3], 0.0))
            squared, freed = [], [tz, tz]
            for n in range(16):
                if n % 4 == 0:
                    s, w, tw = W.take()
                    w = w.rearrange("p (k n) -> p k n", n=512)
                b = bank()
                tmm = gemm_f(w, n % 4 * 128, lambda k: H1[:, k, :], PS[b], b, tw, th)
                if n % 4 == 3:
                    W.give(s, tmm)
                if n >= 12:
                    rel[b] = A(lambda e: e.activation(ZT[:, n - 12, :], PS[b], ACT.Silu), tmm)
                else:
                    u, y = n % 2, QKV[:, n, :]
                    t = rel[b] = A(lambda e: e.activation(U[:, u, 3:515], PS[b], ACT.Copy), tmm, tz, freed[u])
                    for j in range(4):
                        cw = VF[:, r_cw + j * 12 + n:r_cw + j * 12 + n + 1]
                        uv = U[:, u, j:j + 512]
                        if j == 0:
                            t = V(lambda e: e.tensor_scalar(y, uv, cw, None, ALU.mult), t)
                        else:
                            t = V(lambda e: e.scalar_tensor_tensor(y, uv, cw, y, ALU.mult, ALU.add), t)
                    freed[u] = t
                    t = A(lambda e: e.activation(y, y, ACT.Silu), t)
                    if n < 8:
                        squared.append(A(lambda e: e.activation(U[:, u, 3:515], y, ACT.Square), t))
                if 1 <= n <= 8:
                    m = n - 1
                    b, x, r = bank(), QKV[:, m, :], U[:, m % 2, 3:515]
                    t = T(mms(PS[b], [(ones, r)]), squared[m], rel[b])
                    t, rel[b] = rsqrt(r, PS[b], 1.0, t)
                    f = 128.0 ** -0.5 if m < 4 else 1.0
                    freed[m % 2] = V(lambda e: e.scalar_tensor_tensor(x, x, f, r, ALU.mult, ALU.mult), t)
                yield

        filler = delta_projections()
        sw_squared, sw_summed, sw_normed = [], [], []

        def sw_square(i, x, t):
            sw_squared.append(A(lambda e: e.activation(tmp[:, i % 2, :], x, ACT.Square), t,
                                sw_summed[i - 2] if i >= 2 else None))

        def sw_norm(i):
            x = swq[:, i, :] if i < 4 else swk[:, i - 4, :]
            g = VF[:, r_qn:r_qn + 1] if i < 4 else VF[:, r_kn:r_kn + 1]
            u = i % 2
            b = bank()
            sw_summed.append(T(mms(PS[b], [(BD, tmp[:, u, :])]), sw_squared[i], rel[b], tk1))
            t, rel[b] = rsqrt(rs[:, u, :], PS[b], 1.0 / 64, sw_summed[i], sw_normed[i - 2] if i >= 2 else None)
            sw_normed.append(V(lambda e: e.scalar_tensor_tensor(x, x, g, rs[:, u, :], ALU.mult, ALU.mult), t))

        s, w, tw = W.take()
        w = w.rearrange("p (k n) -> p k n", n=512)
        for i in range(4):
            b = bank()
            t = gemm_f(w, i * 128, lambda k: H1[:, k, :], PS[b], b, tw, th)
            rel[b] = evac(swq[:, i, :], PS[b], t)
            sw_square(i, swq[:, i, :], rel[b])
            if i:
                sw_norm(i - 1)
        W.give(s, t)
        s, w, tw = W.take()
        w = w.rearrange("p (k n) -> p k n", n=512)
        for i in range(2):
            b = bank()
            t = gemm_f(w, 8 + i * 128, lambda k: H1[:, k, :], PS[b], b, tw)
            rel[b] = evac(swk[:, i, :], PS[b], t)
            sw_square(4 + i, swk[:, i, :], rel[b])
            sw_norm(3 + i)
        for i in range(4):
            b = bank()
            t = T(mms(PS[b][:, 0:8], [(H1[:, k, i * 128:i * 128 + 128], w[:, k, 0:8]) for k in range(8)]), rel[b])
            t = T(mms(PS[b][:, 8:136], [(H1[:, k, i * 128:i * 128 + 128], w[:, k, 264:392]) for k in range(8)]))
            tbg = V(lambda e: e.tensor_copy(BG[:, i, :], PS[b][:, 0:8]), t)
            rel[b] = tsv = V(lambda e: e.tensor_copy(swv[:, i, :], PS[b][:, 8:136]))
        W.give(s, t)
        sw_norm(5)
        tn = sw_normed[5]
        gv = g16.rearrange("p (a b) -> p a b", b=4)
        bv = bet.rearrange("p (a b) -> p a b", b=4)
        nv_ = ngm.rearrange("p (a b) -> p a b", b=4)
        t = A(lambda e: e.activation(bv, BG[:, :, 4:8], ACT.Sigmoid), tbg)
        dtb = rows4[:, 4:8]
        for i in range(4):
            t1 = V(lambda e: e.tensor_tensor(gv[:, i, :], BG[:, i, 0:4], dtb, ALU.add), tbg)
        t2 = A(lambda e: e.activation(ngm, g16, ACT.Abs), t1)
        t2 = A(lambda e: e.activation(ngm, ngm, ACT.Exp, scale=-1.0), t2)
        t3 = A(lambda e: e.activation(rows4[:, 8:12], rows4[:, 0:4], ACT.Exp))
        t2 = V(lambda e: e.tensor_scalar(ngm, ngm, 1.0, None, ALU.add), t2)
        t2 = A(lambda e: e.activation(ngm, ngm, ACT.Ln), t2)
        t2 = V(lambda e: e.scalar_tensor_tensor(g16, g16, 0.0, ngm, ALU.max, ALU.add), t2)
        t2 = V(lambda e: e.tensor_scalar(g16, g16, -1.0, None, ALU.mult), t2)
        for i in range(4):
            tg = V(lambda e: e.tensor_tensor(gv[:, i, :], gv[:, i, :], rows4[:, 8:12], ALU.mult), t2, t3)
        b = bank()
        t = T(mms(PS[b][:, 0:16], [(M1, g16)]), tg, rel[b], tk1)
        t = T(mms(PS[b][:, 16:32], [(M2, g16)]))
        A(lambda e: e.activation(eg, PS[b][:, 0:16], ACT.Exp), t)
        rel[b] = t = A(lambda e: e.activation(kd, PS[b][:, 16:32], ACT.Exp), t)
        tgs = V(lambda e: e.tensor_tensor(bE, bet, eg, ALU.mult), t)
        for u in range(2):
            t0 = G(lambda e: e.memset(LG[:, u, 0:128], NEG), tn)
        lgf, ptf, smf = [None] * 2, [None] * 2, [None] * 2
        for h in range(8):
            u, p0, kv = h % 2, 64 * (h % 2), h // 4
            lg = LG[:, u, :].rearrange("p (a b) -> p a b", b=256)
            pt = PT[:, u, :].rearrange("p (a b) -> p a b", b=256)
            m = sm[:, u, :]
            sk = sinkr[:, h:h + 1]
            for n in range(4):
                lo = max(n - 1, 0) * 128
                N = (n + 1) * 128 - lo
                b = bank()
                q = swq[p0:p0 + 64, h // 2, n * 128:n * 128 + 128]
                k = swk[p0:p0 + 64, kv, lo:lo + N]
                t = T(mms(PS[b][:, 0:N], [(q, k)]), tn, rel[b])
                t = rel[b] = V(lambda e: e.scalar_tensor_tensor(lg[:, n, 256 - N:256], PS[b][:, 0:N], 0.125,
                                                                swb[:, h, 256 - N:256], ALU.mult, ALU.add),
                               t, lgf[u], t0, tk1)
            t = V(lambda e: e.tensor_reduce(m[:, 0:4], lg, AX.X, ALU.max), t, smf[u])
            t = V(lambda e: e.tensor_scalar(m[:, 0:4], m[:, 0:4], sk, -1.0, ALU.max, ALU.mult), t)
            for n in range(4):
                kl = slice(0 if n else 128, 256)
                tp = A(lambda e: e.activation(lg[:, n, kl], lg[:, n, kl], ACT.Exp, bias=m[:, n:n + 1],
                                              accum_out=m[:, 4 + n:5 + n]), t, smf[u])
            t = A(lambda e: e.activation(m[:, 8:12], m[:, 0:4], ACT.Exp, bias=sk), t)
            t = V(lambda e: e.tensor_tensor(m[:, 12:16], m[:, 4:8], m[:, 8:12], ALU.add), t, tp)
            tr = V(lambda e: e.reciprocal(m[:, 16:20], m[:, 12:16]), t)
            for n in range(4):
                kl = slice(0 if n else 128, 256)
                smf[u] = tr = V(lambda e: e.tensor_scalar(lg[:, n, kl], lg[:, n, kl], m[:, 16 + n:17 + n], None, ALU.mult), tr)
            next(filler, None)
            for n in range(4):
                b = bank()
                ks = [0, 1] if n else [1]
                lgf[u] = t = T(transposes([(PS[b][:, k * 128:k * 128 + 128], lg[:, n, k * 128:k * 128 + 128]) for k in ks]),
                               tr, rel[b])
                if n:
                    A(lambda e: e.activation(pt[:, n - 1, 128:256], PS[b][:, 0:128], ACT.Copy), t, ptf[u])
                rel[b] = tpt = A(lambda e: e.activation(pt[:, n, 0:128], PS[b][:, 128:256], ACT.Copy), t, ptf[u])
            next(filler, None)
            b = bank()
            T.wait(tpt, rel[b], tsv)

            def values(e):
                for kt in (0, 2, 1, 3):
                    N = 256 if kt < 3 else 128
                    r = e.matmul(PS[b][p0:p0 + 64, kt * 128:kt * 128 + N], swv[:, kt, kv * 64:kv * 64 + 64], pt[:, kt, 0:N],
                                 start=(kt == 0), stop=(kt == 3))
                return r
            ptf[u] = t = T(values)
            rel[b] = V(lambda e: e.tensor_copy(MIX[p0:p0 + 64, 4 + h // 2, :], PS[b][p0:p0 + 64, :]), t)
        for _ in filler:
            pass
        dump("qkvT", QKV, everyone())
        if stop == "qkv":
            return fin()
        barrier()

        br2, mr2 = alloc(3072, at=WORDS - 4096), alloc(2, 512, at=WORDS - 1024)
        d2b = dsem("mod2b")
        d2 = [dsem(f"mod2{i}") for i in range(2)]
        added, stored = [], []

        def later_modulations(l):
            tb = d2b(G, br2[0:2, :], D["mod_b_2"][l:l + 1, :].partition_broadcast(2), added[-1] if added else None)
            for c in range(6):
                n = 6 * l + c
                s, w, tw = W.take()
                w = w.rearrange("p (k n) -> p k n", n=512)
                o = PS[2 + n % 2][0:2, :]
                T.wait(tw, added[n - 2] if n >= 2 else None)
                for k in range(8):
                    t = T(lambda e: e.matmul(o, cact[:, 1:3, k], w[:, k, :], start=(k == 0), stop=(k == 7)))
                    if (c * 8 + k) % 3 == 2:
                        yield
                W.give(s, t)
                added.append(V(lambda e: e.tensor_tensor(mr2[0:2, n % 2, :], o, br2[0:2, c * 512:c * 512 + 512], ALU.add),
                               t, tb, stored[n - 2] if n >= 2 else None))
                stored.append(d2[n % 2](G, MOD2[l][:, c * 512:c * 512 + 512], mr2[0:2, n % 2, :], added[n]))

        for hp in range(2):
            top[0] = sub
            heads = [2 * hp, 2 * hp + 1]
            units = [(a, h, i) for a, h in enumerate(heads) for i in range(4)]
            VB, KB, KD = alloc(8, 128), alloc(8, 128), alloc(8, 128)
            EE = alloc(8, 384)
            LT, AQ = alloc(8, 128), alloc(8, 128)
            XX = alloc(8, 256)
            UU, WT = EE[:, :, 0:128], EE[:, :, 128:256]
            ST = alloc(2, 128)
            ZZ = alloc(8, 128)
            GM = alloc(4, 256)
            assert top[0] + 512 <= WORDS - 4096
            if hp == 0:
                zero = alloc(512, at=WORDS - 4096 - 512)
                tz = G(lambda e: e.memset(zero, 0.0))
                dz = dsem("zero")
                for j in range(NXB):
                    tz_ = dz(S, YD[(NEXP + j) * 128:(NEXP + j + 1) * 128, :].rearrange("p (a n) -> p a n", n=512),
                             zero.unsqueeze(1).to_broadcast([128, 2, 512]), tz)
            ttok = {}
            for a, h, i in units:
                n = a * 4 + i
                c = i * 4 + h
                tok = slice(i * 128, i * 128 + 128)
                b = bank()
                t = T(transposes([(PS[b][:, 0:128], QKV[:, 8 + h, tok]), (PS[b][:, 128:256], QKV[:, 4 + h, tok])]),
                      rel[b])
                A(lambda e: e.activation(VB[:, n, :], PS[b][:, 0:128], ACT.Copy, scale=bet[:, c:c + 1]), t)
                A(lambda e: e.activation(KB[:, n, :], PS[b][:, 128:256], ACT.Copy, scale=bE[:, c:c + 1]))
                rel[b] = A(lambda e: e.activation(KD[:, n, :], PS[b][:, 128:256], ACT.Copy, scale=kd[:, c:c + 1]))
            gf = [None] * 4
            tE = {}
            for a, h, i in units:
                n = a * 4 + i
                c = i * 4 + h
                gm = GM[:, n % 4, :]
                t = V(lambda e: e.tensor_scalar(gm[:, 0:128], M2, g16[:, c:c + 1], None, ALU.mult), gf[n % 4])
                t2 = G(lambda e: e.tensor_scalar(gm[:, 128:256], ones, g16[:, c:c + 1], None, ALU.mult), gf[n % 4])
                b = bank()
                T(mms(PS[b][:, 0:128], [(M1, gm[:, 0:128])]), t, rel[b])
                T(mms(PS[b][:, 128:256], [(gm[:, 0:128], M1)]))
                t = gf[n % 4] = T(mms(PS[b][:, 256:384], [(gm[:, 128:256], M1)]), t2)
                rel[b] = t = A(lambda e: e.activation(EE[:, n, :], PS[b][:, 0:384], ACT.Exp), t)
                tE[n] = V(lambda e: e.tensor_tensor(EE[:, n, 0:256], EE[:, n, 0:256],
                                                    c1[:, 0:2, :].rearrange("p a b -> p (a b)"), ALU.mult), t)
            tX, tL = {}, {}

            def turn_l(n):
                L = ZZ[:, n, :]
                b = bank()
                t = T(transposes([(PS[b][:, 0:128], L)]), tL[n], rel[b])
                rel[b] = t = A(lambda e: e.activation(LT[:, n, :], PS[b][:, 0:128], ACT.Copy), t)
                t1 = G(lambda e: e.tensor_tensor(XX[:, n, 0:128], L, c1[:, 9, :], ALU.mult), tL[n])
                t2 = G(lambda e: e.tensor_tensor(XX[:, n, 128:256], LT[:, n, :], c1[:, 3, :], ALU.mult), t)
                t1 = G(lambda e: e.tensor_tensor(XX[:, n, 0:128], ident, XX[:, n, 0:128], ALU.subtract), t1)
                tX[n] = G(lambda e: e.tensor_tensor(XX[:, n, 128:256], ident, XX[:, n, 128:256], ALU.subtract), t2)

            for a, h, i in units:
                n = a * 4 + i
                c = i * 4 + h
                tok = slice(i * 128, i * 128 + 128)
                kT, qT = QKV[:, 4 + h, tok], QKV[:, h, tok]
                b = bank()
                T(mms(PS[b][:, 0:128], [(kT, kT)]), rel[b])
                t = T(mms(PS[b][:, 128:256], [(kT, qT)]))
                L = ZZ[:, n, :]
                tL[n] = V(lambda e: e.scalar_tensor_tensor(L, PS[b][:, 0:128], bet[:, c:c + 1], EE[:, n, 0:128],
                                                        ALU.mult, ALU.mult), t, tE[n])
                rel[b] = V(lambda e: e.tensor_tensor(AQ[:, n, :], PS[b][:, 128:256], EE[:, n, 128:256], ALU.mult))
                tqd = V(lambda e: e.tensor_tensor(qT, qT, EE[:, n, 256:384], ALU.mult), t)
                if n:
                    turn_l(n - 1)
            turn_l(7)
            for lv in range(1, 6):
                mk = c1[:, 3 + lv, :]
                tb = {}
                for n in range(8):
                    gm = GM[:, n % 4, 0:128]
                    t = G(lambda e: e.tensor_tensor(gm, LT[:, n, :], mk, ALU.mult), gf[n % 4])
                    b = bank()
                    gf[n % 4] = t = T(mms(PS[b][:, 0:128], [(gm, XX[:, n, 0:128])]), t, tX[n], rel[b])
                    rel[b] = tb[n] = A(lambda e: e.activation(ZZ[:, n, :], PS[b][:, 0:128], ACT.Copy), t)
                for n in range(8):
                    b = bank()
                    T(mms(PS[b][:, 0:128], [(XX[:, n, 128:256], ZZ[:, n, :])]), tb[n], rel[b])
                    t = T(mms(PS[b][:, 128:256], [(ZZ[:, n, :], XX[:, n, 128:256])]))
                    rel[b] = tX[n] = V(lambda e: e.tensor_tensor(XX[:, n, :], XX[:, n, :], PS[b][:, 0:256],
                                                                 ALU.subtract), t)
            tU = {}
            for n in range(8):
                XT = XX[:, n, 128:256]
                b = bank()
                T(mms(PS[b][:, 0:128], [(XT, VB[:, n, :])]), tX[n], rel[b])
                t = T(mms(PS[b][:, 128:256], [(KB[:, n, :], XT)]))
                V(lambda e: e.tensor_copy(UU[:, n, :], PS[b][:, 0:128]), t)
                rel[b] = tU[n] = V(lambda e: e.tensor_copy(WT[:, n, :], PS[b][:, 128:256]))
            barrier()
            VN = alloc(2, 128, at=sub + 8 * 128 * 3 + 8 * 384)
            OB = [PS[6], PS[7]]
            filler = later_modulations(hp)
            tS, tO, tV, wt_read = [None, None], [None, None], [None, None], [None, None]
            kd_read = [[None, None], [None, None]]
            for i in range(8):
                n_, hf = i // 2, 64 * (i % 2)
                hs = slice(hf, hf + 64)
                for a, h in enumerate(heads):
                    n, vn, sb = a * 4 + n_, VN[:, a, :], ST[:, a, :]
                    if i:
                        t = T(mms(PS[a][:, 0:128], [(WT[:, n, :], sb)]), tS[a], wt_read[a])
                        tV[a] = wt_read[a] = V(lambda e: e.tensor_tensor(vn[hs, :], UU[hs, n, :], PS[a][hs, 0:128],
                                                                         ALU.subtract), t, tO[a])
                    else:
                        tV[a] = V(lambda e: e.tensor_copy(vn[hs, :], UU[hs, n, :]))
                next(filler, None)
                for a, h in enumerate(heads):
                    n, vn, sb = a * 4 + n_, VN[:, a, :], ST[:, a, :]
                    q = QKV[:, h, i * 64:i * 64 + 64]
                    ko = PS[a][:, 128 + 128 * (i % 2):256 + 128 * (i % 2)]
                    t = T(mms(ko, [(KD[hs, n, :], vn[hs, :])]), tV[a], kd_read[a][i % 2])
                    pairs = ([(sb, q)] if i else []) + [(vn[hs, :], AQ[hs, n, hs])]
                    tO[a] = T(mms(OB[a][:, i * 64:i * 64 + 64], pairs))
                    if i:
                        dcol = EE[:, n, 256 + hf + 63:256 + hf + 64]
                        t = V(lambda e: e.scalar_tensor_tensor(sb, sb, dcol, ko, ALU.mult, ALU.add), t, tO[a])
                    else:
                        t = V(lambda e: e.tensor_copy(sb, ko), t)
                    kd_read[a][i % 2] = tS[a] = t
                next(filler, None)
            for _ in filler:
                pass
            rel[0:2] = tS
            rel[6], rel[7] = None, None
            tmp = alloc(2, 512, at=sub)
            rs = alloc(2, 512, at=sub + 1024)
            osb = alloc(2, 512, at=sub + 2048)
            for a, h in enumerate(heads):
                te = A(lambda e: e.activation(osb[:, a, :], OB[a], ACT.Copy), tO[a], tO[0], tO[1])
                t = A(lambda e: e.activation(tmp[:, a, :], OB[a], ACT.Square))
                rel[6 + a] = t
                b = a
                t = T(mms(PS[b], [(ones, tmp[:, a, :])]), t, rel[b])
                t, rel[b] = rsqrt(rs[:, a, :], PS[b], 1.0 / 128, t)
                t = V(lambda e: e.scalar_tensor_tensor(osb[:, a, :], osb[:, a, :], VF[:, r_dn:r_dn + 1], rs[:, a, :],
                                                       ALU.mult, ALU.mult), t, te)
                V(lambda e: e.tensor_tensor(MIX[:, h, :], osb[:, a, :], ZT[:, h, :], ALU.mult), t)
            barrier()
        dump("mixT", MIX, V.last())
        if stop == "mix":
            return fin()

        X = alloc(4, 1024, at=WORDS - 4096)
        tx = dx(G, X, D["x"][0].rearrange("(t p) d -> p t d", p=128), added, stored)

        top[0] = mark
        GR = alloc(1024)
        TM = alloc(2, 512)
        dg = dsem("gate")
        tg = dg(G, GR, MOD[2048:3072].rearrange("(a n) -> a n", a=1).partition_broadcast(128), everyone())

        def project(src, tcs, x_of, gate_of, TM, *deps):
            freed, done = [None, None], []
            for c in range(2):
                s, w, tw = W.take()
                w = w.rearrange("p (k n) -> p k n", n=512)
                for i in tcs:
                    b = bank()
                    t = T(mms(PS[b], [(src[:, k, i * 128:i * 128 + 128], w[:, k, :]) for k in range(8)]), tw, rel[b], *deps)
                    u = i % 2
                    gr = gate_of(i)[:, c * 512:c * 512 + 512]
                    xo = x_of(i)[:, c * 512:c * 512 + 512]
                    rel[b] = tt = V(lambda e: e.tensor_tensor(TM[:, u, :], PS[b], gr, ALU.mult), t, freed[u])
                    freed[u] = V(lambda e: e.tensor_tensor(xo, xo, TM[:, u, :], ALU.add), tt)
                    done.append(freed[u])
                W.give(s, t)
            return done[len(tcs):]

        vrows = alloc(2, 128)
        for l in range(2):
            db = dsem(f"bf2{l}")
            t = db(G, vrows[0:48, l, :], MOD2[l].rearrange("r (a p) -> (r a) p", p=128), stored)
            b = bank()
            t = T(transposes([(PS[b][:, 0:48], vrows[0:48, l, :])]), t, rel[b])
            rel[b] = V(lambda e: e.tensor_copy(mod2F[:, l, :], PS[b][:, 0:48]), t)
        t = project(MIX, range(4), lambda i: X[:, i, :], lambda i: GR, TM, tg, tx)
        dump("x1", X, t)
        barrier()
        if stop == "x1":
            return fin()

        top[0] = base
        A2, B2, N2 = alloc(1024), alloc(1024), alloc(1024)
        H2 = alloc(4, 1024)
        H2T = alloc(8, 512)
        c2 = alloc(128 + 128 + 32 + NXB * 32 + 4)
        wr = alloc(8, 32)
        brt = alloc(32)
        dr = dsem("rt")
        row = lambda a: a.rearrange("(a n) -> a n", a=1).partition_broadcast(128)
        ev = everyone()
        dr(G, A2, row(MOD[4096:5120]), ev)
        dr(G, B2, row(MOD[3072:4096]))
        dr(G, N2, D["norm2_w"].partition_broadcast(128))
        dr(G, c2, D["cst2"])
        dr(G, wr, kp(D["w_router"][0]))
        tr = dr(G, brt, D["b_router"].partition_broadcast(128))
        ta = V(lambda e: e.scalar_tensor_tensor(A2, A2, 1.0, N2, ALU.add, ALU.mult), tr)
        st = small[:, 8:16]
        t = rstd_rows(X, 4, st, H2[:, 0, :], None)
        dh = dsem("h2")
        for i in range(4):
            th = V(lambda e: e.scalar_tensor_tensor(H2[:, i, :], X[:, i, :], st[:, i:i + 1], A2, ALU.mult, ALU.mult), t, ta)
            th = V(lambda e: e.tensor_tensor(H2[:, i, :], H2[:, i, :], B2, ALU.add), th)
            td = dh(G, H2D[i * 128:i * 128 + 128, :], H2[:, i, :], th)
        t = to_features(H2, H2T, range(4), 0, None, None, th)
        U_, I128 = c2[:, 0:128], c2[:, 128:256]
        B0 = c2[:, 256:288]
        JJ = c2[:, 288:288 + NXB * 32].rearrange("p (a b) -> p a b", b=32)
        TID = c2[:, 288 + NXB * 32:292 + NXB * 32]
        LGT = rout
        for i in range(4):
            b = bank()
            t1 = T(mms(PS[b][:, 0:32], [(H2T[:, k, i * 128:i * 128 + 128], wr[:, k, :]) for k in range(8)]), t, tr, rel[b])
            rel[b] = tl = V(lambda e: e.tensor_tensor(LGT[:, i, :], PS[b][:, 0:32], brt, ALU.add), t1)
        dump("logits", LGT, tl)
        V8 = alloc(4, 8)
        I8 = alloc(4, 8, dt=U32)
        I8f = alloc(4, 8)
        OH = alloc(16, 32)
        MM = alloc(4, 32)
        POS = alloc(4, 32)
        CN, NX, CS, BD1 = alloc(32), alloc(32), alloc(32), alloc(32)
        SL = alloc(4, 32)
        T5 = alloc(NXB, 32)
        DF = alloc(16)
        DI = alloc(2, 16, dt=I32)
        DIF = alloc(2, 16)
        gs = alloc(16)
        for i in range(4):
            t = V(lambda e: e.max(V8[:, i, :], LGT[:, i, :]), tl)
            t = V(lambda e: e.max_index(I8[:, i, :], V8[:, i, :], LGT[:, i, :]), t)
        t = V(lambda e: e.tensor_copy(I8f, I8), t)
        for i in range(4):
            for k in range(4):
                to = V(lambda e: e.tensor_scalar(OH[:, i * 4 + k, :], I128[:, 0:32], I8f[:, i, k:k + 1], None,
                                                 ALU.is_equal), t, tr)
        O4 = OH.rearrange("p (i k) e -> p i k e", k=4)
        t = V(lambda e: e.tensor_tensor(MM, O4[:, :, 0, :], O4[:, :, 1, :], ALU.add), to)
        t = V(lambda e: e.tensor_tensor(MM, MM, O4[:, :, 2, :], ALU.add), t)
        tmk = V(lambda e: e.tensor_tensor(MM, MM, O4[:, :, 3, :], ALU.add), t)
        b = bank()
        for i in range(4):
            t = T(mms(PS[b][:, i * 32:i * 32 + 32], [(U_, MM[:, i, :])] + [(ones, MM[:, q, :]) for q in range(i)]), tmk, rel[b])
        t = T(mms(PS[b][:, 128:160], [(ones, MM[:, q, :]) for q in range(4)]))
        V(lambda e: e.tensor_copy(POS, PS[b][:, 0:128].rearrange("p (a b) -> p a b", b=32)), t)
        rel[b] = t = V(lambda e: e.tensor_copy(CN, PS[b][:, 128:160]))
        t = V(lambda e: e.tensor_scalar(NX, CN, 128.0, None, ALU.is_gt), t)
        t = V(lambda e: e.scalar_tensor_tensor(NX, CN, 256.0, NX, ALU.is_gt, ALU.add), t)
        t = V(lambda e: e.scalar_tensor_tensor(NX, CN, 384.0, NX, ALU.is_gt, ALU.add), t)
        t = V(lambda e: e.tensor_tensor_scan(CS, ones[:, 0:32], NX, 0.0, ALU.mult, ALU.add), t)
        t1 = V(lambda e: e.tensor_tensor(BD1, CS, NX, ALU.subtract), t)
        t1 = V(lambda e: e.tensor_scalar(BD1, BD1, 128.0, 128.0 * (NEXP - 1), ALU.mult, ALU.add), t1)
        t1 = V(lambda e: e.tensor_tensor(BD1, BD1, B0, ALU.subtract), t1)
        bc = lambda v, n: v.unsqueeze(1).to_broadcast([128, n, 32])
        t5 = V(lambda e: e.tensor_tensor(T5, bc(CS, NXB), JJ, ALU.is_le), t)
        t5 = V(lambda e: e.tensor_reduce(gs[:, 0:NXB], T5, AX.X, ALU.add), t5)
        t5 = V(lambda e: e.tensor_scalar(gs[:, 0:NXB], gs[:, 0:NXB], float(NEXP - 1), None, ALU.min), t5)
        V(lambda e: e.tensor_copy(XE[:, 0:NXB], gs[:, 0:NXB]), t5)
        txe = V(lambda e: e.tensor_copy(XE[:, NXB:NXB + 1], CS[:, 31:32]))
        t = V(lambda e: e.tensor_scalar(SL, POS, 128.0, None, ALU.is_ge), t1)
        t = V(lambda e: e.tensor_tensor(SL, SL, bc(BD1, 4), ALU.mult), t)
        t = V(lambda e: e.tensor_tensor(SL, SL, POS, ALU.add), t)
        ts = V(lambda e: e.tensor_tensor(SL, SL, bc(B0, 4), ALU.add), t)
        for i in range(4):
            t = V(lambda e: e.tensor_tensor(O4[:, i, :, :], O4[:, i, :, :], bc(SL[:, i, :], 4), ALU.mult), ts)
        t = V(lambda e: e.tensor_reduce(DF, OH, AX.X, ALU.add), t)
        td1 = V(lambda e: e.tensor_copy(DEST, DF), t)
        V(lambda e: e.tensor_scalar(DI[:, 0, :], DEST, 7, None, ALU.logical_shift_right), td1)
        t = V(lambda e: e.tensor_scalar(DI[:, 1, :], DEST, 127, None, ALU.bitwise_and))
        tdf = V(lambda e: e.tensor_copy(DIF, DI), t)
        OP = alloc(2, 128)
        OBK = alloc(2, 48)
        opf = [None, None]
        b = bank()
        rb = rel[b]
        for n in range(16):
            u = n % 2
            V(lambda e: e.tensor_scalar(OP[:, u, :], I128, DIF[:, 1, n:n + 1], None, ALU.is_equal), tdf, opf[u])
            t = V(lambda e: e.tensor_scalar(OBK[:, u, 0:NBLK], I128[:, 0:NBLK], DIF[:, 0, n:n + 1],
                                            TID[:, n // 4:n // 4 + 1], ALU.is_equal, ALU.mult))
            T.wait(t, rb)
            opf[u] = T(lambda e: e.matmul(PS[b][:, 0:NBLK], OP[:, u, :], OBK[:, u, 0:NBLK], start=(n == 0), stop=(n == 15)))
        rel[b] = trow = V(lambda e: e.tensor_copy(ROW[:, 0:NBLK], PS[b][:, 0:NBLK]), opf[1])
        gf_ = gs
        for i in range(4):
            t = V(lambda e: e.tensor_scalar(gs[:, i:i + 1], V8[:, i, 0:1], -1.0, None, ALU.mult), V.last())
            t = A(lambda e: e.activation(GT[:, i, :], V8[:, i, 0:4], ACT.Exp, bias=gs[:, i:i + 1], accum_out=gs[:, 4 + i:5 + i]), t)
            t = V(lambda e: e.reciprocal(gs[:, 8 + i:9 + i], gs[:, 4 + i:5 + i]), t)
            tgt = V(lambda e: e.tensor_scalar(GT[:, i, :], GT[:, i, :], gs[:, 8 + i:9 + i], None, ALU.mult), t)
        dump("gt", GT, tgt)
        dump("dest", DEST, tgt)
        dump("row", ROW[:, 0:NBLK], tgt)
        dump("xe", XE, tgt)
        barrier(td, tz_)
        if stop == "route":
            return fin()

        top[0] = base
        XG, XGT = alloc(2, 1024), alloc(2, 1024)
        T1, SG, T2 = alloc(1024), alloc(1024), alloc(1024)
        ACTV, ACTT = alloc(1024), alloc(1024)
        Y = alloc(2, 1024)
        BU = alloc(NBU * 1536).bitcast(BF16).rearrange("p (a n) -> p a n", n=3072)
        assert top[0] <= WORDS - 4096

        def expert_steps(w, gather_sem, bias_sem, store_sem):
            gathered, biased, x_turned, x_copied, up_done, glu_read, lin_read = [], [], [], [], [], [], []
            act_done, a_turned, a_copied, down_done, y_copied, stored = [], [], [], [], [], []

            def before(steps, i):
                return steps[i] if i >= 0 else None

            def gather(i, col):
                gathered.append(gather_sem[i % 2](G, None, None, before(x_turned, 2 * (i - 2) + 1), f=lambda e: e.indirect_dma_start(
                    XG[:, i % 2, :], None, H2D, bass.IndirectOffsetOnAxis(ap=ROW[:, col:col + 1], axis=0))))

            def biases(i, rows):
                biased.append(bias_sem[i % NBU](G, BU[0:3, i % NBU, :], rows, before(down_done, i - NBU)))

            def turn_x(i, hh):
                u, n = i % 2, 2 * i + hh
                x_turned.append(T(transposes([(PS[4][:, q * 128:q * 128 + 128], XG[:, u, (hh * 4 + q) * 128:(hh * 4 + q + 1) * 128])
                                              for q in range(4)]), gathered[i], before(x_copied, n - 1)))
                x_copied.append(V(lambda e: e.tensor_copy(XGT[:, u, hh * 512:hh * 512 + 512], PS[4]), x_turned[n],
                                  before(up_done, i - 2)))

            def up(i, between):
                u = i % 2
                T.wait(biased[i], before(glu_read, i - 1), before(lin_read, i - 1))

                def bias_rows(e):
                    for n in range(4):
                        r = e.matmul(PS[n], ones3[0:3, :], BU[0:3, i % NBU, n * 512:n * 512 + 512], start=True, stop=False)
                    return r
                T(bias_rows)
                for q in range(4):
                    s, wt, loaded = w.take()
                    wt = wt.rearrange("p (k n) -> p k n", n=2048)

                    def products(e):
                        for kk in range(2):
                            k = 2 * q + kk
                            for n in range(4):
                                r = e.matmul(PS[n], XGT[:, u, k * 128:k * 128 + 128], wt[:, kk, n * 512:n * 512 + 512],
                                             start=False, stop=(k == 7))
                        return r
                    t = T(products, loaded, x_copied[2 * i + q // 2])
                    w.give(s, t)
                    between(q)
                up_done.append(t)
                for n in range(2):
                    c = slice(n * 512, n * 512 + 512)
                    ta = V(lambda e: e.tensor_scalar(T1[:, c], PS[n], 7.0, None, ALU.min), up_done[i], before(act_done, i - 1))
                    sg = A(lambda e: e.activation(SG[:, c], T1[:, c], ACT.Sigmoid, scale=1.702), ta, before(act_done, i - 1))
                glu_read.append(ta)
                for n in range(2):
                    c = slice(n * 512, n * 512 + 512)
                    tb = V(lambda e: e.tensor_scalar(T2[:, c], PS[2 + n], 7.0, -7.0, ALU.min, ALU.max), up_done[i])
                lin_read.append(tb)
                tb = V(lambda e: e.scalar_tensor_tensor(T2, T2, 1.0, T1, ALU.add, ALU.mult), tb, ta)
                act_done.append(V(lambda e: e.tensor_tensor(ACTV, T2, SG, ALU.mult), tb, sg, before(a_turned, 2 * (i - 1) + 1)))

            def turn_a(i, hh):
                n = 2 * i + hh
                a_turned.append(T(transposes([(PS[5][:, q * 128:q * 128 + 128], ACTV[:, (hh * 4 + q) * 128:(hh * 4 + q + 1) * 128])
                                              for q in range(4)]), act_done[i], before(a_copied, n - 1)))
                a_copied.append(V(lambda e: e.tensor_copy(ACTT[:, hh * 512:hh * 512 + 512], PS[5]), a_turned[n],
                                  before(down_done, i - 1)))

            def down(i, col):
                u = i % 2
                T.wait(before(y_copied, i - 1))

                def bias_rows(e):
                    for n in range(2):
                        r = e.matmul(PS[6 + n], ones3[0:3, :], BU[0:3, i % NBU, 2048 + n * 512:2560 + n * 512], start=True, stop=False)
                    return r
                T(bias_rows)
                for q in range(2):
                    s, wt, loaded = w.take()
                    wt = wt.rearrange("p (k n) -> p k n", n=1024)

                    def products(e):
                        for kk in range(4):
                            k = 4 * q + kk
                            for n in range(2):
                                r = e.matmul(PS[6 + n], ACTT[:, k * 128:k * 128 + 128], wt[:, kk, n * 512:n * 512 + 512],
                                             start=False, stop=(k == 7))
                        return r
                    t = T(products, loaded, a_copied[2 * i + q])
                    w.give(s, t)
                down_done.append(t)
                for n in range(2):
                    ty = A(lambda e: e.activation(Y[:, u, n * 512:n * 512 + 512], PS[6 + n], ACT.Copy), t, before(stored, i - 2))
                y_copied.append(ty)
                stored.append(store_sem[u](G, YD[col * 128:col * 128 + 128, :], Y[:, u, :], ty))
                return stored[i]

            return gather, biases, turn_x, up, turn_a, down

        def expert_sems(tag):
            return [[dsem(f"{n}{tag}{i}") for i in range(c)] for n, c in (("gather", 2), ("bias", NBU), ("store", 2))]

        gather, biases, turn_x, up, turn_a, down = expert_steps(W, *expert_sems("a"))
        for i in range(NBU):
            biases(i, BIASD[i])
        for i in range(2):
            gather(i, i)
        turn_x(0, 0)
        turn_x(0, 1)
        stored = [None, None]
        for i in range(NEXP):
            def between(q):
                if q < 2 and i:
                    turn_a(i - 1, q)
                if q >= 2 and i + 1 < NEXP:
                    turn_x(i + 1, q - 2)
            up(i, between)
            if i + 2 < NEXP:
                gather(i + 2, i + 2)
            if i:
                stored[(i - 1) % 2] = down(i - 1, i - 1)
                if i - 1 + NBU < NEXP:
                    biases(i - 1 + NBU, BIASD[i - 1 + NBU])
        turn_a(NEXP - 1, 0)
        turn_a(NEXP - 1, 1)
        stored[1] = down(NEXP - 1, NEXP - 1)
        barrier(stored)

        main = [(e.sem, e.n, dict(e.seen)) for e in EN]
        S.wait(txe)
        slots = list(W.free)
        xsem = [sem("x_" + n) for n in names]
        loads[:] = []
        proto = Stream("x")
        extra_sems = expert_sems("x")
        counted = [proto.sems] + extra_sems

        def extras(E):
            for e, q in zip(EN, xsem):
                e.sem, e.n, e.on, e.seen = q, 0, e is E, {}
            loads[:] = []
            for grp in counted:
                for q in grp:
                    q.n = 0
            proto.issued = proto.taken = 0
            proto.free = list(slots)
            gather, biases, turn_x, up, turn_a, down = expert_steps(proto, *extra_sems)
            eng, ends = E.eng, []
            cnt = eng.value_load(XE[0:1, NXB:NXB + 1], min_val=0, max_val=NXB)
            for j in range(NXB):
                with eng.If(cnt > j):
                    if E is S or E is G:
                        ex = eng.value_load(XE[0:1, j:j + 1], min_val=0, max_val=NEXP - 1)
                        w1 = D["w_up"][0, bass.ds(ex, 1)].rearrange("a k n -> (a k) n")
                        w2 = D["w_down"][0, bass.ds(ex, 1)].rearrange("a k n -> (a k) n")
                        b3 = BIASD[bass.ds(ex, 1)].rearrange("a k n -> (a k) n")
                    else:
                        w1, w2, b3 = D["w_up"][0, 0], D["w_down"][0, 0], BIASD[0]
                    loads.extend(up_loads(w1) + down_loads(w2))
                    gather(j, NEXP + j)
                    biases(j, b3)
                    while proto.issued < proto.taken + NSLOT and proto.issued < len(loads):
                        proto.issue()
                    turn_x(j, 0)
                    turn_x(j, 1)
                    up(j, lambda q: None)
                    turn_a(j, 0)
                    turn_a(j, 1)
                    ends.append(([(q, e.n) for e, q in zip(EN[:4], xsem)], down(j, NEXP + j)))
            for j in range(NXB):
                with eng.If(cnt == j + 1):
                    E.wait(*ends[j])

        with nc.Block() as block:
            @block.tensor
            def _(e):
                extras(T)

            @block.vector
            def _(e):
                extras(V)

            @block.scalar
            def _(e):
                extras(A)

            @block.gpsimd
            def _(e):
                extras(G)

            @block.sync
            def _(e):
                extras(S)
        for e, (q, n, seen) in zip(EN, main):
            e.sem, e.n, e.seen, e.on = q, n, seen, True
        rel[:] = [None] * 8
        loads[:] = later
        W = Stream("b", 3)
        for _ in range(3):
            W.issue()

        top[0] = base
        XC = alloc(2, 1024)
        mark = top[0]
        c3 = alloc(640)
        GTE = alloc(8, 768)
        CQ = alloc(4, 768)
        KR = alloc(6, 32)
        GKV = alloc(6, 256)
        GQ = alloc(6, 512)
        HT = alloc(8, 768)
        tail = top[0]
        YG = mem[:, mark + 640:mark + 640 + 4096].rearrange("p (a n) -> p a n", n=1024)
        ACC = mem[:, mark + 640 + 4096:mark + 640 + 6144].rearrange("p (a n) -> p a n", n=1024)
        GR = alloc(1024)
        XN = alloc(2, 1024)
        rt = alloc(1024)
        assert top[0] <= WORDS - 4096
        sb = small[:, 32:48]
        spare = ring[:, 3 * 4096:5 * 4096]
        d3 = dsem("late")
        dgr = dsem("gate2")
        txc = d3(A, XC, D["ctx_2"][0].rearrange("(t p) d -> p t d", p=128))
        tgr = dgr(A, GR, MOD[5120:6144].rearrange("(a n) -> a n", a=1).partition_broadcast(128))
        dc3 = dsem("cst3")
        tc3 = dc3(A, c3, D["cst3"])
        dyg = [dsem(f"yg{k}") for k in range(4)]
        yg_read, acc_read = [None] * 4, [None] * 2

        def combine(i):
            acc = ACC[:, i % 2, :]
            for k in range(4):
                n = i * 4 + k
                ty = dyg[k](G, None, None, yg_read[k], f=lambda e: e.indirect_dma_start(
                    YG[:, k, :], None, YD, bass.IndirectOffsetOnAxis(ap=DEST[:, n:n + 1], axis=0)))
                if k == 0:
                    t = V(lambda e: e.tensor_scalar(acc, YG[:, k, :], GT[:, i, 0:1], None, ALU.mult), ty, acc_read[i % 2])
                else:
                    t = V(lambda e: e.scalar_tensor_tensor(acc, YG[:, k, :], GT[:, i, k:k + 1], acc, ALU.mult, ALU.add), ty, t)
                yg_read[k] = t
            t = V(lambda e: e.tensor_tensor(acc, acc, GR, ALU.mult), t, tgr)
            acc_read[i % 2] = V(lambda e: e.tensor_tensor(X[:, i, :], X[:, i, :], acc, ALU.add), t)
            return acc_read[i % 2]

        xrow = lambda i: X[:, i, :] if i < 4 else XC[:, i - 4, :]
        xn_read = [None, None]

        def adaln(l, i, n, HT, tx):
            st = small[:, 8 + i:9 + i]
            xn = XN[:, n % 2, :]
            t = A(lambda e: e.activation(xn, xrow(i), ACT.Square, accum_out=st), tx, xn_read[n % 2])
            t, _ = rsqrt(st, st, 1.0 / 1024, t)
            t = V(lambda e: e.tensor_scalar(xn, xrow(i), st, None, ALU.mult), t)
            r = 0 if i < 4 else 1
            mul, add = mp[:, r * 8:r * 8 + 8], mod2F[:, l, r * 24:r * 24 + 8]
            done = []
            for g in range(2):
                b = bank()
                xn_read[n % 2] = t1 = T(transposes([(PS[b][:, q * 128:q * 128 + 128], xn[:, (4 * g + q) * 128:(4 * g + q + 1) * 128])
                                                    for q in range(4)]), t, rel[b])
                rel[b] = []
                for q in range(4):
                    k = 4 * g + q
                    o, p = HT[:, k, i * 128:i * 128 + 128], PS[b][:, q * 128:q * 128 + 128]
                    if g:
                        t1_ = V(lambda e: e.tensor_scalar(o, p, mul[:, k:k + 1], add[:, k:k + 1], ALU.mult, ALU.add), t1, tmp_)
                    else:
                        t1_ = A(lambda e: e.activation(o, p, ACT.Identity, bias=add[:, k:k + 1], scale=mul[:, k:k + 1]), t1, tmp_)
                    rel[b].append(t1_)
                done += rel[b]
            return done

        def scales(l):
            m2 = mod2F[:, l, :].rearrange("p (r a) -> p r a", a=24)
            return V(lambda e: e.tensor_scalar(mp.rearrange("p (r a) -> p r a", a=8), m2[:, :, 8:16], 1.0, None, ALU.add))

        mp = small[:, 16:32]
        tmp_ = scales(0)
        def gemm_t(HT, w, n0, n, i, dst, *deps, func=ACT.Copy):
            b = bank()
            t = T(mms(PS[b][:, 0:n], [(HT[:, k, i * 128:i * 128 + 128], w[:, k, n0:n0 + n]) for k in range(8)]),
                  rel[b], *deps)
            rel[b] = A(lambda e: e.activation(dst, PS[b][:, 0:n], func), t)
            return rel[b], t
        def run(steps):
            while True:
                try:
                    next(steps)
                except StopIteration as end:
                    return end.value

        def head_norm(x, H, d, gain, scale, sq, st, *deps):
            x3 = x.rearrange("p (h d) -> p h d", d=d)
            s3 = sq[:, 0:H * d].rearrange("p (h d) -> p h d", d=d)
            t = V(lambda e: e.tensor_tensor(s3, x3, x3, ALU.mult), *deps)
            t = V(lambda e: e.tensor_reduce(st[:, 0:H], s3, AX.X, ALU.add), t)
            t = V(lambda e: e.tensor_scalar(st[:, 0:H], st[:, 0:H], 1.0 / d, EPS, ALU.mult, ALU.add), t)
            t = A(lambda e: e.activation(st[:, 0:H], st[:, 0:H], ACT.Sqrt), t)
            yield
            t = V(lambda e: e.reciprocal(st[:, 0:H], st[:, 0:H]), t)
            t = V(lambda e: e.tensor_tensor(x3, x3, st[:, 0:H].unsqueeze(2).to_broadcast([128, H, d]), ALU.mult), t)
            yield
            return V(lambda e: e.scalar_tensor_tensor(x3, x3, scale, gain.unsqueeze(1).to_broadcast([128, H, d]),
                                                      ALU.mult, ALU.mult), t)

        def rope(x, H, d, off, r, i, big, tmp, *deps):
            o, n = (0, 2 * r) if big else (256, 2 * r)
            x3 = x.rearrange("p (h d) -> p h d", d=d)[:, :, off:off + 4 * r].rearrange("p h (a m) -> p h a m", m=n)
            x1, x2 = x3[:, :, :, 0:r], x3[:, :, :, r:n]
            bc = lambda c: c.rearrange("p (a r) -> p a r", r=r).unsqueeze(1).to_broadcast([128, H, 2, r])
            cs, sn = bc(c3[:, o + i * n:o + i * n + n]), bc(c3[:, o + 4 * n + i * n:o + 4 * n + i * n + n])
            m = 2 * H * r
            ta, tb, tc, td = [tmp[:, q * m:(q + 1) * m].rearrange("p (h a r) -> p h a r", a=2, r=r) for q in range(4)]
            V(lambda e: e.tensor_tensor(ta, x1, cs, ALU.mult), *deps)
            V(lambda e: e.tensor_tensor(tb, x2, sn, ALU.mult))
            yield
            V(lambda e: e.tensor_tensor(tc, x2, cs, ALU.mult))
            t = V(lambda e: e.tensor_tensor(td, x1, sn, ALU.mult))
            yield
            V(lambda e: e.tensor_tensor(x1, ta, tb, ALU.subtract), t)
            return V(lambda e: e.tensor_tensor(x2, tc, td, ALU.add), t)

        def pairs_t(src, H, dst, tcs, *deps):
            for h in range(H // 2):
                for g in range(0, len(tcs), 4):
                    part = list(tcs)[g:g + 4]
                    b = bank()
                    t = T(transposes([(PS[b][:, q * 128:q * 128 + 128], src(i)[:, h * 128:h * 128 + 128])
                                      for q, i in enumerate(part)]), rel[b], *deps)
                    lo, n = part[0] * 128, len(part) * 128
                    rel[b] = A(lambda e: e.activation(dst[:, h, lo:lo + n], PS[b][:, 0:n], ACT.Copy), t, *deps)

        def twice_t(src, H, dst, tcs, *deps):
            for h in range(H):
                for g in range(0, len(tcs), 4):
                    part = list(tcs)[g:g + 4]
                    b = bank()
                    t = T(transposes([(PS[b][0:64, q * 128:q * 128 + 128], src(i)[:, h * 64:h * 64 + 64])
                                      for q, i in enumerate(part)]), rel[b], *deps)
                    lo, n = part[0] * 128, len(part) * 128
                    A(lambda e: e.activation(dst[0:64, h, lo:lo + n], PS[b][0:64, 0:n], ACT.Copy), t, *deps)
                    rel[b] = A(lambda e: e.activation(dst[64:128, h, lo:lo + n], PS[b][0:64, 0:n], ACT.Copy), t)

        def attention(groups, PB, filler=iter(()), rate=1):
            units, scored, exped, scaled, turned, copied = [], [], [], [], [], []
            valued, taken, todo = [], [], []
            for g, (us, buf, vals, cols_, out_) in enumerate(groups):
                units += [(g, n == len(us) - 1) + u for n, u in enumerate(us)]
            sunk = []

            def before(steps, x):
                return steps[x] if x >= 0 else None

            def score(x):
                g, end, q, ks, lo, n, masks, sink, c, places = units[x]
                p = PP[x % 2]
                T.wait(before(exped, x - 2))
                for k, at in ks:
                    t = T(lambda e: e.matmul(p[:, at:at + k.shape[1]], q, k, start=True, stop=True))
                for m, at in masks:
                    t = V(lambda e: e.tensor_tensor(p[:, at:at + 128], p[:, at:at + 128], m, ALU.add), t)
                scored.append(t)

            def soften(x):
                g, end, q, ks, lo, n, masks, sink, c, places = units[x]
                u = x % 2
                p = PP[u]
                m = sb[:, u * 8:u * 8 + 8]
                t = V(lambda e: e.tensor_reduce(m[:, 0:1], p[:, lo:lo + n], AX.X, ALU.max), scored[x], before(scaled, x - 2))
                if sink is not None:
                    t = V(lambda e: e.tensor_scalar(m[:, 0:1], m[:, 0:1], sink, -1.0, ALU.max, ALU.mult), t)
                else:
                    t = V(lambda e: e.tensor_scalar(m[:, 0:1], m[:, 0:1], -1.0, None, ALU.mult), t)
                exped.append(A(lambda e: e.activation(PB[:, u, 0:n], p[:, lo:lo + n], ACT.Exp, bias=m[:, 0:1],
                                                      accum_out=m[:, 1:2]), t, before(turned, x - 2)))
                if sink is not None:
                    sunk.append(A(lambda e: e.activation(m[:, 2:3], m[:, 0:1], ACT.Exp, bias=sink), t))

            def scale(x):
                g, end, q, ks, lo, n, masks, sink, c, places = units[x]
                u = x % 2
                m = sb[:, u * 8:u * 8 + 8]
                t = exped[x]
                if sink is not None:
                    t = V(lambda e: e.tensor_tensor(m[:, 1:2], m[:, 1:2], m[:, 2:3], ALU.add), t, sunk[x])
                t = V(lambda e: e.reciprocal(m[:, 3:4], m[:, 1:2]), t)
                scaled.append(V(lambda e: e.tensor_scalar(PB[:, u, 0:n], PB[:, u, 0:n], m[:, 3:4], None, ALU.mult), t))

            def turn(x):
                g, end, q, ks, lo, n, masks, sink, c, places = units[x]
                u, pt, buf = x % 2, PP[2], groups[g][1]
                turned.append(T(transposes([(pt[:, k * 128:k * 128 + 128], PB[:, u, k * 128:k * 128 + 128])
                                            for k in range(n // 128)]), scaled[x], before(copied, x - 1)))
                for k0, k1, to in places:
                    t = A(lambda e: e.activation(buf[:, to:to + k1 - k0, c * 128:c * 128 + 128],
                                                 pt[:, k0 * 128:k1 * 128].rearrange("p (k n) -> p k n", n=128), ACT.Copy),
                          turned[x], before(valued, g - 2))
                copied.append(t)
                if end:
                    todo.extend((g, k, v, c0, c1, j, x) for j, (k, v, c0, c1) in enumerate(groups[g][2]))

            def values(count):
                for _ in range(min(count, len(todo))):
                    g, k, v, c0, c1, j, x = todo.pop(0)
                    us, buf, vals, cols_, out_ = groups[g]
                    p0, dst = out_
                    t = T(lambda e: e.matmul(PS[6][p0:p0 + 64, c0:c1], v, buf[:, k, c0:c1], start=(j == 0),
                                             stop=(j == len(vals) - 1)), copied[x], before(taken, g - 1))
                    if j == len(vals) - 1:
                        valued.append(t)
                        taken.append(V(lambda e: e.tensor_tensor(dst, dst, PS[6][p0:p0 + 64, 0:cols_], ALU.mult), t))

            score(0)
            for x in range(len(units)):
                soften(x)
                if x + 1 < len(units):
                    score(x + 1)
                for _ in range(rate):
                    next(filler, None)
                scale(x)
                values(2)
                if x:
                    turn(x - 1)
                for _ in range(rate):
                    next(filler, None)
            turn(len(units) - 1)
            values(len(todo))
            for _ in filler:
                pass
            rel[:] = [None] * 8
            return [taken[-1], valued[-1], copied[-1]]

        x512 = lambda w: w.rearrange("p (k n) -> p k n", n=512)
        thc = [adaln(0, i, i - 4, HT, txc) for i in (4, 5)]
        s1, w1, tw1 = W.take()
        s2, w2, tw2 = W.take()
        tgq, tkv = {}, {}

        def gqa_projections(i, th):
            tgq[i], _ = gemm_t(HT, x512(w1), 0, 512, i, GQ[:, i, :], tw1, th)
            gemm_t(HT, x512(w2), 0, 32, i, KR[:, i, :], tw2)
            tkv[i], t = gemm_t(HT, x512(w2), 32, 256, i, GKV[:, i, :])
            return t

        for i in (4, 5):
            gqa_projections(i, thc[i - 4])
        th = [adaln(0, i, i, HT, combine(i)) for i in range(4)]
        dump("x2", X, V.last())
        if stop == "x2":
            barrier(tgr, txc, tc3)
            return fin()
        for i in range(4):
            t = gqa_projections(i, th[i])
        W.give(s1, t)
        W.give(s2, t)
        th = [th, thc]

        def gqa_norms(i, t):
            t = run(head_norm(GQ[:, i, :], 8, 64, gains[:, 192:256], 0.125, rt, small[:, 48:56], tgq[i], t))
            if i < 4:
                t = run(rope(GQ[:, i, :], 8, 64, 0, 16, i, True, rt, t, tc3))
            t = run(head_norm(GKV[:, i, 0:128], 2, 64, gains[:, 256:320], 1.0, rt, small[:, 48:56], t, tkv[i]))
            if i < 4:
                t = run(rope(GKV[:, i, 0:128], 2, 64, 0, 16, i, True, rt, t))
            return t

        s, w, tw = W.take()
        w = x512(w)
        tn = gqa_norms(4, V.last())
        sq, rs = spare[:, 0:1536].rearrange("p (a n) -> p a n", n=768), spare[:, 1536:2304]
        cq_squared = [None] * 4
        for i in range(4):
            for lo, n in ((0, 512), (512, 256)):
                b = bank()
                t = gemm_f(w, i * 128, lambda k: HT[:, k, lo:lo + n], PS[b][:, 0:n], b, tw, th)
                rel[b] = tcq = A(lambda e: e.activation(CQ[:, i, lo:lo + n], PS[b][:, 0:n], ACT.Copy), t)
        W.give(s, t)
        tn = gqa_norms(5, tn)
        tcn, tsum = [], None
        for a in range(2):
            for i in range(2):
                ts = A(lambda e: e.activation(sq[:, i, :], CQ[:, 2 * a + i, :], ACT.Square), tcq, tsum)
            g0 = r_cq if a == 0 else r_ck
            for lo, n in ((0, 512), (512, 256)):
                b = bank()
                tsum = T(mms(PS[b][:, 0:n], [(ones, sq[:, i, lo:lo + n]) for i in range(2)]), ts, rel[b])
                t2, rel[b] = rsqrt(rs[:, lo:lo + n], PS[b][:, 0:n], 1.0 / 256, tsum, tcn)
            for i in range(2):
                x = CQ[:, 2 * a + i, :]
                tcn.append(V(lambda e: e.scalar_tensor_tensor(x, x, VF[:, g0 + i:g0 + i + 1], rs, ALU.mult, ALU.mult), t2))
        for c in range(2):
            s, w, tw = W.take()
            w = x512(w)
            for i in range(4):
                for lo, n in ((0, 512), (512, 256)):
                    b = bank()
                    t = gemm_f(w, i * 128, lambda k: HT[:, k, lo:lo + n], PS[b][:, 0:n], b, tw, th, acc_read, yg_read)
                    rel[b] = A(lambda e: e.activation(GTE[:, c * 4 + i, lo:lo + n], PS[b][:, 0:n], ACT.Silu), t)
                if c == 0:
                    tn = gqa_norms(i, tn)
            W.give(s, t)
        dump("gq", GQ, tn)
        R = lambda at, *dims: spare[:, at:at + int(np.prod(dims))].rearrange("p (a n) -> p a n", n=dims[1])
        QT, KT, PTM = R(0, 4, 768), R(3072, 2, 768), R(4608, 6, 512)
        PTC = spare[:, 7680:8192].rearrange("p (k n) -> p k n", n=256)
        gq_ = GQ.rearrange("p a n -> p (a n)")
        PB, LK1 = [gq_[:, a * 1536:a * 1536 + 1536].rearrange("p (a n) -> p a n", n=768) for a in range(2)]
        pairs_t(lambda i: GQ[:, i, :], 8, QT, range(6), tn, tcn)
        twice_t(lambda i: GKV[:, i, 0:128], 2, KT, range(6))
        barrier()
        top[0] = tail - 6144
        LQ, LK, LV = [alloc(4, 768), R(0, 4, 768)], [[alloc(2, 768), alloc(2, 768)], [LK1, R(3072, 2, 768)]], [alloc(6, 256), GKV]
        QA, KA = alloc(2, 384), alloc(2, 384)
        assert top[0] <= tail + 3072
        sl, wl, twl = W.take()
        wq = wl[:, 0:1536].rearrange("p (k n) -> p k n", n=768)
        wkv = wl[:, 1536:3584].rearrange("p (k n) -> p k n", n=1024)
        latent = {}

        def latent_heads(hh, free):
            VAl = LV[hh]
            QTl = [(LQ[hh], PS[7][0:96, :])]
            KTl = [(LK[hh][a], PS[7][0:96, a * 256:a * 256 + 256]) for a in range(2)]
            normed, turned, read = {}, {}, None
            st = small[:, 48:56]

            def turn(i, src, dst, key):
                nonlocal read
                t = T(transposes([(PS[7][0:96, h * 128:h * 128 + 128], src[:, i % 2, h * 96:h * 96 + 96]) for h in range(4)]),
                      normed[key, i], read)
                turned[key, i] = t
                for d, p in dst:
                    read = A(lambda e: e.activation(d[0:96, :, i * 128:i * 128 + 128], p.rearrange("p (h n) -> p h n", n=128),
                                                    ACT.Copy), t, free)

            t = None
            for i in range(6):
                tok = slice(i * 128, i * 128 + 128)
                tm = T(mms(PS[7][:, 0:384], [(CQ[:, k, tok], wq[:, k, hh * 384:hh * 384 + 384]) for k in range(2)]), twl, tcn, read)
                read = te = A(lambda e: e.activation(QA[:, i % 2, :], PS[7][:, 0:384], ACT.Copy), tm, turned.get(("q", i - 2)))
                t = yield from head_norm(QA[:, i % 2, :], 4, 96, gains[:, 0:96], 96.0 ** -0.5, rt, st, te, t)
                if i < 4:
                    t = yield from rope(QA[:, i % 2, :], 4, 96, 64, 8, i, False, rt, t)
                normed["q", i] = t
                yield
                if i:
                    turn(i - 1, QA, QTl, "q")
                    yield
                tm = T(mms(PS[7], [(CQ[:, 2 + k, tok], wkv[:, k, hh * 512:hh * 512 + 512]) for k in range(2)]), read)
                kv = PS[7].rearrange("p (h d) -> p h d", d=128)
                ka = KA[:, i % 2, :].rearrange("p (h d) -> p h d", d=96)
                va = VAl[:, i, :].rearrange("p (h d) -> p h d", d=64)
                t1 = A(lambda e: e.activation(ka[:, :, 0:64], kv[:, :, 0:64], ACT.Copy), tm, turned.get(("k", i - 2)))
                read = A(lambda e: e.activation(va, kv[:, :, 64:128], ACT.Copy), tm, free)
                t2 = G(lambda e: e.tensor_copy(ka[:, :, 64:96], KR[:, i, :].unsqueeze(1).to_broadcast([128, 4, 32])),
                       turned.get(("k", i - 2)))
                t = yield from head_norm(KA[:, i % 2, :], 4, 96, gains[:, 96:192], 1.0, rt, st, t, t1, t2)
                if i < 4:
                    t = yield from rope(KA[:, i % 2, :], 4, 96, 64, 8, i, False, rt, t)
                normed["k", i] = t
                yield
                if i:
                    turn(i - 1, KA, KTl, "k")
                    yield
            if hh == 1:
                W.give(sl, tm)
            turn(5, QA, QTl, "q")
            yield
            turn(5, KA, KTl, "k")
            latent[hh] = read

        def dense(H, qs, kts, vals, tile):
            groups = []
            for h in range(H):
                q, k, p0 = qs(h), kts(h), 64 * (h % 2)
                units = [(q[:, i * 128:i * 128 + 128], [(k[:, 0:512], 0), (k[:, 512:768], 512)], 0, 768, [], None, i,
                          [(0, 6, 0)]) for i in range(4)]
                groups.append((units, PTM, [(j, vals(h, j), 0, 512) for j in range(6)], 512,
                               (p0, GTE[p0:p0 + 64, tile + h // 2, 0:512])))
                units = [(q[:, i * 128:i * 128 + 128], [(k[:, 512:768], 512)], 512, 256, [], None, i - 4, [(0, 2, 0)])
                         for i in (4, 5)]
                groups.append((units, PTC, [(j, vals(h, 4 + j), 0, 256) for j in range(2)], 256,
                               (p0, GTE[p0:p0 + 64, tile + h // 2, 512:768])))
            return groups

        half = lambda h: slice(64 * (h % 2), 64 * (h % 2) + 64)
        ta = attention(dense(8, lambda h: QT[half(h), h // 2, :], lambda h: KT[half(h), h // 4, :],
                             lambda h, k: GKV[:, k, 128 + 64 * (h // 4):192 + 64 * (h // 4)], 4), PB,
                       latent_heads(0, None), 1)
        dump("gte", GTE, V.last())
        barrier()
        if stop == "gqa":
            return fin()
        for hh in range(2):
            ta = attention(dense(4, lambda h: LQ[hh][0:96, h, :], lambda h: LK[hh][h // 2][0:96, h % 2, :],
                                 lambda h, k: LV[hh][:, k, h * 64:h * 64 + 64], hh * 2), PB,
                           latent_heads(1, ta) if hh == 0 else iter(()), 2)
            barrier()
        dump("gte2", GTE, V.last())
        top[0] = tail - 6144
        GR, GC = alloc(1024), alloc(1024)
        TM = alloc(2, 512)
        for g, r in ((GR, 0), (GC, 1)):
            t3 = d3(A, g, MOD2[0, r:r + 1, 2048:3072].partition_broadcast(128), everyone())
        tx = project(GTE, range(6), xrow, lambda i: GR if i < 4 else GC, TM, ta, t3)
        dump("x3", X, V.last())
        dump("xc3", XC, V.last())
        barrier()
        if stop == "x3":
            return fin()

        top[0] = mark + 640
        PQ = alloc(4, 512)
        PKV = alloc(6, 256)
        MT = alloc(8, 512)
        UP = alloc(4, 514)
        HT = alloc(8, 768)
        YF = alloc(2, 512)
        XN = alloc(2, 1024)
        rt = alloc(1024)
        GR = alloc(1024)
        assert top[0] <= WORDS - 4096, top[0]
        t3 = d3(A, GR, MOD2[1, 0:1, 2048:3072].partition_broadcast(128))
        tz = G(lambda e: e.memset(UP, 0.0))
        xn_read[:] = [None, None]
        tmp_ = scales(1)
        th = [adaln(1, i, i, HT, tx[i]) for i in range(6)]
        s, w, tw = W.take()
        tpq, tpk = {}, {}
        for i in range(4):
            tpq[i], t = gemm_t(HT, x512(w), 0, 512, i, PQ[:, i, :], tw, th[i])
        W.give(s, t)
        s, w, tw = W.take()
        for i in range(6):
            tpk[i], t = gemm_t(HT, x512(w), 0, 256, i, PKV[:, i, :], tw, th[i])
        W.give(s, t)

        def win_norms(i, t):
            if i < 4:
                t = run(head_norm(PQ[:, i, :], 8, 64, gains[:, 320:384], 0.125, rt, small[:, 48:56], t, tpq[i]))
                t = run(rope(PQ[:, i, :], 8, 64, 0, 16, i, True, rt, t))
            t = run(head_norm(PKV[:, i, 0:128], 2, 64, gains[:, 384:448], 1.0, rt, small[:, 48:56], t, tpk[i]))
            if i < 4:
                t = run(rope(PKV[:, i, 0:128], 2, 64, 0, 16, i, True, rt, t))
            return t

        tn, tgb, tup = V.last(), [], []
        for c in range(3):
            s, w, tw = W.take()
            w = x512(w)
            for i in range(4):
                b = bank()
                t = gemm_f(w, i * 128, lambda k: HT[:, k, 0:512], PS[b], b, tw)
                if c == 0:
                    rel[b] = A(lambda e: e.activation(MT[:, 4 + i, :], PS[b], ACT.Copy), t)
                    tgb.append(rel[b])
                elif c == 1:
                    rel[b] = A(lambda e: e.activation(UP[:, i, 1:513], PS[b], ACT.Copy), t, tz)
                    tup.append(rel[b])
                else:
                    rel[b] = V(lambda e: e.tensor_tensor(UP[:, i, 1:513], UP[:, i, 1:513], PS[b], ALU.mult), t, tup[i])
                    tup[i] = rel[b]
                n = 4 * c + i
                if n % 2 == 0:
                    tn = win_norms(n // 2, tn)
            W.give(s, t)
        yf = [None, None]
        tod = []
        for i in range(4):
            y = YF[:, i % 2, :]
            t = tup[i]
            for j in range(3):
                cw = VF[:, r_c2 + j * 4 + i:r_c2 + j * 4 + i + 1]
                uv = UP[:, i, j:j + 512]
                if j == 0:
                    t = V(lambda e: e.tensor_scalar(y, uv, cw, None, ALU.mult), t, yf[i % 2])
                else:
                    t = V(lambda e: e.scalar_tensor_tensor(y, uv, cw, y, ALU.mult, ALU.add), t)
            yf[i % 2] = V(lambda e: e.tensor_tensor(MT[:, 4 + i, :], MT[:, 4 + i, :], y, ALU.mult), t, tgb[i])
            tod.append(yf[i % 2])
        s, w, tw = W.take()
        w = x512(w)
        for i in range(4):
            b = bank()
            t = gemm_f(w, i * 128, lambda k: HT[:, k, 0:512], PS[b], b, tw)
            rel[b] = tga = A(lambda e: e.activation(MT[:, i, :], PS[b], ACT.Silu), t)
        W.give(s, t)
        s, w, tw = W.take()
        w = x512(w)
        for i in range(4):
            b = bank()
            u = i % 2
            t = gemm_f(w, i * 128, lambda k: HT[:, k, 0:512], PS[b], b, tw)
            rel[b] = t1 = A(lambda e: e.activation(YF[:, u, :], PS[b], ACT.Silu), t, yf[0], yf[1])
            yf[u] = V(lambda e: e.tensor_tensor(MT[:, 4 + i, :], MT[:, 4 + i, :], YF[:, u, :], ALU.mult), t1, tod[i])
        W.give(s, t)
        QT, KT = R(0, 4, 512), R(2048, 2, 768)
        pairs_t(lambda i: PQ[:, i, :], 8, QT, range(4), tn)
        twice_t(lambda i: PKV[:, i, 0:128], 2, KT, range(6))
        barrier()
        PTW = [HT.rearrange("p a n -> p (a n)")[:, a * 3072:a * 3072 + 3072].rearrange("p (k n) -> p k n", n=512) for a in range(2)]
        PB = XN.rearrange("p a n -> p (a n)")[:, 0:1536].rearrange("p (a n) -> p a n", n=768)
        wmp, wmn = c3[:, 384:512], c3[:, 512:640]
        groups = []
        for h in range(8):
            q, k, p0 = QT[half(h), h // 2, :], KT[half(h), h // 4, :], 64 * (h % 2)
            units = []
            for n in range(4):
                lo, hi = max(n - 1, 0), min(n + 2, 4)
                L = (hi - lo) * 128
                at = 512 - L
                masks = ([(wmp, at)] if n else []) + ([(wmn, 384)] if n < 3 else [])
                units.append((q[:, n * 128:n * 128 + 128], [(k[:, lo * 128:hi * 128], at), (k[:, 512:768], 512)],
                              at, L + 256, masks, sinkr[:, 8 + h:9 + h], n, [(0, hi - lo, lo), (hi - lo, hi - lo + 2, 4)]))
            v = lambda j: PKV[:, j, 128 + 64 * (h // 4):192 + 64 * (h // 4)]
            vals = [(j, v(j), 0, 512) for j in (4, 5)] \
                + [(j, v(j), max(j - 1, 0) * 128, min(j + 2, 4) * 128) for j in range(4)]
            groups.append((units, PTW[h % 2], vals, 512, (p0, MT[p0:p0 + 64, h // 2, :])))
        ta = attention(groups, PB)
        TM = YF
        tx = project(MT, range(4), xrow, lambda i: GR, TM, ta, yf, t3)
        do = dsem("out")
        for i in range(4):
            t = do(S, out[0, i * 128:i * 128 + 128, :], X[:, i, :], tx[i])
        S.wait(t)


_INS = ['x', 'c', 'w_ada', 'b_ada', 'norm1_w', 'w_in', 'conv_w', 'a_log', 'dt_bias', 'dn_norm_w', 'q_norm_w',
        'k_norm_w', 'sinks', 'w_out', 'norm2_w', 'w_router', 'b_router', 'w_up', 'b_up', 'w_down', 'b_down', 'c_2',
        'ctx_2', 'c_ctx_2', 'mod_w_2', 'mod_b_2', 'ab_w_in_2', 'ab_w_out_2', 'mla_cq_gain_2', 'mla_ckv_gain_2',
        'mla_w_uq_2', 'mla_w_ukv_2', 'mla_q_gain_2', 'mla_k_gain_2', 'gqa_q_gain_2', 'gqa_k_gain_2', 'cd_w_in_2',
        'cd_w_out_2', 'win_q_gain_2', 'win_k_gain_2', 'win_sink_2', 'conv_w_2']


def build(nc, arrays, dbg_shapes=None, stop=None):
    D = {}
    for n, a in arrays.items():
        D[n] = nc.dram_tensor("in_" + n, a.shape, F32, kind="ExternalInput").ap()
    out = nc.dram_tensor("out_0", (1, 512, 1024), F32, kind="ExternalOutput").ap()
    dbg = None
    if dbg_shapes:
        dbg = {n: nc.dram_tensor("dbg_" + n, s, dt, kind="ExternalOutput").ap() for n, (s, dt) in dbg_shapes.items()}
    program(nc, D, out, dbg, stop)


def kernel(**inputs):
    import concourse.bacc as _bacc
    from concourse.bass_utils import run_bass_kernel_spmd as _run

    nc = _bacc.Bacc("TRN2", target_bir_lowering=False, num_devices=1)
    arrays = {n: np.ascontiguousarray(inputs[n]) for n in _INS}
    arrays.update(constants())
    build(nc, arrays)
    r = _run(nc, [{"in_" + n: a for n, a in arrays.items()}], core_ids=[0])
    return r.results[0]["out_0"]
```

```python
import numpy as np
import concourse.bass as bass
from concourse import mybir
from concourse.alu_op_type import AluOpType as ALU
from contextlib import ExitStack

F32 = mybir.dt.float32
I32 = mybir.dt.int32
U32 = mybir.dt.uint32
BF16 = mybir.dt.bfloat16
ACT = mybir.ActivationFunctionType
AX = mybir.AxisListType
EPS = 1e-6
NEG = -1e30
NSLOT = 5
NEXP = 32
NXB = 15
NBLK = NEXP + NXB
NBU = 3


class Engine:

    def __init__(self, eng, sem):
        self.eng, self.sem, self.n, self.on = eng, sem, 0, True
        self.seen = {}

    def wait(self, *deps):
        for d in deps:
            if d is None:
                continue
            if isinstance(d, list):
                self.wait(*d)
                continue
            sem, v = d
            if self.on and self.seen.get(id(sem), 0) < v:
                self.eng.wait_ge(sem, v)
                self.seen[id(sem)] = v

    def __call__(self, f, *deps):
        self.wait(*deps)
        if self.on:
            f(self.eng).then_inc(self.sem, 1)
        self.n += 1
        return (self.sem, self.n)

    def last(self):
        return (self.sem, self.n)


class DmaSem:

    def __init__(self, sem):
        self.sem, self.n = sem, 0

    def __call__(self, E, out, in_, *deps, f=None):
        E.wait(*deps)
        if E.on:
            i = E.eng.dma_start(out, in_) if f is None else f(E.eng)
            i.then_inc(self.sem, 16)
        self.n += 16
        return (self.sem, self.n)


def constants():
    p = np.arange(128)[:, None]
    j = np.arange(128)[None, :]
    same = (p // 64) == (j // 64)
    eye = np.eye(128)
    c0 = np.concatenate([eye, np.ones((128, 128))], 1)
    m1 = same & (p <= j)
    m2 = same & (p > j)
    cols = [m2, m1, same]
    for b in (1, 2, 4, 8, 16, 32):
        cols.append((p // (2 * b) == j // (2 * b)) & ((p // b) % 2 == 0) & ((j // b) % 2 == 1))
    cols.append((p // 2 == j // 2) & (p % 2 == 1) & (j % 2 == 0))
    c1 = np.concatenate(cols, 1)
    k2 = np.arange(256)[None, :]
    rel = (p + 128 - k2).astype(np.float32)
    slopes = 2.0 ** (-8.0 * np.arange(1, 9, dtype=np.float32) / 8)
    ok = (rel >= 0) & (rel < 128)
    swa = np.concatenate([np.where(ok, -s * rel, NEG) for s in slopes], 1)
    c2 = np.concatenate([
        p < j,
        np.broadcast_to(j, (128, 128)),
        np.broadcast_to(128.0 * np.arange(32), (128, 32)),
        np.broadcast_to(np.repeat(np.arange(NXB), 32), (128, NXB * 32)),
        p + 128 * np.arange(4)[None, :]], 1)
    t = np.arange(512)
    pos = np.stack([(t // 64), (t % 64)], 1).astype(np.float32)

    def rope(half):
        inv = (np.float32(10000.0) ** (-np.arange(half, dtype=np.float32) / np.float32(half))).astype(np.float32)
        ang = (pos[:, :, None] * inv).astype(np.float32)
        out = []
        for f in (np.cos, np.sin):
            out.append(f(ang).reshape(4, 128, 2 * half).transpose(1, 0, 2).reshape(128, 8 * half))
        return out

    wm = [np.where(j >= p, 0.0, NEG), np.where(j <= p, 0.0, NEG)]
    c3 = np.concatenate(rope(16) + rope(8) + wm, 1)
    return {n: np.ascontiguousarray(a, np.float32) for n, a in
            dict(cst0=c0, cst1=c1, cst1b=swa, cst2=c2, cst3=c3).items()}


def program(nc, D, out, dbg=None, stop=None):
    ctx = ExitStack()
    with ctx:
        def sem(name):
            return ctx.enter_context(nc.semaphore(name))

        def dram(name, shape, dt=F32):
            return nc.dram_tensor(name, shape, dt, kind="Internal").ap()

        engs = [nc.tensor, nc.vector, nc.scalar, nc.gpsimd, nc.sync]
        names = ["pe", "dve", "act", "pool", "sp"]
        T, V, A, G, S = [Engine(e, sem("s_" + n)) for e, n in zip(engs, names)]
        EN = [T, V, A, G, S]

        def dsem(name):
            return DmaSem(sem("d_" + name))

        def everyone():
            return [e.last() for e in EN[:4]]

        def fin():
            S.wait(*[(q.sem, q.n) for q in W.sems], everyone())

        dead = []

        def barrier(*dmas):
            t = everyone()
            for e in EN[:4]:
                e.wait(t, *dmas)
            dead[:] = t

        ring = ctx.enter_context(nc.sbuf_tensor("ring", [128, NSLOT * 4096], F32))
        WORDS = 32400
        mem = ctx.enter_context(nc.sbuf_tensor("mem", [128, WORDS], F32))
        PP = [ctx.enter_context(nc.psum_tensor(f"ps{i}", [128, 1024], F32)) for i in range(4)]
        PS = [PP[b // 2][:, (b % 2) * 512:(b % 2) * 512 + 512] for b in range(8)]
        rel = [None] * 8
        turn, banks = [0], list(range(8))

        def bank():
            turn[0] = (turn[0] + 1) % len(banks)
            return banks[turn[0]]

        top = [0]

        def alloc(*dims, dt=F32, at=None):
            n = int(np.prod(dims))
            if at is None:
                at = top[0]
                top[0] += n
            assert at + n <= WORDS, (at, n)
            v = mem[:, at:at + n]
            if dt != F32:
                v = v.bitcast(dt)
            if len(dims) == 2:
                v = v.rearrange("p (a b) -> p a b", b=dims[1])
            if len(dims) == 3:
                v = v.rearrange("p (a b c) -> p a b c", b=dims[1], c=dims[2])
            return v

        loads = []

        class Stream:
            def __init__(self, tag, slots=NSLOT):
                self.slots = slots
                self.sems = [dsem(f"w{tag}{i}") for i in range(slots)]
                self.issued = self.taken = 0
                self.free = [None] * slots

            def issue(self):
                if self.issued >= len(loads):
                    return
                s = self.issued % self.slots
                for dst, src in loads[self.issued]:
                    self.sems[s](S, dst(ring[:, s * 4096:(s + 1) * 4096]), src, self.free[s])
                self.issued += 1

            def take(self):
                s = self.taken % self.slots
                assert self.taken < self.issued
                self.taken += 1
                return s, ring[:, s * 4096:(s + 1) * 4096], (self.sems[s].sem, self.sems[s].n)

            def give(self, s, tok):
                self.free[s] = tok
                self.issue()

        def cols(n0, n):
            return lambda v: v.rearrange("p (k n) -> p k n", n=512)[:, :, n0:n0 + n]

        def kp(w):
            return w.rearrange("(k p) n -> p k n", p=128)

        def pk(w):
            return w.rearrange("(p k) n -> p k n", k=8)

        for c in range(4):
            loads.append([(cols(0, 512), pk(D["w_ada"][0])[:, :, c * 512:c * 512 + 512])])
        wi = kp(D["w_in"][0])
        loads.append([(cols(0, 512), wi[:, :, 2056:2568])])
        loads.append([(cols(0, 8), wi[:, :, 2048:2056])]
                     + [(cols(8 + 64 * i, 64), wi[:, :, 2568 + 64 * (i // 2):2632 + 64 * (i // 2)]) for i in range(4)]
                     + [(cols(264, 128), wi[:, :, 2696:2824])])
        for c in range(4):
            loads.append([(cols(0, 512), wi[:, :, c * 512:c * 512 + 512])])
        for c in range(4, 12):
            loads.append([(cols(0, 512), pk(D["w_ada"][0])[:, :, c * 512:c * 512 + 512])])
        for l in range(2):
            for c in range(6):
                loads.append([(cols(0, 512), pk(D["mod_w_2"][l])[:, :, c * 512:c * 512 + 512])])
        wo = kp(D["w_out"][0])
        for c in range(2):
            loads.append([(cols(0, 512), wo[:, :, c * 512:c * 512 + 512])])

        def up_loads(w):
            w = kp(w)
            return [[(lambda v: v.rearrange("p (k n) -> p k n", n=2048), w[:, 2 * q:2 * q + 2, :])] for q in range(4)]

        def down_loads(w):
            w = kp(w)
            return [[(lambda v: v.rearrange("p (k n) -> p k n", n=1024), w[:, 4 * q:4 * q + 4, :])] for q in range(2)]

        for e in range(NEXP):
            loads += up_loads(D["w_up"][0, e])
            if e:
                loads += down_loads(D["w_down"][0, e - 1])
        loads += down_loads(D["w_down"][0, NEXP - 1])
        n_first = len(loads)
        ab = kp(D["ab_w_in_2"][0])
        loads.append([(cols(0, 512), ab[:, :, 544:1056])])
        loads.append([(cols(0, 32), ab[:, :, 512:544]), (cols(32, 256), ab[:, :, 1056:1312])])
        loads.append([(cols(0, 512), ab[:, :, 0:512])])
        loads.append([(cols(0, 512), ab[:, :, 1312:1824])])
        loads.append([(cols(0, 512), ab[:, :, 1824:2336])])
        uq = D["mla_w_uq_2"][0].rearrange("(k p) n -> p k n", p=128)
        ukv = D["mla_w_ukv_2"][0].rearrange("(k p) n -> p k n", p=128)
        loads.append([(lambda v: v[:, 0:1536].rearrange("p (k n) -> p k n", n=768), uq),
                      (lambda v: v[:, 1536:3584].rearrange("p (k n) -> p k n", n=1024), ukv)])
        for c in range(2):
            loads.append([(cols(0, 512), kp(D["ab_w_out_2"][0])[:, :, c * 512:c * 512 + 512])])
        cd = kp(D["cd_w_in_2"][0])
        loads.append([(cols(0, 512), cd[:, :, 0:512])])
        loads.append([(cols(0, 256), cd[:, :, 512:768])])
        for c in range(5):
            loads.append([(cols(0, 512), cd[:, :, 768 + 512 * c:1280 + 512 * c])])
        for c in range(2):
            loads.append([(cols(0, 512), kp(D["cd_w_out_2"][0])[:, :, c * 512:c * 512 + 512])])
        later = loads[n_first:]
        del loads[n_first:]

        W = Stream("a")

        def dump(name, ap, *deps):
            if dbg is not None and name in dbg:
                d = dsem("dbg_" + name)
                t = d(G, dbg[name], ap, *deps)
                for e in EN:
                    e.wait(t)

        alt = [0]

        def evac(o, i, *deps):
            alt[0] ^= 1
            if alt[0]:
                return V(lambda e: e.tensor_copy(o, i), *deps)
            return A(lambda e: e.activation(o, i, ACT.Copy), *deps)

        def rsqrt(o, i, scale, *deps, eps=EPS):
            t = V(lambda e: e.tensor_scalar(o, i, scale, eps, ALU.mult, ALU.add), *deps)
            t2 = A(lambda e: e.activation(o, o, ACT.Sqrt), t)
            return V(lambda e: e.reciprocal(o, o), t2), t

        def mms(o, pairs):
            def f(e):
                for n, (l, r) in enumerate(pairs):
                    i = e.matmul(o, l, r, start=(n == 0), stop=(n == len(pairs) - 1))
                return i
            return f

        def transposes(items):
            def f(e):
                for o, i in items:
                    k = i.shape[0]
                    r = e.transpose(o, i, ident[0:k, 0:k])
                return r
            return f

        cst0 = alloc(256)
        ident, ones = cst0[:, 0:128], cst0[:, 128:256]
        VF = alloc(80)
        modF = alloc(16)
        mod2F = alloc(2, 48)
        small = alloc(64)
        rows4 = alloc(32)
        sinkr = alloc(16)
        gains = alloc(448)
        rout = alloc(4, 32)
        GT = alloc(4, 4)
        DEST = alloc(16, dt=I32)
        ROW = alloc(48, dt=I32)
        XE = alloc(16, dt=I32)
        cact = alloc(3, 8)
        ones3 = alloc(64).bitcast(BF16)
        base = top[0]
        MOD = dram("mod_rows", (6144,))
        MOD2 = dram("mod2_rows", (2, 2, 3072))
        H2D = dram("h2_rows", (512, 1024))
        BIASD = dram("bias_rows", (NEXP, 3, 3072), BF16)
        YD = dram("y_rows", (NBLK * 128, 1024))

        dcv = dsem("cvec")
        for i, n in enumerate(["c", "c_2", "c_ctx_2"]):
            src = D[n] if n == "c_ctx_2" else D[n][0]
            tcv = dcv(S, cact[:, i, :], src.rearrange("(p j) -> p j", j=8))
        top[0] = WORDS - 8192 - 5120 - 128
        brow, modrow, junk = alloc(2048), alloc(2048), alloc(1024)
        W.issue()
        dcb = dsem("b_ada")
        tcb = dcb(S, brow[0:1, :], D["b_ada"][:, 0:2048])
        dcc = dsem("cst0")
        tc0 = dcc(S, cst0, D["cst0"])
        for _ in range(3):
            W.issue()
        X = alloc(4, 1024, at=WORDS - 8192)
        dx = dsem("x")
        tx = dx(S, X, D["x"][0].rearrange("(t p) d -> p t d", p=128))
        W.issue()
        tca = A(lambda e: e.activation(cact, cact, ACT.Silu), tcv)
        dc = dsem("const")
        vrows = alloc(128)
        nv = [0]

        def vrow(src, n):
            dc(A, vrows[nv[0]:nv[0] + n, :], src)
            nv[0] += n
            return nv[0] - n

        r_n1 = vrow(D["norm1_w"][0].rearrange("(a p) -> a p", p=128), 8)
        r_cw = vrow(D["conv_w"][0].rearrange("i (t p) -> (i t) p", p=128), 48)
        r_dn = vrow(D["dn_norm_w"], 1)

        def vrow2(src):
            for h in range(2):
                dc(A, vrows[nv[0]:nv[0] + 1, 64 * h:64 * h + 64], src)
            nv[0] += 1
            return nv[0] - 1

        r_qn = vrow2(D["q_norm_w"])
        r_kn = vrow2(D["k_norm_w"])
        r_c2 = vrow(D["conv_w_2"][0].rearrange("i (t p) -> (i t) p", p=128), 12)
        r_cq = vrow(D["mla_cq_gain_2"][0].rearrange("(a p) -> a p", p=128), 2)
        r_ck = vrow(D["mla_ckv_gain_2"][0].rearrange("(a p) -> a p", p=128), 2)
        dc(A, rows4[:, 0:4], D["a_log"].partition_broadcast(128))
        dc(A, rows4[:, 4:8], D["dt_bias"].partition_broadcast(128))
        dc(A, sinkr[:, 0:8], D["sinks"].partition_broadcast(128))
        dc(A, sinkr[:, 8:16], D["win_sink_2"].partition_broadcast(128))
        for n, (o, k) in dict(mla_q_gain_2=(0, 96), mla_k_gain_2=(96, 96), gqa_q_gain_2=(192, 64),
                              gqa_k_gain_2=(256, 64), win_q_gain_2=(320, 64), win_k_gain_2=(384, 64)).items():
            dc(A, gains[:, o:o + k], D[n].partition_broadcast(128))
        tc_ = (dc.sem, dc.n)

        d1 = dsem("cst1")
        tc1 = d1(A, mem[:, base + 4096:base + 4096 + 1280].rearrange("p (a b) -> p a b", b=128),
                 D["cst1"].rearrange("p (a b) -> p a b", b=128))

        BI = mem[:, base:base + 1536]
        BH = mem[:, base + 1536:base + 1536 + 2304].bitcast(BF16).rearrange("p (a n) -> p a n", n=1536)
        dbi = dsem("bias_in")
        dbo = dsem("bias_out")

        def split_biases(half, *deps):
            if half == 0:
                t = dbi(A, BI[0:NEXP, :], D["b_up"][0, :, 0:1536], *deps)
            else:
                dbi(A, BI[0:NEXP, 0:512], D["b_up"][0, :, 1536:2048], *deps)
                t = dbi(A, BI[0:NEXP, 512:1536], D["b_down"][0])
            for a in range(3):
                t = V(lambda e: e.tensor_copy(BH[0:NEXP, a, :], BI[0:NEXP, :]), t, *deps)
                if a < 2:
                    t = V(lambda e: e.tensor_tensor(BI[0:NEXP, :], BI[0:NEXP, :], BH[0:NEXP, a, :], ALU.subtract), t)
            return dbo(G, BIASD[:, :, half * 1536:half * 1536 + 1536], BH[0:NEXP], t)

        V(lambda e: e.memset(ones3, 1.0))

        b1 = 7
        banks[:] = list(range(7))
        for c in range(4):
            s, w, tw = W.take()
            w = w.rearrange("p (k n) -> p k n", n=512)
            b = bank()
            o, r = PS[b][0:1, :], modrow[0:1, c * 512:c * 512 + 512]
            t = T(mms(o, [(cact[:, 0:1, k], w[:, k, :]) for k in range(8)]), tw, tca, rel[b])
            W.give(s, t)
            rel[b] = t = V(lambda e: e.tensor_tensor(r, o, brow[0:1, c * 512:c * 512 + 512], ALU.add), t, tcb)

            def columns(e, c=c, r=r):
                for j in range(4):
                    i = e.matmul(PS[b1][:, c * 4 + j:c * 4 + j + 1], r[:, j * 128:j * 128 + 128], ones[0:1, 0:1],
                                 start=True, stop=True)
                return i
            if c:
                T(columns_before, t_before, tc0)
            columns_before, t_before = columns, t
        t = T(columns_before, t_before)
        tmf = V(lambda e: e.tensor_copy(modF, PS[b1][:, 0:16]), t)
        banks[:] = list(range(8))
        rel[b1] = tmf
        b = bank()
        t = T(transposes([(PS[b][:, 0:nv[0]], vrows[0:nv[0], :])]), tc_, tc0, rel[b])
        rel[b] = tvf = V(lambda e: e.tensor_copy(VF[:, 0:nv[0]], PS[b][:, 0:nv[0]]), t)
        A1 = small[:, 0:8]
        ta1 = V(lambda e: e.scalar_tensor_tensor(A1, modF[:, 8:16], 1.0, VF[:, r_n1:r_n1 + 8], ALU.add, ALU.mult), tmf, tvf)

        def rstd_rows(x, n, st, junk, *deps):
            for i in range(n):
                t = A(lambda e: e.activation(junk, x[:, i, :], ACT.Square, accum_out=st[:, i:i + 1]), *deps, *([t] if i else []))
            t, _ = rsqrt(st[:, 0:n], st[:, 0:n], 1.0 / 1024, t)
            return t

        st = small[:, 8:16]
        t = rstd_rows(X, 4, st, junk, tx)
        for i in range(4):
            t = V(lambda e: e.tensor_scalar(X[:, i, :], X[:, i, :], st[:, i:i + 1], None, ALU.mult), t)

        def to_features(src, dst, tcs, off, mul, add, *deps):
            for k in range(8):
                b = bank()
                n = len(tcs) * 128
                t = T(transposes([(PS[b][:, i * 128:i * 128 + 128], src[:, c, k * 128:k * 128 + 128])
                                  for i, c in enumerate(tcs)]), rel[b], *deps)
                o = dst[:, k, off:off + n]
                if mul is None:
                    rel[b] = evac(o, PS[b][:, 0:n], t)
                elif k % 2:
                    rel[b] = V(lambda e: e.tensor_scalar(o, PS[b][:, 0:n], mul[:, k:k + 1], add[:, k:k + 1],
                                                         ALU.mult, ALU.add), t)
                else:
                    rel[b] = A(lambda e: e.activation(o, PS[b][:, 0:n], ACT.Identity, bias=add[:, k:k + 1],
                                                      scale=mul[:, k:k + 1]), t)
            return [V.last(), A.last()]

        top[0] = X_at = base
        H1 = alloc(8, 512, at=WORDS - 4096)
        t = to_features(X, H1, range(4), 0, A1, modF[:, 0:8], t, ta1)
        dump("h1T", H1, t)
        barrier()
        th = t
        if stop == "h":
            return fin()

        top[0] = base
        MIX = alloc(8, 512)
        mark = top[0]
        c1 = alloc(10, 128)
        QKV = alloc(12, 512)
        ZT = alloc(4, 512)
        gsm = alloc(8, 16)
        g16, bet, eg, kd, bE, ngm = [gsm[:, i, :] for i in range(6)]
        sub = top[0]
        U = alloc(2, 515)
        swq = alloc(4, 512)
        swk = alloc(2, 512)
        swv = alloc(4, 128)
        BG = alloc(4, 8)
        swb = alloc(8, 256)
        LG_at = top[0]
        tmp = alloc(2, 512)
        rs = alloc(2, 512)
        LG = alloc(2, 4 * 256, at=LG_at)
        PT = alloc(2, 4 * 256)
        sm = alloc(2, 24)
        assert top[0] <= WORDS - 4096
        assert mark == base + 4096
        tbs = split_biases(0, everyone())
        tk1 = dsem("cst1b")(G, swb, D["cst1b"].rearrange("p (a b) -> p a b", b=256), everyone())
        M2, M1, BD = c1[:, 0, :], c1[:, 1, :], c1[:, 2, :]

        def gemm_f(w, n0, tok, o, b, *deps):
            return T(mms(o, [(w[:, k, n0:n0 + 128], tok(k)) for k in range(8)]), rel[b], *deps)

        def delta_projections():
            tz = G(lambda e: e.memset(U[:, :, 0:3], 0.0))
            squared, freed = [], [tz, tz]
            for n in range(16):
                if n % 4 == 0:
                    s, w, tw = W.take()
                    w = w.rearrange("p (k n) -> p k n", n=512)
                b = bank()
                tmm = gemm_f(w, n % 4 * 128, lambda k: H1[:, k, :], PS[b], b, tw, th)
                if n % 4 == 3:
                    W.give(s, tmm)
                if n >= 12:
                    rel[b] = A(lambda e: e.activation(ZT[:, n - 12, :], PS[b], ACT.Silu), tmm)
                else:
                    u, y = n % 2, QKV[:, n, :]
                    t = rel[b] = A(lambda e: e.activation(U[:, u, 3:515], PS[b], ACT.Copy), tmm, tz, freed[u])
                    for j in range(4):
                        cw = VF[:, r_cw + j * 12 + n:r_cw + j * 12 + n + 1]
                        uv = U[:, u, j:j + 512]
                        if j == 0:
                            t = V(lambda e: e.tensor_scalar(y, uv, cw, None, ALU.mult), t)
                        else:
                            t = V(lambda e: e.scalar_tensor_tensor(y, uv, cw, y, ALU.mult, ALU.add), t)
                    freed[u] = t
                    t = A(lambda e: e.activation(y, y, ACT.Silu), t)
                    if n < 8:
                        squared.append(A(lambda e: e.activation(U[:, u, 3:515], y, ACT.Square), t))
                if 1 <= n <= 8:
                    m = n - 1
                    b, x, r = bank(), QKV[:, m, :], U[:, m % 2, 3:515]
                    t = T(mms(PS[b], [(ones, r)]), squared[m], rel[b])
                    t, rel[b] = rsqrt(r, PS[b], 1.0, t)
                    f = 128.0 ** -0.5 if m < 4 else 1.0
                    freed[m % 2] = V(lambda e: e.scalar_tensor_tensor(x, x, f, r, ALU.mult, ALU.mult), t)
                yield

        filler = delta_projections()
        sw_squared, sw_summed, sw_normed = [], [], []

        def sw_square(i, x, t):
            sw_squared.append(A(lambda e: e.activation(tmp[:, i % 2, :], x, ACT.Square), t,
                                sw_summed[i - 2] if i >= 2 else None))

        def sw_norm(i):
            x = swq[:, i, :] if i < 4 else swk[:, i - 4, :]
            g = VF[:, r_qn:r_qn + 1] if i < 4 else VF[:, r_kn:r_kn + 1]
            u = i % 2
            b = bank()
            sw_summed.append(T(mms(PS[b], [(BD, tmp[:, u, :])]), sw_squared[i], rel[b], tc1))
            t, rel[b] = rsqrt(rs[:, u, :], PS[b], 1.0 / 64, sw_summed[i], sw_normed[i - 2] if i >= 2 else None)
            sw_normed.append(V(lambda e: e.scalar_tensor_tensor(x, x, g, rs[:, u, :], ALU.mult, ALU.mult), t))

        s, w, tw = W.take()
        w = w.rearrange("p (k n) -> p k n", n=512)
        for i in range(4):
            b = bank()
            t = gemm_f(w, i * 128, lambda k: H1[:, k, :], PS[b], b, tw, th)
            rel[b] = evac(swq[:, i, :], PS[b], t)
            sw_square(i, swq[:, i, :], rel[b])
            if i:
                sw_norm(i - 1)
        W.give(s, t)
        s, w, tw = W.take()
        w = w.rearrange("p (k n) -> p k n", n=512)
        for i in range(2):
            b = bank()
            t = gemm_f(w, 8 + i * 128, lambda k: H1[:, k, :], PS[b], b, tw)
            rel[b] = evac(swk[:, i, :], PS[b], t)
            sw_square(4 + i, swk[:, i, :], rel[b])
            sw_norm(3 + i)
        tbs = split_biases(1, tbs)
        for i in range(4):
            b = bank()
            t = T(mms(PS[b][:, 0:8], [(H1[:, k, i * 128:i * 128 + 128], w[:, k, 0:8]) for k in range(8)]), rel[b])
            t = T(mms(PS[b][:, 8:136], [(H1[:, k, i * 128:i * 128 + 128], w[:, k, 264:392]) for k in range(8)]))
            tbg = V(lambda e: e.tensor_copy(BG[:, i, :], PS[b][:, 0:8]), t)
            rel[b] = tsv = V(lambda e: e.tensor_copy(swv[:, i, :], PS[b][:, 8:136]))
        W.give(s, t)
        sw_norm(5)
        tn = sw_normed[5]
        gv = g16.rearrange("p (a b) -> p a b", b=4)
        bv = bet.rearrange("p (a b) -> p a b", b=4)
        nv_ = ngm.rearrange("p (a b) -> p a b", b=4)
        t = A(lambda e: e.activation(bv, BG[:, :, 4:8], ACT.Sigmoid), tbg)
        dtb = rows4[:, 4:8]
        for i in range(4):
            t1 = V(lambda e: e.tensor_tensor(gv[:, i, :], BG[:, i, 0:4], dtb, ALU.add), tbg)
        t2 = A(lambda e: e.activation(ngm, g16, ACT.Abs), t1)
        t2 = A(lambda e: e.activation(ngm, ngm, ACT.Exp, scale=-1.0), t2)
        t3 = A(lambda e: e.activation(rows4[:, 8:12], rows4[:, 0:4], ACT.Exp))
        t2 = V(lambda e: e.tensor_scalar(ngm, ngm, 1.0, None, ALU.add), t2)
        t2 = A(lambda e: e.activation(ngm, ngm, ACT.Ln), t2)
        t2 = V(lambda e: e.scalar_tensor_tensor(g16, g16, 0.0, ngm, ALU.max, ALU.add), t2)
        t2 = V(lambda e: e.tensor_scalar(g16, g16, -1.0, None, ALU.mult), t2)
        for i in range(4):
            tg = V(lambda e: e.tensor_tensor(gv[:, i, :], gv[:, i, :], rows4[:, 8:12], ALU.mult), t2, t3)
        next(filler)
        next(filler)
        b = bank()
        t = T(mms(PS[b][:, 0:16], [(M1, g16)]), tg, rel[b], tc1)
        t = T(mms(PS[b][:, 16:32], [(M2, g16)]))
        A(lambda e: e.activation(eg, PS[b][:, 0:16], ACT.Exp), t)
        rel[b] = t = A(lambda e: e.activation(kd, PS[b][:, 16:32], ACT.Exp), t)
        tgs = V(lambda e: e.tensor_tensor(bE, bet, eg, ALU.mult), t)
        for u in range(2):
            t0 = G(lambda e: e.memset(LG[:, u, 0:128], NEG), tn)
        lgf, ptf, smf = [None] * 2, [None] * 2, [None] * 2
        probs_done = []

        def sw_scores(h):
            u, p0, kv = h % 2, 64 * (h % 2), h // 4
            lg = LG[:, u, :].rearrange("p (a b) -> p a b", b=256)
            m = sm[:, u, :]
            sk = sinkr[:, h:h + 1]
            for n in range(4):
                lo = max(n - 1, 0) * 128
                N = (n + 1) * 128 - lo
                b = bank()
                q = swq[p0:p0 + 64, h // 2, n * 128:n * 128 + 128]
                k = swk[p0:p0 + 64, kv, lo:lo + N]
                t = T(mms(PS[b][:, 0:N], [(q, k)]), tn, rel[b])
                t = rel[b] = V(lambda e: e.scalar_tensor_tensor(lg[:, n, 256 - N:256], PS[b][:, 0:N], 0.125,
                                                                swb[:, h, 256 - N:256], ALU.mult, ALU.add),
                               t, lgf[u], t0, tk1)
            t = V(lambda e: e.tensor_reduce(m[:, 0:4], lg, AX.X, ALU.max), t, smf[u])
            t = V(lambda e: e.tensor_scalar(m[:, 0:4], m[:, 0:4], sk, -1.0, ALU.max, ALU.mult), t)
            for n in range(4):
                kl = slice(0 if n else 128, 256)
                tp = A(lambda e: e.activation(lg[:, n, kl], lg[:, n, kl], ACT.Exp, bias=m[:, n:n + 1],
                                              accum_out=m[:, 4 + n:5 + n]), t, smf[u])
            t = A(lambda e: e.activation(m[:, 8:12], m[:, 0:4], ACT.Exp, bias=sk), t)
            t = V(lambda e: e.tensor_tensor(m[:, 12:16], m[:, 4:8], m[:, 8:12], ALU.add), t, tp)
            tr = V(lambda e: e.reciprocal(m[:, 16:20], m[:, 12:16]), t)
            for n in range(4):
                kl = slice(0 if n else 128, 256)
                smf[u] = tr = V(lambda e: e.tensor_scalar(lg[:, n, kl], lg[:, n, kl], m[:, 16 + n:17 + n], None, ALU.mult), tr)
            probs_done.append(tr)

        sw_scores(0)
        for h in range(8):
            u, p0, kv = h % 2, 64 * (h % 2), h // 4
            lg = LG[:, u, :].rearrange("p (a b) -> p a b", b=256)
            pt = PT[:, u, :].rearrange("p (a b) -> p a b", b=256)
            if h < 7:
                sw_scores(h + 1)
            next(filler, None)
            for n in range(4):
                b = bank()
                ks = [0, 1] if n else [1]
                lgf[u] = t = T(transposes([(PS[b][:, k * 128:k * 128 + 128], lg[:, n, k * 128:k * 128 + 128]) for k in ks]),
                               probs_done[h], rel[b])
                if n:
                    A(lambda e: e.activation(pt[:, n - 1, 128:256], PS[b][:, 0:128], ACT.Copy), t, ptf[u])
                rel[b] = tpt = A(lambda e: e.activation(pt[:, n, 0:128], PS[b][:, 128:256], ACT.Copy), t, ptf[u])
            next(filler, None)
            b = bank()
            T.wait(tpt, rel[b], tsv)

            def values(e):
                for kt in (0, 2, 1, 3):
                    N = 256 if kt < 3 else 128
                    r = e.matmul(PS[b][p0:p0 + 64, kt * 128:kt * 128 + N], swv[:, kt, kv * 64:kv * 64 + 64], pt[:, kt, 0:N],
                                 start=(kt == 0), stop=(kt == 3))
                return r
            ptf[u] = t = T(values)
            rel[b] = V(lambda e: e.tensor_copy(MIX[p0:p0 + 64, 4 + h // 2, :], PS[b][p0:p0 + 64, :]), t, tbs)
        for _ in filler:
            pass
        dump("qkvT", QKV, everyone())
        if stop == "qkv":
            return fin()
        barrier()

        mbias, mrow = alloc(2, 512, at=WORDS - 4096), alloc(2, 512, at=WORDS - 3072)
        dmb, dms = [[dsem(f"{n}{i}") for i in range(2)] for n in ("mod_bias", "mod_row")]
        chunks = [(0, 1, D["b_ada"][:, c * 512:c * 512 + 512],
                   MOD[c * 512:c * 512 + 512].rearrange("(a n) -> a n", a=1)) for c in range(4, 12)]
        chunks += [(1, 2, D["mod_b_2"][l:l + 1, c * 512:c * 512 + 512].partition_broadcast(2),
                    MOD2[l][:, c * 512:c * 512 + 512]) for l in range(2) for c in range(6)]
        added, stored = [], []
        banks[:] = [0, 1, 4, 5, 6, 7]

        def other_modulations():
            steps = 0
            tb = [dmb[n](G, mbias[0:chunks[n][1], n, :], chunks[n][2]) for n in range(2)]
            for n, (first, m, bias, to) in enumerate(chunks):
                s, w, tw = W.take()
                w = w.rearrange("p (k n) -> p k n", n=512)
                o = PS[2 + n % 2][0:m, :]
                T.wait(tw, added[n - 2] if n >= 2 else None)
                for k in range(8):
                    t = T(lambda e: e.matmul(o, cact[:, first:first + m, k], w[:, k, :], start=(k == 0), stop=(k == 7)))
                    steps += 1
                    if steps % 3 == 0:
                        yield
                W.give(s, t)
                added.append(V(lambda e: e.tensor_tensor(mrow[0:m, n % 2, :], o, mbias[0:m, n % 2, :], ALU.add),
                               t, tb[n], stored[n - 2] if n >= 2 else None))
                stored.append(dms[n % 2](G, to, mrow[0:m, n % 2, :], added[n]))
                if n + 2 < len(chunks):
                    tb.append(dmb[n % 2](G, mbias[0:chunks[n + 2][1], n % 2, :], chunks[n + 2][2], added[n]))

        filler = other_modulations()

        for hp in range(2):
            top[0] = sub
            heads = [2 * hp, 2 * hp + 1]
            units = [(a, h, i) for a, h in enumerate(heads) for i in range(4)]
            VB, KB, KD = alloc(8, 128), alloc(8, 128), alloc(8, 128)
            EE = alloc(8, 384)
            LT, AQ = alloc(8, 128), alloc(8, 128)
            XX = alloc(8, 256)
            UU, WT = EE[:, :, 0:128], EE[:, :, 128:256]
            ST = alloc(2, 128)
            ZZ = alloc(8, 128)
            GM = alloc(4, 256)
            assert top[0] + 512 <= WORDS - 4096
            if hp == 0:
                zero = alloc(512, at=WORDS - 4096 - 512)
                tz = G(lambda e: e.memset(zero, 0.0))
                dz = dsem("zero")
                for j in range(NXB):
                    tz_ = dz(S, YD[(NEXP + j) * 128:(NEXP + j + 1) * 128, :].rearrange("p (a n) -> p a n", n=512),
                             zero.unsqueeze(1).to_broadcast([128, 2, 512]), tz)
            ttok = {}
            for a, h, i in units:
                n = a * 4 + i
                c = i * 4 + h
                tok = slice(i * 128, i * 128 + 128)
                b = bank()
                t = T(transposes([(PS[b][:, 0:128], QKV[:, 8 + h, tok]), (PS[b][:, 128:256], QKV[:, 4 + h, tok])]),
                      rel[b])
                A(lambda e: e.activation(VB[:, n, :], PS[b][:, 0:128], ACT.Copy, scale=bet[:, c:c + 1]), t)
                A(lambda e: e.activation(KB[:, n, :], PS[b][:, 128:256], ACT.Copy, scale=bE[:, c:c + 1]))
                rel[b] = A(lambda e: e.activation(KD[:, n, :], PS[b][:, 128:256], ACT.Copy, scale=kd[:, c:c + 1]))
            gf = [None] * 4
            tE, tD = {}, {}
            for a, h, i in units:
                n = a * 4 + i
                c = i * 4 + h
                gm = GM[:, n % 4, :]
                t = V(lambda e: e.tensor_scalar(gm[:, 0:128], M2, g16[:, c:c + 1], None, ALU.mult), gf[n % 4])
                t2 = G(lambda e: e.tensor_scalar(gm[:, 128:256], ones, g16[:, c:c + 1], None, ALU.mult), gf[n % 4])
                b = bank()
                T(mms(PS[b][:, 0:128], [(M1, gm[:, 0:128])]), t, rel[b])
                T(mms(PS[b][:, 128:256], [(gm[:, 0:128], M1)]))
                t = gf[n % 4] = T(mms(PS[b][:, 256:384], [(gm[:, 128:256], M1)]), t2)
                rel[b] = tD[n] = A(lambda e: e.activation(EE[:, n, :], PS[b][:, 0:384], ACT.Exp), t)
                for q in ([n - 2] if 2 <= n < 7 else [5, 6, 7] if n == 7 else []):
                    tE[q] = V(lambda e: e.tensor_tensor(EE[:, q, 0:256], EE[:, q, 0:256],
                                                        c1[:, 0:2, :].rearrange("p a b -> p (a b)"), ALU.mult), tD[q])
            tX, tL = {}, {}

            def turn_l(n):
                L = ZZ[:, n, :]
                b = bank()
                t = T(transposes([(PS[b][:, 0:128], L)]), tL[n], rel[b])
                rel[b] = t = A(lambda e: e.activation(LT[:, n, :], PS[b][:, 0:128], ACT.Copy), t)
                t1 = G(lambda e: e.tensor_tensor(XX[:, n, 0:128], L, c1[:, 9, :], ALU.mult), tL[n])
                t2 = G(lambda e: e.tensor_tensor(XX[:, n, 128:256], LT[:, n, :], c1[:, 3, :], ALU.mult), t)
                t1 = G(lambda e: e.tensor_tensor(XX[:, n, 0:128], ident, XX[:, n, 0:128], ALU.subtract), t1)
                tX[n] = G(lambda e: e.tensor_tensor(XX[:, n, 128:256], ident, XX[:, n, 128:256], ALU.subtract), t2)

            for a, h, i in units:
                n = a * 4 + i
                c = i * 4 + h
                tok = slice(i * 128, i * 128 + 128)
                kT, qT = QKV[:, 4 + h, tok], QKV[:, h, tok]
                b = bank()
                T(mms(PS[b][:, 0:128], [(kT, kT)]), rel[b])
                t = T(mms(PS[b][:, 128:256], [(kT, qT)]))
                L = ZZ[:, n, :]
                tL[n] = V(lambda e: e.scalar_tensor_tensor(L, PS[b][:, 0:128], bet[:, c:c + 1], EE[:, n, 0:128],
                                                        ALU.mult, ALU.mult), t, tE[n])
                rel[b] = V(lambda e: e.tensor_tensor(AQ[:, n, :], PS[b][:, 128:256], EE[:, n, 128:256], ALU.mult))
                tqd = V(lambda e: e.tensor_tensor(qT, qT, EE[:, n, 256:384], ALU.mult), t)
                if n:
                    turn_l(n - 1)
            turn_l(7)
            for _ in range(3):
                next(filler, None)
            for lv in range(1, 6):
                mk = c1[:, 3 + lv, :]
                tb = {}
                for n in range(8):
                    gm = GM[:, n % 4, 0:128]
                    t = G(lambda e: e.tensor_tensor(gm, LT[:, n, :], mk, ALU.mult), gf[n % 4])
                    b = bank()
                    gf[n % 4] = t = T(mms(PS[b][:, 0:128], [(gm, XX[:, n, 0:128])]), t, tX[n], rel[b])
                    rel[b] = tb[n] = A(lambda e: e.activation(ZZ[:, n, :], PS[b][:, 0:128], ACT.Copy), t)
                for n in range(8):
                    b = bank()
                    T(mms(PS[b][:, 0:128], [(XX[:, n, 128:256], ZZ[:, n, :])]), tb[n], rel[b])
                    t = T(mms(PS[b][:, 128:256], [(ZZ[:, n, :], XX[:, n, 128:256])]))
                    rel[b] = tX[n] = V(lambda e: e.tensor_tensor(XX[:, n, :], XX[:, n, :], PS[b][:, 0:256],
                                                                 ALU.subtract), t)
            tU = {}
            for n in range(8):
                XT = XX[:, n, 128:256]
                b = bank()
                T(mms(PS[b][:, 0:128], [(XT, VB[:, n, :])]), tX[n], rel[b])
                t = T(mms(PS[b][:, 128:256], [(KB[:, n, :], XT)]))
                V(lambda e: e.tensor_copy(UU[:, n, :], PS[b][:, 0:128]), t)
                rel[b] = tU[n] = V(lambda e: e.tensor_copy(WT[:, n, :], PS[b][:, 128:256]))
            barrier()
            VN = alloc(2, 128, at=sub + 8 * 128 * 3 + 8 * 384)
            OB = [PS[6], PS[7]]
            tS, tO, tV, wt_read = [None, None], [None, None], [None, None], [None, None]
            kd_read = [[None, None], [None, None]]
            for i in range(8):
                n_, hf = i // 2, 64 * (i % 2)
                hs = slice(hf, hf + 64)
                for a, h in enumerate(heads):
                    n, vn, sb = a * 4 + n_, VN[:, a, :], ST[:, a, :]
                    if i:
                        t = T(mms(PS[a][:, 0:128], [(WT[:, n, :], sb)]), tS[a], wt_read[a])
                        tV[a] = wt_read[a] = V(lambda e: e.tensor_tensor(vn[hs, :], UU[hs, n, :], PS[a][hs, 0:128],
                                                                         ALU.subtract), t, tO[a])
                    else:
                        tV[a] = V(lambda e: e.tensor_copy(vn[hs, :], UU[hs, n, :]))
                next(filler, None)
                for a, h in enumerate(heads):
                    n, vn, sb = a * 4 + n_, VN[:, a, :], ST[:, a, :]
                    q = QKV[:, h, i * 64:i * 64 + 64]
                    ko = PS[a][:, 128 + 128 * (i % 2):256 + 128 * (i % 2)]
                    t = T(mms(ko, [(KD[hs, n, :], vn[hs, :])]), tV[a], kd_read[a][i % 2])
                    pairs = ([(sb, q)] if i else []) + [(vn[hs, :], AQ[hs, n, hs])]
                    tO[a] = T(mms(OB[a][:, i * 64:i * 64 + 64], pairs))
                    if i:
                        dcol = EE[:, n, 256 + hf + 63:256 + hf + 64]
                        t = V(lambda e: e.scalar_tensor_tensor(sb, sb, dcol, ko, ALU.mult, ALU.add), t, tO[a])
                    else:
                        t = V(lambda e: e.tensor_copy(sb, ko), t)
                    kd_read[a][i % 2] = tS[a] = t
                next(filler, None)
            for _ in range(2 if hp == 0 else 99):
                next(filler, None)
            rel[0:2] = tS
            rel[6], rel[7] = None, None
            tmp = alloc(2, 512, at=sub)
            rs = alloc(2, 512, at=sub + 1024)
            osb = alloc(2, 512, at=sub + 2048)
            for a, h in enumerate(heads):
                te = A(lambda e: e.activation(osb[:, a, :], OB[a], ACT.Copy), tO[a], tO[0], tO[1])
                t = A(lambda e: e.activation(tmp[:, a, :], OB[a], ACT.Square))
                rel[6 + a] = t
                b = a
                t = T(mms(PS[b], [(ones, tmp[:, a, :])]), t, rel[b])
                t, rel[b] = rsqrt(rs[:, a, :], PS[b], 1.0 / 128, t)
                t = V(lambda e: e.scalar_tensor_tensor(osb[:, a, :], osb[:, a, :], VF[:, r_dn:r_dn + 1], rs[:, a, :],
                                                       ALU.mult, ALU.mult), t, te)
                V(lambda e: e.tensor_tensor(MIX[:, h, :], osb[:, a, :], ZT[:, h, :], ALU.mult), t)
            barrier()
        dump("mixT", MIX, V.last())
        if stop == "mix":
            return fin()

        banks[:] = list(range(8))
        X = alloc(4, 1024, at=WORDS - 4096)
        tx = dsem("x_again")(G, X, D["x"][0].rearrange("(t p) d -> p t d", p=128), added, stored)

        top[0] = mark
        GR = alloc(1024)
        TM = alloc(2, 512)
        dg = dsem("gate")
        tg = dg(G, GR, MOD[2048:3072].rearrange("(a n) -> a n", a=1).partition_broadcast(128), everyone())

        def project(src, tcs, x_of, gate_of, TM, *deps, after=None):
            freed, done = [None, None], []
            for c in range(2):
                s, w, tw = W.take()
                w = w.rearrange("p (k n) -> p k n", n=512)
                for i in tcs:
                    b = bank()
                    t = T(mms(PS[b], [(src[:, k, i * 128:i * 128 + 128], w[:, k, :]) for k in range(8)]), tw, rel[b], *deps)
                    u = i % 2
                    gr = gate_of(i)[:, c * 512:c * 512 + 512]
                    xo = x_of(i)[:, c * 512:c * 512 + 512]
                    rel[b] = tt = V(lambda e: e.tensor_tensor(TM[:, u, :], PS[b], gr, ALU.mult), t, freed[u])
                    freed[u] = V(lambda e: e.tensor_tensor(xo, xo, TM[:, u, :], ALU.add), tt)
                    done.append(freed[u])
                    if c and after:
                        after(i, freed[u])
                W.give(s, t)
            return done[len(tcs):]

        vrows = alloc(2, 128)
        tvr = [dsem(f"bf2{l}")(G, vrows[0:48, l, :], MOD2[l].rearrange("r (a p) -> (r a) p", p=128), stored)
               for l in range(2)]

        def later_rows():
            for l in range(2):
                b = bank()
                t = T(transposes([(PS[b][:, 0:48], vrows[0:48, l, :])]), tvr[l], rel[b])
                rel[b] = V(lambda e: e.tensor_copy(mod2F[:, l, :], PS[b][:, 0:48]), t)

        A2, B2, N2 = alloc(1024), alloc(1024), alloc(1024)
        H2 = alloc(4, 1024)
        H2T = alloc(8, 512)
        c2 = alloc(128 + 128 + 32 + NXB * 32 + 4)
        wr = alloc(8, 32)
        brt = alloc(32)
        assert top[0] <= WORDS - 4096
        dr = dsem("rt")
        row = lambda a: a.rearrange("(a n) -> a n", a=1).partition_broadcast(128)
        dr(G, A2, row(MOD[4096:5120]))
        dr(G, B2, row(MOD[3072:4096]))
        dr(G, N2, D["norm2_w"].partition_broadcast(128))
        dr(G, c2, D["cst2"])
        dr(G, wr, kp(D["w_router"][0]))
        tr = dr(G, brt, D["b_router"].partition_broadcast(128))
        ta = V(lambda e: e.scalar_tensor_tensor(A2, A2, 1.0, N2, ALU.add, ALU.mult), tr)
        LGT = rout
        V8 = alloc(4, 8)
        I8 = alloc(4, 8, dt=U32)
        I8f = alloc(4, 8)
        OH = alloc(16, 32)
        dh = dsem("h2")
        h2_done, top_done = [], []

        def h2_rows(i, t):
            st = small[:, 8 + i:9 + i]
            t = A(lambda e: e.activation(H2[:, i, :], X[:, i, :], ACT.Square, accum_out=st), t)
            t, _ = rsqrt(st, st, 1.0 / 1024, t)
            t = V(lambda e: e.scalar_tensor_tensor(H2[:, i, :], X[:, i, :], st, A2, ALU.mult, ALU.mult), t, ta)
            t = V(lambda e: e.tensor_tensor(H2[:, i, :], H2[:, i, :], B2, ALU.add), t)
            h2_done.append(t)
            return dh(G, H2D[i * 128:i * 128 + 128, :], H2[:, i, :], t)

        def h2_logits(i):
            copied = []
            for g in range(2):
                b = bank()
                t = T(transposes([(PS[b][:, q * 128:q * 128 + 128], H2[:, i, (4 * g + q) * 128:(4 * g + q + 1) * 128])
                                  for q in range(4)]), h2_done[i], rel[b])
                rel[b] = evac(H2T[:, 4 * g:4 * g + 4, i * 128:i * 128 + 128], PS[b].rearrange("p (k n) -> p k n", n=128), t)
                copied.append(rel[b])
            b = bank()
            t = T(mms(PS[b][:, 0:32], [(H2T[:, k, i * 128:i * 128 + 128], wr[:, k, :]) for k in range(8)]), copied, tr, rel[b])
            rel[b] = t = V(lambda e: e.tensor_tensor(LGT[:, i, :], PS[b][:, 0:32], brt, ALU.add), t)
            t = V(lambda e: e.max(V8[:, i, :], LGT[:, i, :]), t)
            t = V(lambda e: e.max_index(I8[:, i, :], V8[:, i, :], LGT[:, i, :]), t)
            t = V(lambda e: e.tensor_copy(I8f[:, i, :], I8[:, i, :]), t)
            for k in range(4):
                top_done.append(V(lambda e: e.tensor_scalar(OH[:, i * 4 + k, :], c2[:, 128:160], I8f[:, i, k:k + 1], None,
                                                            ALU.is_equal), t, tr))

        def router_between(i, t):
            h2_stored.append(h2_rows(i, t))
            if i:
                h2_logits(i - 1)

        h2_stored = []
        t = project(MIX, range(4), lambda i: X[:, i, :], lambda i: GR, TM, tg, tx, after=router_between)
        dump("x1", X, t)
        if stop == "x1":
            barrier(h2_stored[-1])
            return fin()
        h2_logits(3)
        td, to = h2_stored[-1], top_done
        later_rows()
        U_, I128 = c2[:, 0:128], c2[:, 128:256]
        B0 = c2[:, 256:288]
        JJ = c2[:, 288:288 + NXB * 32].rearrange("p (a b) -> p a b", b=32)
        TID = c2[:, 288 + NXB * 32:292 + NXB * 32]
        dump("logits", LGT, top_done)
        MM = alloc(4, 32)
        POS = alloc(4, 32)
        CN, NX, CS, BD1 = alloc(32), alloc(32), alloc(32), alloc(32)
        SL = alloc(4, 32)
        T5 = alloc(NXB, 32)
        DF = alloc(16)
        DI = alloc(2, 16, dt=I32)
        DIF = alloc(2, 16)
        gs = alloc(16)
        O4 = OH.rearrange("p (i k) e -> p i k e", k=4)
        t = V(lambda e: e.tensor_tensor(MM, O4[:, :, 0, :], O4[:, :, 1, :], ALU.add), to)
        t = V(lambda e: e.tensor_tensor(MM, MM, O4[:, :, 2, :], ALU.add), t)
        tmk = V(lambda e: e.tensor_tensor(MM, MM, O4[:, :, 3, :], ALU.add), t)
        b = bank()
        for i in range(4):
            t = T(mms(PS[b][:, i * 32:i * 32 + 32], [(U_, MM[:, i, :])] + [(ones, MM[:, q, :]) for q in range(i)]), tmk, rel[b])
        t = T(mms(PS[b][:, 128:160], [(ones, MM[:, q, :]) for q in range(4)]))
        V(lambda e: e.tensor_copy(POS, PS[b][:, 0:128].rearrange("p (a b) -> p a b", b=32)), t)
        rel[b] = t = V(lambda e: e.tensor_copy(CN, PS[b][:, 128:160]))
        t = V(lambda e: e.tensor_scalar(NX, CN, 128.0, None, ALU.is_gt), t)
        t = V(lambda e: e.scalar_tensor_tensor(NX, CN, 256.0, NX, ALU.is_gt, ALU.add), t)
        t = V(lambda e: e.scalar_tensor_tensor(NX, CN, 384.0, NX, ALU.is_gt, ALU.add), t)
        t = V(lambda e: e.tensor_tensor_scan(CS, ones[:, 0:32], NX, 0.0, ALU.mult, ALU.add), t)
        t1 = V(lambda e: e.tensor_tensor(BD1, CS, NX, ALU.subtract), t)
        t1 = V(lambda e: e.tensor_scalar(BD1, BD1, 128.0, 128.0 * (NEXP - 1), ALU.mult, ALU.add), t1)
        t1 = V(lambda e: e.tensor_tensor(BD1, BD1, B0, ALU.subtract), t1)
        bc = lambda v, n: v.unsqueeze(1).to_broadcast([128, n, 32])
        t5 = V(lambda e: e.tensor_tensor(T5, bc(CS, NXB), JJ, ALU.is_le), t)
        t5 = V(lambda e: e.tensor_reduce(gs[:, 0:NXB], T5, AX.X, ALU.add), t5)
        t5 = V(lambda e: e.tensor_scalar(gs[:, 0:NXB], gs[:, 0:NXB], float(NEXP - 1), None, ALU.min), t5)
        V(lambda e: e.tensor_copy(XE[:, 0:NXB], gs[:, 0:NXB]), t5)
        txe = V(lambda e: e.tensor_copy(XE[:, NXB:NXB + 1], CS[:, 31:32]))
        t = V(lambda e: e.tensor_scalar(SL, POS, 128.0, None, ALU.is_ge), t1)
        t = V(lambda e: e.tensor_tensor(SL, SL, bc(BD1, 4), ALU.mult), t)
        t = V(lambda e: e.tensor_tensor(SL, SL, POS, ALU.add), t)
        ts = V(lambda e: e.tensor_tensor(SL, SL, bc(B0, 4), ALU.add), t)
        for i in range(4):
            t = V(lambda e: e.tensor_tensor(O4[:, i, :, :], O4[:, i, :, :], bc(SL[:, i, :], 4), ALU.mult), ts)
        t = V(lambda e: e.tensor_reduce(DF, OH, AX.X, ALU.add), t)
        td1 = V(lambda e: e.tensor_copy(DEST, DF), t)
        V(lambda e: e.tensor_scalar(DI[:, 0, :], DEST, 7, None, ALU.logical_shift_right), td1)
        t = V(lambda e: e.tensor_scalar(DI[:, 1, :], DEST, 127, None, ALU.bitwise_and))
        tdf = V(lambda e: e.tensor_copy(DIF, DI), t)
        OP = alloc(2, 128)
        OBK = alloc(2, 48)
        opf = [None, None]
        b = bank()
        rb = rel[b]
        for n in range(16):
            u = n % 2
            V(lambda e: e.tensor_scalar(OP[:, u, :], I128, DIF[:, 1, n:n + 1], None, ALU.is_equal), tdf, opf[u])
            t = V(lambda e: e.tensor_scalar(OBK[:, u, 0:NBLK], I128[:, 0:NBLK], DIF[:, 0, n:n + 1],
                                            TID[:, n // 4:n // 4 + 1], ALU.is_equal, ALU.mult))
            T.wait(t, rb)
            opf[u] = T(lambda e: e.matmul(PS[b][:, 0:NBLK], OP[:, u, :], OBK[:, u, 0:NBLK], start=(n == 0), stop=(n == 15)))
        rel[b] = trow = V(lambda e: e.tensor_copy(ROW[:, 0:NBLK], PS[b][:, 0:NBLK]), opf[1])
        gf_ = gs
        for i in range(4):
            t = V(lambda e: e.tensor_scalar(gs[:, i:i + 1], V8[:, i, 0:1], -1.0, None, ALU.mult), V.last())
            t = A(lambda e: e.activation(GT[:, i, :], V8[:, i, 0:4], ACT.Exp, bias=gs[:, i:i + 1], accum_out=gs[:, 4 + i:5 + i]), t)
            t = V(lambda e: e.reciprocal(gs[:, 8 + i:9 + i], gs[:, 4 + i:5 + i]), t)
            tgt = V(lambda e: e.tensor_scalar(GT[:, i, :], GT[:, i, :], gs[:, 8 + i:9 + i], None, ALU.mult), t)
        dump("gt", GT, tgt)
        dump("dest", DEST, tgt)
        dump("row", ROW[:, 0:NBLK], tgt)
        dump("xe", XE, tgt)
        barrier(td, tz_)
        if stop == "route":
            return fin()

        top[0] = base
        XG, XGT = alloc(2, 1024), alloc(2, 1024)
        T1, SG, T2 = alloc(1024), alloc(1024), alloc(1024)
        ACTV, ACTT = alloc(1024), alloc(1024)
        Y = alloc(2, 1024)
        BU = alloc(NBU * 1536).bitcast(BF16).rearrange("p (a n) -> p a n", n=3072)
        assert top[0] <= WORDS - 4096

        def expert_steps(w, gather_sem, bias_sem, store_sem):
            gathered, biased, x_turned, x_copied, up_done, glu_read, lin_read = [], [], [], [], [], [], []
            act_done, a_turned, a_copied, down_done, y_copied, stored = [], [], [], [], [], []

            def before(steps, i):
                return steps[i] if i >= 0 else None

            def gather(i, col):
                gathered.append(gather_sem[i % 2](G, None, None, before(x_turned, 2 * (i - 2) + 1), f=lambda e: e.indirect_dma_start(
                    XG[:, i % 2, :], None, H2D, bass.IndirectOffsetOnAxis(ap=ROW[:, col:col + 1], axis=0))))

            def biases(i, rows):
                biased.append(bias_sem[i % NBU](G, BU[0:3, i % NBU, :], rows, before(down_done, i - NBU)))

            def turn_x(i, hh):
                u, n = i % 2, 2 * i + hh
                x_turned.append(T(transposes([(PS[4][:, q * 128:q * 128 + 128], XG[:, u, (hh * 4 + q) * 128:(hh * 4 + q + 1) * 128])
                                              for q in range(4)]), gathered[i], before(x_copied, n - 1)))
                x_copied.append(V(lambda e: e.tensor_copy(XGT[:, u, hh * 512:hh * 512 + 512], PS[4]), x_turned[n],
                                  before(up_done, i - 2)))

            def up(i, between):
                u = i % 2
                T.wait(biased[i], before(glu_read, i - 1), before(lin_read, i - 1))

                def bias_rows(e):
                    for n in range(4):
                        r = e.matmul(PS[n], ones3[0:3, :], BU[0:3, i % NBU, n * 512:n * 512 + 512], start=True, stop=False)
                    return r
                T(bias_rows)
                for q in range(4):
                    s, wt, loaded = w.take()
                    wt = wt.rearrange("p (k n) -> p k n", n=2048)

                    def products(e):
                        for kk in range(2):
                            k = 2 * q + kk
                            for n in range(4):
                                r = e.matmul(PS[n], XGT[:, u, k * 128:k * 128 + 128], wt[:, kk, n * 512:n * 512 + 512],
                                             start=False, stop=(k == 7))
                        return r
                    t = T(products, loaded, x_copied[2 * i + q // 2])
                    w.give(s, t)
                    between(q)
                up_done.append(t)
                for n in range(2):
                    c = slice(n * 512, n * 512 + 512)
                    ta = V(lambda e: e.tensor_scalar(T1[:, c], PS[n], 7.0, None, ALU.min), up_done[i], before(act_done, i - 1))
                    sg = A(lambda e: e.activation(SG[:, c], T1[:, c], ACT.Sigmoid, scale=1.702), ta, before(act_done, i - 1))
                glu_read.append(ta)
                for n in range(2):
                    c = slice(n * 512, n * 512 + 512)
                    tb = V(lambda e: e.tensor_scalar(T2[:, c], PS[2 + n], 7.0, -7.0, ALU.min, ALU.max), up_done[i])
                lin_read.append(tb)
                tb = V(lambda e: e.scalar_tensor_tensor(T2, T2, 1.0, T1, ALU.add, ALU.mult), tb, ta)
                act_done.append(V(lambda e: e.tensor_tensor(ACTV, T2, SG, ALU.mult), tb, sg, before(a_turned, 2 * (i - 1) + 1)))

            def turn_a(i, hh):
                n = 2 * i + hh
                a_turned.append(T(transposes([(PS[5][:, q * 128:q * 128 + 128], ACTV[:, (hh * 4 + q) * 128:(hh * 4 + q + 1) * 128])
                                              for q in range(4)]), act_done[i], before(a_copied, n - 1)))
                a_copied.append(V(lambda e: e.tensor_copy(ACTT[:, hh * 512:hh * 512 + 512], PS[5]), a_turned[n],
                                  before(down_done, i - 1)))

            def down(i, col):
                u = i % 2
                T.wait(before(y_copied, i - 1))

                def bias_rows(e):
                    for n in range(2):
                        r = e.matmul(PS[6 + n], ones3[0:3, :], BU[0:3, i % NBU, 2048 + n * 512:2560 + n * 512], start=True, stop=False)
                    return r
                T(bias_rows)
                for q in range(2):
                    s, wt, loaded = w.take()
                    wt = wt.rearrange("p (k n) -> p k n", n=1024)

                    def products(e):
                        for kk in range(4):
                            k = 4 * q + kk
                            for n in range(2):
                                r = e.matmul(PS[6 + n], ACTT[:, k * 128:k * 128 + 128], wt[:, kk, n * 512:n * 512 + 512],
                                             start=False, stop=(k == 7))
                        return r
                    t = T(products, loaded, a_copied[2 * i + q])
                    w.give(s, t)
                down_done.append(t)
                for n in range(2):
                    ty = A(lambda e: e.activation(Y[:, u, n * 512:n * 512 + 512], PS[6 + n], ACT.Copy), t, before(stored, i - 2))
                y_copied.append(ty)
                stored.append(store_sem[u](G, YD[col * 128:col * 128 + 128, :], Y[:, u, :], ty))
                return stored[i]

            return gather, biases, turn_x, up, turn_a, down

        def expert_sems(tag):
            return [[dsem(f"{n}{tag}{i}") for i in range(c)] for n, c in (("gather", 2), ("bias", NBU), ("store", 2))]

        gather, biases, turn_x, up, turn_a, down = expert_steps(W, *expert_sems("a"))
        for i in range(NBU):
            biases(i, BIASD[i])
        for i in range(2):
            gather(i, i)
        turn_x(0, 0)
        turn_x(0, 1)
        stored = [None, None]
        for i in range(NEXP):
            def between(q):
                if q < 2 and i:
                    turn_a(i - 1, q)
                if q >= 2 and i + 1 < NEXP:
                    turn_x(i + 1, q - 2)
            up(i, between)
            if i + 2 < NEXP:
                gather(i + 2, i + 2)
            if i:
                stored[(i - 1) % 2] = down(i - 1, i - 1)
                if i - 1 + NBU < NEXP:
                    biases(i - 1 + NBU, BIASD[i - 1 + NBU])
        turn_a(NEXP - 1, 0)
        turn_a(NEXP - 1, 1)
        stored[1] = down(NEXP - 1, NEXP - 1)
        barrier(stored)

        main = [(e.sem, e.n, dict(e.seen)) for e in EN]
        S.wait(txe)
        slots = list(W.free)
        xsem = [sem("x_" + n) for n in names]
        loads[:] = []
        proto = Stream("x")
        extra_sems = expert_sems("x")
        counted = [proto.sems] + extra_sems

        def extras(E):
            for e, q in zip(EN, xsem):
                e.sem, e.n, e.on, e.seen = q, 0, e is E, {}
            loads[:] = []
            for grp in counted:
                for q in grp:
                    q.n = 0
            proto.issued = proto.taken = 0
            proto.free = list(slots)
            gather, biases, turn_x, up, turn_a, down = expert_steps(proto, *extra_sems)
            eng, ends = E.eng, []
            cnt = eng.value_load(XE[0:1, NXB:NXB + 1], min_val=0, max_val=NXB)
            for j in range(NXB):
                with eng.If(cnt > j):
                    if E is S or E is G:
                        ex = eng.value_load(XE[0:1, j:j + 1], min_val=0, max_val=NEXP - 1)
                        w1 = D["w_up"][0, bass.ds(ex, 1)].rearrange("a k n -> (a k) n")
                        w2 = D["w_down"][0, bass.ds(ex, 1)].rearrange("a k n -> (a k) n")
                        b3 = BIASD[bass.ds(ex, 1)].rearrange("a k n -> (a k) n")
                    else:
                        w1, w2, b3 = D["w_up"][0, 0], D["w_down"][0, 0], BIASD[0]
                    loads.extend(up_loads(w1) + down_loads(w2))
                    gather(j, NEXP + j)
                    biases(j, b3)
                    while proto.issued < proto.taken + NSLOT and proto.issued < len(loads):
                        proto.issue()
                    turn_x(j, 0)
                    turn_x(j, 1)
                    up(j, lambda q: None)
                    turn_a(j, 0)
                    turn_a(j, 1)
                    ends.append(([(q, e.n) for e, q in zip(EN[:4], xsem)], down(j, NEXP + j)))
            for j in range(NXB):
                with eng.If(cnt == j + 1):
                    E.wait(*ends[j])

        with nc.Block() as block:
            @block.tensor
            def _(e):
                extras(T)

            @block.vector
            def _(e):
                extras(V)

            @block.scalar
            def _(e):
                extras(A)

            @block.gpsimd
            def _(e):
                extras(G)

            @block.sync
            def _(e):
                extras(S)
        for e, (q, n, seen) in zip(EN, main):
            e.sem, e.n, e.seen, e.on = q, n, seen, True
        rel[:] = [None] * 8
        loads[:] = later
        W = Stream("b", 3)
        for _ in range(3):
            W.issue()

        top[0] = base
        XC = alloc(2, 1024)
        mark = top[0]
        c3 = alloc(640)
        GTE = alloc(8, 768)
        CQ = alloc(4, 768)
        KR = alloc(6, 32)
        GKV = alloc(6, 256)
        GQ = alloc(6, 512)
        HT = alloc(8, 768)
        tail = top[0]
        ACC = mem[:, mark + 640:mark + 640 + 2048].rearrange("p (a n) -> p a n", n=1024)
        GR = alloc(1024)
        XN = alloc(2, 1024)
        rt = alloc(1024)
        assert top[0] <= WORDS - 4096
        sb = small[:, 32:48]
        stats = rout.rearrange("p a b -> p (a b)")[:, 0:64]
        spare = ring[:, 3 * 4096:5 * 4096]
        YG = spare.rearrange("p (a n) -> p a n", n=1024)
        d3 = dsem("late")
        dgr = dsem("gate2")
        txc = d3(A, XC, D["ctx_2"][0].rearrange("(t p) d -> p t d", p=128))
        tgr = dgr(A, GR, MOD[5120:6144].rearrange("(a n) -> a n", a=1).partition_broadcast(128))
        dc3 = dsem("cst3")
        tc3 = dc3(A, c3, D["cst3"])
        dyg = [dsem(f"yg{k}") for k in range(8)]
        yg_read, acc_read = [None] * 8, [None] * 2

        def combine(i):
            acc = ACC[:, i % 2, :]
            for k in range(4):
                n, u = i * 4 + k, i % 2 * 4 + k
                ty = dyg[u](G, None, None, yg_read[u], f=lambda e: e.indirect_dma_start(
                    YG[:, u, :], None, YD, bass.IndirectOffsetOnAxis(ap=DEST[:, n:n + 1], axis=0)))
                if k == 0:
                    t = V(lambda e: e.tensor_scalar(acc, YG[:, u, :], GT[:, i, 0:1], None, ALU.mult), ty, acc_read[i % 2])
                else:
                    t = V(lambda e: e.scalar_tensor_tensor(acc, YG[:, u, :], GT[:, i, k:k + 1], acc, ALU.mult, ALU.add), ty, t)
                yg_read[u] = t
            t = V(lambda e: e.tensor_tensor(acc, acc, GR, ALU.mult), t, tgr)
            acc_read[i % 2] = V(lambda e: e.tensor_tensor(X[:, i, :], X[:, i, :], acc, ALU.add), t)
            return acc_read[i % 2]

        xrow = lambda i: X[:, i, :] if i < 4 else XC[:, i - 4, :]
        xn_read = [None, None]

        def adaln_rows(i, n, tx):
            st = small[:, 8 + i:9 + i]
            xn = XN[:, n % 2, :]
            t = A(lambda e: e.activation(xn, xrow(i), ACT.Square, accum_out=st), tx, xn_read[n % 2])
            t, _ = rsqrt(st, st, 1.0 / 1024, t)
            return V(lambda e: e.tensor_scalar(xn, xrow(i), st, None, ALU.mult), t)

        def adaln_turn(l, i, n, HT, t):
            xn = XN[:, n % 2, :]
            r = 0 if i < 4 else 1
            mul, add = mp[:, r * 8:r * 8 + 8], mod2F[:, l, r * 24:r * 24 + 8]
            done = []
            for g in range(2):
                b = bank()
                xn_read[n % 2] = t1 = T(transposes([(PS[b][:, q * 128:q * 128 + 128], xn[:, (4 * g + q) * 128:(4 * g + q + 1) * 128])
                                                    for q in range(4)]), t, rel[b])
                rel[b] = []
                for q in range(4):
                    k = 4 * g + q
                    o, p = HT[:, k, i * 128:i * 128 + 128], PS[b][:, q * 128:q * 128 + 128]
                    if g:
                        t1_ = V(lambda e: e.tensor_scalar(o, p, mul[:, k:k + 1], add[:, k:k + 1], ALU.mult, ALU.add), t1, tmp_)
                    else:
                        t1_ = A(lambda e: e.activation(o, p, ACT.Identity, bias=add[:, k:k + 1], scale=mul[:, k:k + 1]), t1, tmp_)
                    rel[b].append(t1_)
                done += rel[b]
            return done

        def scales(l):
            m2 = mod2F[:, l, :].rearrange("p (r a) -> p r a", a=24)
            return V(lambda e: e.tensor_scalar(mp.rearrange("p (r a) -> p r a", a=8), m2[:, :, 8:16], 1.0, None, ALU.add))

        mp = small[:, 16:32]
        tmp_ = scales(0)
        def gemm_t(HT, w, n0, n, i, dst, *deps, func=ACT.Copy):
            b = bank()
            t = T(mms(PS[b][:, 0:n], [(HT[:, k, i * 128:i * 128 + 128], w[:, k, n0:n0 + n]) for k in range(8)]),
                  rel[b], *deps)
            rel[b] = A(lambda e: e.activation(dst, PS[b][:, 0:n], func), t)
            return rel[b], t
        def run(steps):
            while True:
                try:
                    next(steps)
                except StopIteration as end:
                    return end.value

        def head_sums(x, H, d, sq, st, *deps):
            x3 = x.rearrange("p (h d) -> p h d", d=d)
            s3 = sq[:, 0:H * d].rearrange("p (h d) -> p h d", d=d)
            t = V(lambda e: e.tensor_tensor(s3, x3, x3, ALU.mult), *deps)
            return V(lambda e: e.tensor_reduce(st, s3, AX.X, ALU.add), t)

        def head_scale(x, H, d, gain, scale, st, *deps):
            x3 = x.rearrange("p (h d) -> p h d", d=d)
            t = V(lambda e: e.tensor_tensor(x3, x3, st.unsqueeze(2).to_broadcast([128, H, d]), ALU.mult), *deps)
            yield
            return V(lambda e: e.scalar_tensor_tensor(x3, x3, scale, gain.unsqueeze(1).to_broadcast([128, H, d]),
                                                      ALU.mult, ALU.mult), t)

        def rope(x, H, d, off, r, i, big, tmp, *deps):
            o, n = (0, 2 * r) if big else (256, 2 * r)
            x3 = x.rearrange("p (h d) -> p h d", d=d)[:, :, off:off + 4 * r].rearrange("p h (a m) -> p h a m", m=n)
            x1, x2 = x3[:, :, :, 0:r], x3[:, :, :, r:n]
            bc = lambda c: c.rearrange("p (a r) -> p a r", r=r).unsqueeze(1).to_broadcast([128, H, 2, r])
            cs, sn = bc(c3[:, o + i * n:o + i * n + n]), bc(c3[:, o + 4 * n + i * n:o + 4 * n + i * n + n])
            m = 2 * H * r
            ta, tb, tc, td = [tmp[:, q * m:(q + 1) * m].rearrange("p (h a r) -> p h a r", a=2, r=r) for q in range(4)]
            V(lambda e: e.tensor_tensor(ta, x1, cs, ALU.mult), *deps)
            V(lambda e: e.tensor_tensor(tb, x2, sn, ALU.mult))
            yield
            V(lambda e: e.tensor_tensor(tc, x2, cs, ALU.mult))
            t = V(lambda e: e.tensor_tensor(td, x1, sn, ALU.mult))
            yield
            V(lambda e: e.tensor_tensor(x1, ta, tb, ALU.subtract), t)
            return V(lambda e: e.tensor_tensor(x2, tc, td, ALU.add), t)

        def pairs_t(src, H, dst, tcs, *deps):
            for h in range(H // 2):
                for g in range(0, len(tcs), 4):
                    part = list(tcs)[g:g + 4]
                    b = bank()
                    t = T(transposes([(PS[b][:, q * 128:q * 128 + 128], src(i)[:, h * 128:h * 128 + 128])
                                      for q, i in enumerate(part)]), rel[b], *deps)
                    lo, n = part[0] * 128, len(part) * 128
                    rel[b] = A(lambda e: e.activation(dst[:, h, lo:lo + n], PS[b][:, 0:n], ACT.Copy), t, *deps)

        def twice_t(src, H, dst, tcs, *deps):
            for h in range(H):
                for g in range(0, len(tcs), 4):
                    part = list(tcs)[g:g + 4]
                    b = bank()
                    t = T(transposes([(PS[b][0:64, q * 128:q * 128 + 128], src(i)[:, h * 64:h * 64 + 64])
                                      for q, i in enumerate(part)]), rel[b], *deps)
                    lo, n = part[0] * 128, len(part) * 128
                    A(lambda e: e.activation(dst[0:64, h, lo:lo + n], PS[b][0:64, 0:n], ACT.Copy), t, *deps)
                    rel[b] = A(lambda e: e.activation(dst[64:128, h, lo:lo + n], PS[b][0:64, 0:n], ACT.Copy), t)

        def attention(groups, PB, filler=iter(()), rate=1):
            units, scored, exped, scaled, turned, copied = [], [], [], [], [], []
            valued, taken, todo = [], [], []
            for g, (us, buf, vals, cols_, out_) in enumerate(groups):
                units += [(g, n == len(us) - 1) + u for n, u in enumerate(us)]
            sunk = []

            def before(steps, x):
                return steps[x] if x >= 0 else None

            def score(x):
                g, end, q, ks, lo, n, masks, sink, c, places = units[x]
                p = PP[x % 2]
                T.wait(before(exped, x - 2))
                for k, at in ks:
                    t = T(lambda e: e.matmul(p[:, at:at + k.shape[1]], q, k, start=True, stop=True))
                for m, at in masks:
                    t = V(lambda e: e.tensor_tensor(p[:, at:at + 128], p[:, at:at + 128], m, ALU.add), t)
                scored.append(t)

            def soften(x):
                g, end, q, ks, lo, n, masks, sink, c, places = units[x]
                u = x % 2
                p = PP[u]
                m = sb[:, u * 8:u * 8 + 8]
                t = V(lambda e: e.tensor_reduce(m[:, 0:1], p[:, lo:lo + n], AX.X, ALU.max), scored[x], before(scaled, x - 2))
                if sink is not None:
                    t = V(lambda e: e.tensor_scalar(m[:, 0:1], m[:, 0:1], sink, -1.0, ALU.max, ALU.mult), t)
                else:
                    t = V(lambda e: e.tensor_scalar(m[:, 0:1], m[:, 0:1], -1.0, None, ALU.mult), t)
                exped.append(A(lambda e: e.activation(PB[:, u, 0:n], p[:, lo:lo + n], ACT.Exp, bias=m[:, 0:1],
                                                      accum_out=m[:, 1:2]), t, before(turned, x - 2)))
                if sink is not None:
                    sunk.append(A(lambda e: e.activation(m[:, 2:3], m[:, 0:1], ACT.Exp, bias=sink), t))

            def scale(x):
                g, end, q, ks, lo, n, masks, sink, c, places = units[x]
                u = x % 2
                m = sb[:, u * 8:u * 8 + 8]
                t = exped[x]
                if sink is not None:
                    t = V(lambda e: e.tensor_tensor(m[:, 1:2], m[:, 1:2], m[:, 2:3], ALU.add), t, sunk[x])
                t = V(lambda e: e.reciprocal(m[:, 3:4], m[:, 1:2]), t)
                scaled.append(V(lambda e: e.tensor_scalar(PB[:, u, 0:n], PB[:, u, 0:n], m[:, 3:4], None, ALU.mult), t))

            def turn(x):
                g, end, q, ks, lo, n, masks, sink, c, places = units[x]
                u, pt, buf = x % 2, PP[2], groups[g][1]
                turned.append(T(transposes([(pt[:, k * 128:k * 128 + 128], PB[:, u, k * 128:k * 128 + 128])
                                            for k in range(n // 128)]), scaled[x], before(copied, x - 1)))
                for k0, k1, to in places:
                    t = A(lambda e: e.activation(buf[:, to:to + k1 - k0, c * 128:c * 128 + 128],
                                                 pt[:, k0 * 128:k1 * 128].rearrange("p (k n) -> p k n", n=128), ACT.Copy),
                          turned[x], before(valued, g - 2))
                copied.append(t)
                if end:
                    todo.extend((g, k, v, c0, c1, j, x) for j, (k, v, c0, c1) in enumerate(groups[g][2]))

            def values(count):
                for _ in range(min(count, len(todo))):
                    g, k, v, c0, c1, j, x = todo.pop(0)
                    us, buf, vals, cols_, out_ = groups[g]
                    p0, dst = out_
                    t = T(lambda e: e.matmul(PS[6][p0:p0 + 64, c0:c1], v, buf[:, k, c0:c1], start=(j == 0),
                                             stop=(j == len(vals) - 1)), copied[x], before(taken, g - 1))
                    if j == len(vals) - 1:
                        valued.append(t)
                        taken.append(V(lambda e: e.tensor_tensor(dst, dst, PS[6][p0:p0 + 64, 0:cols_], ALU.mult), t))

            score(0)
            for x in range(len(units)):
                soften(x)
                if x + 1 < len(units):
                    score(x + 1)
                for _ in range(rate):
                    next(filler, None)
                scale(x)
                values(2)
                if x:
                    turn(x - 1)
                for _ in range(rate):
                    next(filler, None)
            turn(len(units) - 1)
            values(len(todo))
            for _ in filler:
                pass
            rel[:] = [None] * 8
            return [taken[-1], valued[-1], copied[-1]]

        x512 = lambda w: w.rearrange("p (k n) -> p k n", n=512)
        tcr = [adaln_rows(4, 0, txc), adaln_rows(5, 1, txc)]
        thc = [adaln_turn(0, 4, 0, HT, tcr[0]), adaln_turn(0, 5, 1, HT, tcr[1])]
        s1, w1, tw1 = W.take()
        s2, w2, tw2 = W.take()
        tgq, tkv = {}, {}

        def gqa_projections(i, th):
            tgq[i], _ = gemm_t(HT, x512(w1), 0, 512, i, GQ[:, i, :], tw1, th)
            gemm_t(HT, x512(w2), 0, 32, i, KR[:, i, :], tw2)
            tkv[i], t = gemm_t(HT, x512(w2), 32, 256, i, GKV[:, i, :])
            return t

        for i in (4, 5):
            gqa_projections(i, thc[i - 4])
        th, t1 = [], adaln_rows(0, 0, combine(0))
        for i in range(4):
            t = t1
            if i < 3:
                t1 = adaln_rows(i + 1, i + 1, combine(i + 1))
            th.append(adaln_turn(0, i, i, HT, t))
        dump("x2", X, V.last())
        if stop == "x2":
            barrier(tgr, txc, tc3)
            return fin()
        for i in range(4):
            t = gqa_projections(i, th[i])
        W.give(s1, t)
        W.give(s2, t)
        th = [th, thc]

        def gqa_sums(i, t):
            t = head_sums(GQ[:, i, :], 8, 64, rt, stats[:, 10 * i:10 * i + 8], tgq[i], t)
            return head_sums(GKV[:, i, 0:128], 2, 64, rt, stats[:, 10 * i + 8:10 * i + 10], tkv[i], t)

        def gqa_norms(i, t):
            st = stats[:, 10 * i:10 * i + 10]
            t = run(head_scale(GQ[:, i, :], 8, 64, gains[:, 192:256], 0.125, st[:, 0:8], t))
            if i < 4:
                t = run(rope(GQ[:, i, :], 8, 64, 0, 16, i, True, rt, t, tc3))
            t = run(head_scale(GKV[:, i, 0:128], 2, 64, gains[:, 256:320], 1.0, st[:, 8:10], t))
            if i < 4:
                t = run(rope(GKV[:, i, 0:128], 2, 64, 0, 16, i, True, rt, t))
            return t

        tn = None
        for i in (4, 5, 0, 1, 2, 3):
            tn = gqa_sums(i, tn)
        tn, _ = rsqrt(stats[:, 0:60], stats[:, 0:60], 1.0 / 64, tn)

        s, w, tw = W.take()
        w = x512(w)
        tn = gqa_norms(4, tn)
        sq, rs = spare[:, 0:1536].rearrange("p (a n) -> p a n", n=768), spare[:, 1536:2304]
        cq_squared = [None] * 4
        for i in range(4):
            for lo, n in ((0, 512), (512, 256)):
                b = bank()
                t = gemm_f(w, i * 128, lambda k: HT[:, k, lo:lo + n], PS[b][:, 0:n], b, tw, th)
                rel[b] = tcq = A(lambda e: e.activation(CQ[:, i, lo:lo + n], PS[b][:, 0:n], ACT.Copy), t)
        W.give(s, t)
        tn = gqa_norms(5, tn)
        tcn, tsum = [], None
        for a in range(2):
            for i in range(2):
                ts = A(lambda e: e.activation(sq[:, i, :], CQ[:, 2 * a + i, :], ACT.Square), tcq, tsum, yg_read)
            g0 = r_cq if a == 0 else r_ck
            for lo, n in ((0, 512), (512, 256)):
                b = bank()
                tsum = T(mms(PS[b][:, 0:n], [(ones, sq[:, i, lo:lo + n]) for i in range(2)]), ts, rel[b])
                t2, rel[b] = rsqrt(rs[:, lo:lo + n], PS[b][:, 0:n], 1.0 / 256, tsum, tcn)
            for i in range(2):
                x = CQ[:, 2 * a + i, :]
                tcn.append(V(lambda e: e.scalar_tensor_tensor(x, x, VF[:, g0 + i:g0 + i + 1], rs, ALU.mult, ALU.mult), t2))
        for c in range(2):
            s, w, tw = W.take()
            w = x512(w)
            for i in range(4):
                for lo, n in ((0, 512), (512, 256)):
                    b = bank()
                    t = gemm_f(w, i * 128, lambda k: HT[:, k, lo:lo + n], PS[b][:, 0:n], b, tw, th, acc_read, yg_read)
                    rel[b] = A(lambda e: e.activation(GTE[:, c * 4 + i, lo:lo + n], PS[b][:, 0:n], ACT.Silu), t)
                if c == 0:
                    tn = gqa_norms(i, tn)
            W.give(s, t)
        dump("gq", GQ, tn)
        R = lambda at, *dims: spare[:, at:at + int(np.prod(dims))].rearrange("p (a n) -> p a n", n=dims[1])
        QT, KT, PTM = R(0, 4, 768), R(3072, 2, 768), R(4608, 6, 512)
        PTC = spare[:, 7680:8192].rearrange("p (k n) -> p k n", n=256)
        gq_ = GQ.rearrange("p a n -> p (a n)")
        PB, LK1 = [gq_[:, a * 1536:a * 1536 + 1536].rearrange("p (a n) -> p a n", n=768) for a in range(2)]
        pairs_t(lambda i: GQ[:, i, :], 8, QT, range(6), tn, tcn)
        twice_t(lambda i: GKV[:, i, 0:128], 2, KT, range(6))
        barrier()
        top[0] = tail - 6144
        LQ, LK, LV = [alloc(4, 768), R(0, 4, 768)], [[alloc(2, 768), alloc(2, 768)], [LK1, R(3072, 2, 768)]], [alloc(6, 256), GKV]
        QA, KA = alloc(2, 384), alloc(2, 384)
        assert top[0] <= tail + 3072
        sl, wl, twl = W.take()
        wq = wl[:, 0:1536].rearrange("p (k n) -> p k n", n=768)
        wkv = wl[:, 1536:3584].rearrange("p (k n) -> p k n", n=1024)
        latent = {}

        def latent_heads(hh, free):
            VAl = LV[hh]
            QTl = [(LQ[hh], PS[7][0:96, :])]
            KTl = [(LK[hh][a], PS[7][0:96, a * 256:a * 256 + 256]) for a in range(2)]
            normed, turned, read = {}, {}, None

            def turn(i, src, dst, key):
                nonlocal read
                t = T(transposes([(PS[7][0:96, h * 128:h * 128 + 128], src[:, i % 2, h * 96:h * 96 + 96]) for h in range(4)]),
                      normed[key, i], read)
                turned[key, i] = t
                for d, p in dst:
                    read = A(lambda e: e.activation(d[0:96, :, i * 128:i * 128 + 128], p.rearrange("p (h n) -> p h n", n=128),
                                                    ACT.Copy), t, free)

            t = None
            for pair in range(3):
                for i in (2 * pair, 2 * pair + 1):
                    tok = slice(i * 128, i * 128 + 128)
                    st = stats[:, i % 2 * 8:i % 2 * 8 + 8]
                    tm = T(mms(PS[7][:, 0:384], [(CQ[:, k, tok], wq[:, k, hh * 384:hh * 384 + 384]) for k in range(2)]),
                           twl, tcn, read)
                    read = te = A(lambda e: e.activation(QA[:, i % 2, :], PS[7][:, 0:384], ACT.Copy), tm, turned.get(("q", i - 2)))
                    t = head_sums(QA[:, i % 2, :], 4, 96, rt, st[:, 0:4], te, t)
                    yield
                    tm = T(mms(PS[7], [(CQ[:, 2 + k, tok], wkv[:, k, hh * 512:hh * 512 + 512]) for k in range(2)]), read)
                    kv = PS[7].rearrange("p (h d) -> p h d", d=128)
                    ka = KA[:, i % 2, :].rearrange("p (h d) -> p h d", d=96)
                    va = VAl[:, i, :].rearrange("p (h d) -> p h d", d=64)
                    t1 = A(lambda e: e.activation(ka[:, :, 0:64], kv[:, :, 0:64], ACT.Copy), tm, turned.get(("k", i - 2)))
                    read = A(lambda e: e.activation(va, kv[:, :, 64:128], ACT.Copy), tm, free)
                    t2 = G(lambda e: e.tensor_copy(ka[:, :, 64:96], KR[:, i, :].unsqueeze(1).to_broadcast([128, 4, 32])),
                           turned.get(("k", i - 2)))
                    t = head_sums(KA[:, i % 2, :], 4, 96, rt, st[:, 4:8], t1, t2, t)
                    yield
                st = stats[:, 0:16]
                t = V(lambda e: e.tensor_scalar(st, st, 1.0 / 96, EPS, ALU.mult, ALU.add), t)
                t = A(lambda e: e.activation(st, st, ACT.Sqrt), t)
                yield
                t = V(lambda e: e.reciprocal(st, st), t)
                for i in (2 * pair, 2 * pair + 1):
                    for key, src, col, gain, scale in (("q", QA, 0, gains[:, 0:96], 96.0 ** -0.5), ("k", KA, 4, gains[:, 96:192], 1.0)):
                        c = i % 2 * 8 + col
                        t = yield from head_scale(src[:, i % 2, :], 4, 96, gain, scale, stats[:, c:c + 4], t)
                        yield
                        if i < 4:
                            t = yield from rope(src[:, i % 2, :], 4, 96, 64, 8, i, False, rt, t)
                            yield
                        normed[key, i] = t
                    if i % 2:
                        turn(i - 1, QA, QTl, "q")
                        yield
                        turn(i - 1, KA, KTl, "k")
                        yield
                if pair < 2:
                    turn(2 * pair + 1, QA, QTl, "q")
                    yield
                    turn(2 * pair + 1, KA, KTl, "k")
                    yield
            if hh == 1:
                W.give(sl, tm)
            turn(5, QA, QTl, "q")
            yield
            turn(5, KA, KTl, "k")
            latent[hh] = read

        def dense(H, qs, kts, vals, tile):
            groups = []
            for h in range(H):
                q, k, p0 = qs(h), kts(h), 64 * (h % 2)
                units = [(q[:, i * 128:i * 128 + 128], [(k[:, 0:512], 0), (k[:, 512:768], 512)], 0, 768, [], None, i,
                          [(0, 6, 0)]) for i in range(4)]
                groups.append((units, PTM, [(j, vals(h, j), 0, 512) for j in range(6)], 512,
                               (p0, GTE[p0:p0 + 64, tile + h // 2, 0:512])))
                units = [(q[:, i * 128:i * 128 + 128], [(k[:, 512:768], 512)], 512, 256, [], None, i - 4, [(0, 2, 0)])
                         for i in (4, 5)]
                groups.append((units, PTC, [(j, vals(h, 4 + j), 0, 256) for j in range(2)], 256,
                               (p0, GTE[p0:p0 + 64, tile + h // 2, 512:768])))
            return groups

        half = lambda h: slice(64 * (h % 2), 64 * (h % 2) + 64)
        ta = attention(dense(8, lambda h: QT[half(h), h // 2, :], lambda h: KT[half(h), h // 4, :],
                             lambda h, k: GKV[:, k, 128 + 64 * (h // 4):192 + 64 * (h // 4)], 4), PB,
                       latent_heads(0, None), 1)
        dump("gte", GTE, V.last())
        barrier()
        if stop == "gqa":
            return fin()
        for hh in range(2):
            ta = attention(dense(4, lambda h: LQ[hh][0:96, h, :], lambda h: LK[hh][h // 2][0:96, h % 2, :],
                                 lambda h, k: LV[hh][:, k, h * 64:h * 64 + 64], hh * 2), PB,
                           latent_heads(1, ta) if hh == 0 else iter(()), 2)
            barrier()
        dump("gte2", GTE, V.last())
        GR, GC = R(0, 1, 1024)[:, 0, :], R(1024, 1, 1024)[:, 0, :]
        TM, XN = R(2048, 2, 512), R(3072, 2, 1024)
        top[0] = mark + 640
        PQ = alloc(4, 512)
        PKV = alloc(6, 256)
        UP = alloc(4, 514)
        top[0] = mark + 640 + 6144
        MT = alloc(8, 512)
        HT = alloc(8, 768)
        YF = alloc(2, 512)
        rt = alloc(1024)
        GR1 = alloc(1024)
        assert top[0] <= WORDS - 4096, top[0]
        for g, r in ((GR, 0), (GC, 1)):
            t3 = d3(A, g, MOD2[0, r:r + 1, 2048:3072].partition_broadcast(128), everyone())
        xn_read[:] = [None, None]
        tmp_ = scales(1)
        th, rows = [], []

        def norm_between(i, t):
            rows.append(adaln_rows(i, i, t))
            if i:
                th.append(adaln_turn(1, i - 1, i - 1, HT, rows[i - 1]))

        tx = project(GTE, range(6), xrow, lambda i: GR if i < 4 else GC, TM, ta, t3, after=norm_between)
        th.append(adaln_turn(1, 5, 5, HT, rows[5]))
        dump("x3", X, V.last())
        dump("xc3", XC, V.last())
        if stop == "x3":
            barrier()
            return fin()

        t3 = d3(A, GR1, MOD2[1, 0:1, 2048:3072].partition_broadcast(128))
        tz = G(lambda e: e.memset(UP, 0.0), tx)
        s, w, tw = W.take()
        tpq, tpk = {}, {}
        for i in range(4):
            tpq[i], t = gemm_t(HT, x512(w), 0, 512, i, PQ[:, i, :], tw, th[i])
        W.give(s, t)
        s, w, tw = W.take()
        for i in range(6):
            tpk[i], t = gemm_t(HT, x512(w), 0, 256, i, PKV[:, i, :], tw, th[i])
        W.give(s, t)

        def win_sums(i, t):
            if i < 4:
                t = head_sums(PQ[:, i, :], 8, 64, rt, stats[:, 12 + 8 * i:20 + 8 * i], t, tpq[i])
            return head_sums(PKV[:, i, 0:128], 2, 64, rt, stats[:, 2 * i:2 * i + 2], t, tpk[i])

        def win_norms(i, t):
            if i < 4:
                t = run(head_scale(PQ[:, i, :], 8, 64, gains[:, 320:384], 0.125, stats[:, 12 + 8 * i:20 + 8 * i], t))
                t = run(rope(PQ[:, i, :], 8, 64, 0, 16, i, True, rt, t))
            t = run(head_scale(PKV[:, i, 0:128], 2, 64, gains[:, 384:448], 1.0, stats[:, 2 * i:2 * i + 2], t))
            if i < 4:
                t = run(rope(PKV[:, i, 0:128], 2, 64, 0, 16, i, True, rt, t))
            return t

        tgb, tup, tn = [], [], None
        for i in range(6):
            tn = win_sums(i, tn)
        tn, _ = rsqrt(stats[:, 0:44], stats[:, 0:44], 1.0 / 64, tn)
        for c in range(3):
            s, w, tw = W.take()
            w = x512(w)
            for i in range(4):
                b = bank()
                t = gemm_f(w, i * 128, lambda k: HT[:, k, 0:512], PS[b], b, tw)
                if c == 0:
                    rel[b] = A(lambda e: e.activation(MT[:, 4 + i, :], PS[b], ACT.Copy), t)
                    tgb.append(rel[b])
                elif c == 1:
                    rel[b] = A(lambda e: e.activation(UP[:, i, 1:513], PS[b], ACT.Copy), t, tz)
                    tup.append(rel[b])
                else:
                    rel[b] = V(lambda e: e.tensor_tensor(UP[:, i, 1:513], UP[:, i, 1:513], PS[b], ALU.mult), t, tup[i])
                    tup[i] = rel[b]
                n = 4 * c + i
                if n % 2 == 0:
                    tn = win_norms(n // 2, tn)
            W.give(s, t)
        yf = [None, None]
        tod = []
        for i in range(4):
            y = YF[:, i % 2, :]
            t = tup[i]
            for j in range(3):
                cw = VF[:, r_c2 + j * 4 + i:r_c2 + j * 4 + i + 1]
                uv = UP[:, i, j:j + 512]
                if j == 0:
                    t = V(lambda e: e.tensor_scalar(y, uv, cw, None, ALU.mult), t, yf[i % 2])
                else:
                    t = V(lambda e: e.scalar_tensor_tensor(y, uv, cw, y, ALU.mult, ALU.add), t)
            yf[i % 2] = V(lambda e: e.tensor_tensor(MT[:, 4 + i, :], MT[:, 4 + i, :], y, ALU.mult), t, tgb[i])
            tod.append(yf[i % 2])
        s, w, tw = W.take()
        w = x512(w)
        for i in range(4):
            b = bank()
            t = gemm_f(w, i * 128, lambda k: HT[:, k, 0:512], PS[b], b, tw)
            rel[b] = tga = A(lambda e: e.activation(MT[:, i, :], PS[b], ACT.Silu), t)
        W.give(s, t)
        s, w, tw = W.take()
        w = x512(w)
        for i in range(4):
            b = bank()
            u = i % 2
            t = gemm_f(w, i * 128, lambda k: HT[:, k, 0:512], PS[b], b, tw)
            rel[b] = t1 = A(lambda e: e.activation(YF[:, u, :], PS[b], ACT.Silu), t, yf[0], yf[1])
            yf[u] = V(lambda e: e.tensor_tensor(MT[:, 4 + i, :], MT[:, 4 + i, :], YF[:, u, :], ALU.mult), t1, tod[i])
        W.give(s, t)
        QT, KT = R(0, 4, 512), R(2048, 2, 768)
        pairs_t(lambda i: PQ[:, i, :], 8, QT, range(4), tn)
        twice_t(lambda i: PKV[:, i, 0:128], 2, KT, range(6))
        barrier()
        PTW = [HT.rearrange("p a n -> p (a n)")[:, a * 3072:a * 3072 + 3072].rearrange("p (k n) -> p k n", n=512) for a in range(2)]
        PB = R(3584, 2, 768)
        wmp, wmn = c3[:, 384:512], c3[:, 512:640]
        groups = []
        for h in range(8):
            q, k, p0 = QT[half(h), h // 2, :], KT[half(h), h // 4, :], 64 * (h % 2)
            units = []
            for n in range(4):
                lo, hi = max(n - 1, 0), min(n + 2, 4)
                L = (hi - lo) * 128
                at = 512 - L
                masks = ([(wmp, at)] if n else []) + ([(wmn, 384)] if n < 3 else [])
                units.append((q[:, n * 128:n * 128 + 128], [(k[:, lo * 128:hi * 128], at), (k[:, 512:768], 512)],
                              at, L + 256, masks, sinkr[:, 8 + h:9 + h], n, [(0, hi - lo, lo), (hi - lo, hi - lo + 2, 4)]))
            v = lambda j: PKV[:, j, 128 + 64 * (h // 4):192 + 64 * (h // 4)]
            vals = [(j, v(j), 0, 512) for j in (4, 5)] \
                + [(j, v(j), max(j - 1, 0) * 128, min(j + 2, 4) * 128) for j in range(4)]
            groups.append((units, PTW[h % 2], vals, 512, (p0, MT[p0:p0 + 64, h // 2, :])))
        ta = attention(groups, PB)
        TM = YF
        tx = project(MT, range(4), xrow, lambda i: GR1, TM, ta, yf, t3)
        do = dsem("out")
        for i in range(4):
            t = do(S, out[0, i * 128:i * 128 + 128, :], X[:, i, :], tx[i])
        S.wait(t)


_INS = ['x', 'c', 'w_ada', 'b_ada', 'norm1_w', 'w_in', 'conv_w', 'a_log', 'dt_bias', 'dn_norm_w', 'q_norm_w',
        'k_norm_w', 'sinks', 'w_out', 'norm2_w', 'w_router', 'b_router', 'w_up', 'b_up', 'w_down', 'b_down', 'c_2',
        'ctx_2', 'c_ctx_2', 'mod_w_2', 'mod_b_2', 'ab_w_in_2', 'ab_w_out_2', 'mla_cq_gain_2', 'mla_ckv_gain_2',
        'mla_w_uq_2', 'mla_w_ukv_2', 'mla_q_gain_2', 'mla_k_gain_2', 'gqa_q_gain_2', 'gqa_k_gain_2', 'cd_w_in_2',
        'cd_w_out_2', 'win_q_gain_2', 'win_k_gain_2', 'win_sink_2', 'conv_w_2']


def build(nc, arrays, dbg_shapes=None, stop=None):
    D = {}
    for n, a in arrays.items():
        D[n] = nc.dram_tensor("in_" + n, a.shape, F32, kind="ExternalInput").ap()
    out = nc.dram_tensor("out_0", (1, 512, 1024), F32, kind="ExternalOutput").ap()
    dbg = None
    if dbg_shapes:
        dbg = {n: nc.dram_tensor("dbg_" + n, s, dt, kind="ExternalOutput").ap() for n, (s, dt) in dbg_shapes.items()}
    program(nc, D, out, dbg, stop)


def kernel(**inputs):
    import concourse.bacc as _bacc
    from concourse.bass_utils import run_bass_kernel_spmd as _run

    nc = _bacc.Bacc("TRN2", target_bir_lowering=False, num_devices=1)
    arrays = {n: np.ascontiguousarray(inputs[n]) for n in _INS}
    arrays.update(constants())
    build(nc, arrays)
    r = _run(nc, [{"in_" + n: a for n, a in arrays.items()}], core_ids=[0])
    return r.results[0]["out_0"]
```
